# Optimizing a Trainium2 kernel written in Bass

```python
import jax
import jax.numpy as jnp
from jax import lax
import numpy as np
import jax, jax.numpy as jnp

D_MODEL = 1024
BATCH = 1
SEQ = 256
DEPTH = 2

N_MEM = 256
EPS = 1e-6
NEG_INF = -1e30

HEAD_DIM = 64
ROPE_DIM = HEAD_DIM // 4
ROPE_THETA = 500000.0

A_HEADS = 8
A_WIDTH = A_HEADS * HEAD_DIM
MOBA_BLOCK = 256
MOBA_TOPK = 3
MOBA_QCHUNK = 32

B_GROUPS = 8
B_WIDTH = B_GROUPS * HEAD_DIM
GMLP_CHUNK = 128

GLA_HEADS = 4
GLA_DK = (D_MODEL // 2) // GLA_HEADS
GLA_DV = D_MODEL // GLA_HEADS
GLA_LOWRANK = 16
GLA_TAU = 16.0
GLA_CHUNK = 64

X_HEADS = 4
X_HEAD_DIM = D_MODEL // X_HEADS

D_FF = -(-8 * D_MODEL // (3 * 256)) * 256

EV_IN = 3 * A_WIDTH + 2 * B_WIDTH
OD_IN = 2 * GLA_HEADS * GLA_DK + 2 * GLA_HEADS * GLA_DV


def rmsnorm(x, g):
    xf = x.astype(jnp.float32)
    y = xf * lax.rsqrt(jnp.mean(xf * xf, axis=-1, keepdims=True) + EPS)
    return (y * g.astype(jnp.float32)).astype(x.dtype)

def layernorm(x, g, b):
    xf = x.astype(jnp.float32)
    mu = jnp.mean(xf, axis=-1, keepdims=True)
    var = jnp.mean(jnp.square(xf - mu), axis=-1, keepdims=True)
    y = (xf - mu) * lax.rsqrt(var + EPS) * g.astype(jnp.float32) + b.astype(jnp.float32)
    return y.astype(x.dtype)

def partial_rope(x, positions):
    half = ROPE_DIM // 2
    inv_freq = ROPE_THETA ** (-jnp.arange(half, dtype=jnp.float32) * 2.0 / ROPE_DIM)
    ang = positions.astype(jnp.float32)[:, None, :, None] * inv_freq
    cos, sin = jnp.cos(ang), jnp.sin(ang)
    xf = x.astype(jnp.float32)
    x1, x2 = xf[..., :half], xf[..., half:ROPE_DIM]
    out = jnp.concatenate([x1 * cos - x2 * sin, x2 * cos + x1 * sin, xf[..., ROPE_DIM:]], axis=-1)
    return out.astype(x.dtype)

def moba_attention(q, k, v):
    Bn, H, S, Dh = q.shape
    S_pad = -(-S // MOBA_BLOCK) * MOBA_BLOCK
    pad = [(0, 0), (0, 0), (0, S_pad - S), (0, 0)]
    q, k, v = jnp.pad(q, pad), jnp.pad(k, pad), jnp.pad(v, pad)
    nb = S_pad // MOBA_BLOCK
    topk = min(MOBA_TOPK, nb)
    scale = Dh ** -0.5
    kb = k.reshape(Bn, H, nb, MOBA_BLOCK, Dh)
    vb = v.reshape(Bn, H, nb, MOBA_BLOCK, Dh)
    k_mean = jnp.mean(kb.astype(jnp.float32), axis=3)
    gate = jnp.einsum('bhsd,bhnd->bhsn', q.astype(jnp.float32), k_mean)
    own = jnp.arange(S_pad) // MOBA_BLOCK
    past = jnp.arange(nb)[None, :] < own[:, None]
    gate = jnp.where(past[None, None], gate, NEG_INF)
    _, sel = lax.top_k(gate, topk)
    valid = sel < own[None, None, :, None]

    nq = S_pad // MOBA_QCHUNK
    q_c = q.reshape(Bn, H, nq, MOBA_QCHUNK, Dh).transpose(2, 0, 1, 3, 4)
    sel_c = sel.reshape(Bn, H, nq, MOBA_QCHUNK, topk).transpose(2, 0, 1, 3, 4)
    valid_c = valid.reshape(Bn, H, nq, MOBA_QCHUNK, topk).transpose(2, 0, 1, 3, 4)
    chunk_ids = jnp.arange(nq, dtype=jnp.int32)
    bi = jnp.arange(Bn)[:, None, None, None]
    hi = jnp.arange(H)[None, :, None, None]
    key_idx = jnp.arange(MOBA_BLOCK)

    def one_chunk(args):
        qc, selc, validc, ci = args
        blk = (ci * MOBA_QCHUNK) // MOBA_BLOCK
        k_own = lax.dynamic_index_in_dim(kb, blk, axis=2, keepdims=False)
        v_own = lax.dynamic_index_in_dim(vb, blk, axis=2, keepdims=False)
        qpos = (ci * MOBA_QCHUNK) % MOBA_BLOCK + jnp.arange(MOBA_QCHUNK)
        causal = key_idx[None, :] <= qpos[:, None]
        s_own = jnp.einsum('bhqd,bhkd->bhqk', qc, k_own, preferred_element_type=jnp.float32) * scale
        s_own = jnp.where(causal[None, None], s_own, NEG_INF)
        k_sel = kb[bi, hi, selc]
        v_sel = vb[bi, hi, selc]
        s_sel = jnp.einsum('bhqd,bhqnkd->bhqnk', qc, k_sel, preferred_element_type=jnp.float32) * scale
        s_sel = jnp.where(validc[..., None], s_sel, NEG_INF)
        logits = jnp.concatenate([s_own, s_sel.reshape(Bn, H, MOBA_QCHUNK, topk * MOBA_BLOCK)], axis=-1)
        p = jax.nn.softmax(logits, axis=-1)
        p_own = p[..., :MOBA_BLOCK].astype(v.dtype)
        p_sel = p[..., MOBA_BLOCK:].reshape(Bn, H, MOBA_QCHUNK, topk, MOBA_BLOCK).astype(v.dtype)
        out = (jnp.einsum('bhqk,bhkd->bhqd', p_own, v_own, preferred_element_type=jnp.float32)
               + jnp.einsum('bhqnk,bhqnkd->bhqd', p_sel, v_sel, preferred_element_type=jnp.float32))
        return out.astype(q.dtype)

    out = lax.map(one_chunk, (q_c, sel_c, valid_c, chunk_ids))
    out = out.transpose(1, 2, 0, 3, 4).reshape(Bn, H, S_pad, Dh)
    return out[:, :, :S]

def chunked_spatial_gating(u, v, w_s, b_s, ln_g, ln_b):
    Bn, S, G, Dg = v.shape
    nc = S // GMLP_CHUNK
    vn = layernorm(v, ln_g, ln_b).reshape(Bn, nc, GMLP_CHUNK, G, Dg)
    mask = jnp.tril(jnp.ones((GMLP_CHUNK, GMLP_CHUNK), dtype=w_s.dtype))
    ws = w_s * mask[None]
    mixed = jnp.einsum('gij,bcjgd->bcigd', ws, vn) + b_s.T[None, None, :, :, None]
    return u * mixed.reshape(Bn, S, G, Dg).astype(u.dtype)

def even_mixer(h, positions, w_in, q_gain, k_gain, w_s, b_s, ln_g, ln_b, w_out):
    Bn, S, _ = h.shape
    proj = h @ w_in
    q, k, v, pu, pv = jnp.split(proj, [A_WIDTH, 2 * A_WIDTH, 3 * A_WIDTH, 3 * A_WIDTH + B_WIDTH], axis=-1)

    def heads(t):
        return t.reshape(Bn, S, A_HEADS, HEAD_DIM).transpose(0, 2, 1, 3)

    q = partial_rope(rmsnorm(heads(q), q_gain), positions)
    k = partial_rope(rmsnorm(heads(k), k_gain), positions)
    a = moba_attention(q, k, heads(v)).transpose(0, 2, 1, 3).reshape(Bn, S, A_WIDTH)
    u = jax.nn.gelu(pu, approximate=False).reshape(Bn, S, B_GROUPS, HEAD_DIM)
    vg = jax.nn.gelu(pv, approximate=False).reshape(Bn, S, B_GROUPS, HEAD_DIM)
    g = chunked_spatial_gating(u, vg, w_s, b_s, ln_g, ln_b).reshape(Bn, S, B_WIDTH)
    return jnp.concatenate([a, g], axis=-1) @ w_out

def gla_chunked(q, k, v, log_a):
    Bn, H, S, dk = q.shape
    dv = v.shape[-1]
    nc = S // GLA_CHUNK
    f32 = jnp.float32
    qc = q.astype(f32).reshape(Bn, H, nc, GLA_CHUNK, dk)
    kc = k.astype(f32).reshape(Bn, H, nc, GLA_CHUNK, dk)
    vc = v.astype(f32).reshape(Bn, H, nc, GLA_CHUNK, dv)
    b = jnp.cumsum(log_a.astype(f32).reshape(Bn, H, nc, GLA_CHUNK, dk), axis=3)
    b_last = b[:, :, :, -1:, :]
    q_in = qc * jnp.exp(b)
    k_in = kc * jnp.exp(-b)
    causal = jnp.tril(jnp.ones((GLA_CHUNK, GLA_CHUNK), dtype=bool))
    att = jnp.where(causal, jnp.einsum('bhnid,bhnjd->bhnij', q_in, k_in), 0.0)
    o_intra = jnp.einsum('bhnij,bhnjv->bhniv', att, vc)
    k_state = kc * jnp.exp(b_last - b)
    d_state = jnp.einsum('bhnjd,bhnjv->bhndv', k_state, vc)
    decay = jnp.exp(b_last[:, :, :, 0, :])

    def step(s_prev, xs):
        ds_n, dec_n = xs
        return dec_n[..., None] * s_prev + ds_n, s_prev

    _, s_before = lax.scan(step, jnp.zeros((Bn, H, dk, dv), f32),
                           (jnp.moveaxis(d_state, 2, 0), jnp.moveaxis(decay, 2, 0)))
    s_before = jnp.moveaxis(s_before, 0, 2)
    o_inter = jnp.einsum('bhnid,bhndv->bhniv', q_in, s_before)
    return (o_intra + o_inter).reshape(Bn, H, S, dv).astype(v.dtype)

def gla_mixer(h, w_in, w_g1, w_g2, b_g, o_gain, w_out):
    Bn, S, _ = h.shape
    qk_w = GLA_HEADS * GLA_DK
    v_w = GLA_HEADS * GLA_DV
    proj = h @ w_in
    q, k, v, r = jnp.split(proj, [qk_w, 2 * qk_w, 2 * qk_w + v_w], axis=-1)
    log_a = jax.nn.log_sigmoid(((h @ w_g1) @ w_g2 + b_g).astype(jnp.float32)) / GLA_TAU

    def heads(t, d):
        return t.reshape(Bn, S, GLA_HEADS, d).transpose(0, 2, 1, 3)

    o = gla_chunked(heads(q, GLA_DK) * (GLA_DK ** -0.5), heads(k, GLA_DK),
                    heads(v, GLA_DV), heads(log_a, GLA_DK))
    o = rmsnorm(o, o_gain[:, None, :])
    o = o.transpose(0, 2, 1, 3).reshape(Bn, S, v_w) * jax.nn.silu(r)
    return o @ w_out

def mem_cross_attention(h, mem_n, w_q, w_kv, q_gain, k_gain, w_out):
    Bn, S, _ = h.shape
    M = mem_n.shape[1]
    q = rmsnorm((h @ w_q).reshape(Bn, S, X_HEADS, X_HEAD_DIM), q_gain)
    k, v = jnp.split(mem_n @ w_kv, 2, axis=-1)
    k = rmsnorm(k.reshape(Bn, M, X_HEADS, X_HEAD_DIM), k_gain)
    v = v.reshape(Bn, M, X_HEADS, X_HEAD_DIM)
    s = jnp.einsum('bqhd,bkhd->bhqk', q, k, preferred_element_type=jnp.float32) * (X_HEAD_DIM ** -0.5)
    p = jax.nn.softmax(s, axis=-1).astype(v.dtype)
    o = jnp.einsum('bhqk,bkhd->bqhd', p, v).reshape(Bn, S, D_MODEL)
    return o @ w_out

def swiglu(h, w_gu, w_down):
    g, u = jnp.split(h @ w_gu, 2, axis=-1)
    return (jax.nn.silu(g) * u) @ w_down

def first_inputs(seed: int = 0) -> dict:
    key = jax.random.key(seed)
    ks = iter(jax.random.split(key, 32))
    f32 = jnp.float32
    n_ev = (DEPTH + 1) // 2
    n_od = DEPTH // 2

    def nrm(shape, scale):
        return jax.random.normal(next(ks), shape, f32) * scale

    def gain(shape):
        return 1.0 + 0.05 * jax.random.normal(next(ks), shape, f32)

    x = nrm((BATCH, SEQ, D_MODEL), 1.0)
    mem = nrm((BATCH, N_MEM, D_MODEL), 1.0)
    positions = (jnp.arange(SEQ, dtype=jnp.int32)[None, :]
                 + jax.random.randint(next(ks), (BATCH, 1), 0, 4096, dtype=jnp.int32))
    return {
        'x': x,
        'mem': mem,
        'positions': positions,
        'norm_mix': gain((DEPTH, D_MODEL)),
        'norm_mem_q': gain((DEPTH, D_MODEL)),
        'norm_mem_kv': gain((DEPTH, D_MODEL)),
        'norm_ffn': gain((DEPTH, D_MODEL)),
        'ev_w_in': nrm((n_ev, D_MODEL, EV_IN), D_MODEL ** -0.5),
        'ev_q_gain': gain((n_ev, HEAD_DIM)),
        'ev_k_gain': gain((n_ev, HEAD_DIM)),
        'ev_w_s': nrm((n_ev, B_GROUPS, GMLP_CHUNK, GMLP_CHUNK), GMLP_CHUNK ** -0.5),
        'ev_b_s': gain((n_ev, B_GROUPS, GMLP_CHUNK)),
        'ev_ln_g': gain((n_ev, B_GROUPS, HEAD_DIM)),
        'ev_ln_b': nrm((n_ev, B_GROUPS, HEAD_DIM), 0.02),
        'ev_w_out': nrm((n_ev, A_WIDTH + B_WIDTH, D_MODEL), 0.5 * (A_WIDTH + B_WIDTH) ** -0.5),
        'od_w_in': nrm((n_od, D_MODEL, OD_IN), D_MODEL ** -0.5),
        'od_w_g1': nrm((n_od, D_MODEL, GLA_LOWRANK), D_MODEL ** -0.5),
        'od_w_g2': nrm((n_od, GLA_LOWRANK, GLA_HEADS * GLA_DK), GLA_LOWRANK ** -0.5),
        'od_b_g': nrm((n_od, GLA_HEADS * GLA_DK), 0.02),
        'od_o_gain': gain((n_od, GLA_HEADS, GLA_DV)),
        'od_w_out': nrm((n_od, GLA_HEADS * GLA_DV, D_MODEL), 0.5 * (GLA_HEADS * GLA_DV) ** -0.5),
        'xa_w_q': nrm((DEPTH, D_MODEL, D_MODEL), D_MODEL ** -0.5),
        'xa_w_kv': nrm((DEPTH, D_MODEL, 2 * D_MODEL), D_MODEL ** -0.5),
        'xa_q_gain': gain((DEPTH, X_HEAD_DIM)),
        'xa_k_gain': gain((DEPTH, X_HEAD_DIM)),
        'xa_w_out': nrm((DEPTH, D_MODEL, D_MODEL), 0.5 * D_MODEL ** -0.5),
        'ffn_w_gu': nrm((DEPTH, D_MODEL, 2 * D_FF), D_MODEL ** -0.5),
        'ffn_w_down': nrm((DEPTH, D_FF, D_MODEL), 0.5 * D_FF ** -0.5),
    }

def first_block(x, mem, positions, norm_mix, norm_mem_q, norm_mem_kv, norm_ffn,
              ev_w_in, ev_q_gain, ev_k_gain, ev_w_s, ev_b_s, ev_ln_g, ev_ln_b, ev_w_out,
              od_w_in, od_w_g1, od_w_g2, od_b_g, od_o_gain, od_w_out,
              xa_w_q, xa_w_kv, xa_q_gain, xa_k_gain, xa_w_out,
              ffn_w_gu, ffn_w_down):
    for l in range(DEPTH):
        i = l // 2
        h = rmsnorm(x, norm_mix[l])
        if l % 2 == 0:
            x = x + even_mixer(h, positions, ev_w_in[i], ev_q_gain[i], ev_k_gain[i],
                               ev_w_s[i], ev_b_s[i], ev_ln_g[i], ev_ln_b[i], ev_w_out[i])
        else:
            x = x + gla_mixer(h, od_w_in[i], od_w_g1[i], od_w_g2[i], od_b_g[i],
                              od_o_gain[i], od_w_out[i])
        x = x + mem_cross_attention(rmsnorm(x, norm_mem_q[l]), rmsnorm(mem, norm_mem_kv[l]),
                                    xa_w_q[l], xa_w_kv[l], xa_q_gain[l], xa_k_gain[l], xa_w_out[l])
        x = x + swiglu(rmsnorm(x, norm_ffn[l]), ffn_w_gu[l], ffn_w_down[l])
    return x


GRID_W = 64
CTX_LEN = 256
N_MIXERS = 3
N_HEADS = 16
N_KV_HEADS = 4
HEAD_DIM_2 = D_MODEL // N_HEADS
Q_PER_KV = N_HEADS // N_KV_HEADS
QKV_DIM = (N_HEADS + 2 * N_KV_HEADS) * HEAD_DIM_2
ATTN_SCALE = HEAD_DIM_2 ** -0.5
ROPE_THETA_2 = 10000.0
BLOCK_Q = 128
WINDOW = 128
NA_WIN_H = 8
NA_WIN_W = 16
N_GROUPS = 4
EXPERTS_PER_GROUP = 8
N_EXPERTS = N_GROUPS * EXPERTS_PER_GROUP
TOP_K_IN_GROUP = 2
EXPERT_HIDDEN = D_MODEL // 2
MOE_BLOCK = 128
NORM_EPS = 1e-6
NEG_INF_2 = -1e30
N_A_LAYERS = (DEPTH + N_MIXERS - 1) // N_MIXERS
N_B_LAYERS = (DEPTH + N_MIXERS - 2) // N_MIXERS
N_C_LAYERS = DEPTH // N_MIXERS


def _rmsnorm(x, g):
    x32 = x.astype(jnp.float32)
    y = x32 * lax.rsqrt(jnp.mean(x32 * x32, axis=-1, keepdims=True) + NORM_EPS)
    return (y * g.astype(jnp.float32)).astype(x.dtype)

def _modulate(h, shift, scale):
    return h * (1 + scale) + shift

def _axial_rope_tables(n, dtype):
    t = jnp.arange(n)
    row = (t // GRID_W).astype(jnp.float32)
    col = (t % GRID_W).astype(jnp.float32)
    quarter = HEAD_DIM_2 // 4
    inv = ROPE_THETA_2 ** (-jnp.arange(quarter, dtype=jnp.float32) / quarter)
    ar = row[:, None] * inv
    ac = col[:, None] * inv
    ang = jnp.concatenate([ar, ar, ac, ac], axis=-1)
    return jnp.cos(ang).astype(dtype), jnp.sin(ang).astype(dtype)

def _rot_axial(x):
    r1, r2, c1, c2 = jnp.split(x, 4, axis=-1)
    return jnp.concatenate([-r2, r1, -c2, c1], axis=-1)

def _apply_rope(x, cos, sin):
    shp = (1, x.shape[1]) + (1,) * (x.ndim - 3) + (HEAD_DIM_2,)
    return x * cos.reshape(shp) + _rot_axial(x) * sin.reshape(shp)

def _split_qkv(h, w_qkv):
    b, n, _ = h.shape
    qkv = h @ w_qkv
    q, k, v = jnp.split(qkv, [N_HEADS * HEAD_DIM_2, (N_HEADS + N_KV_HEADS) * HEAD_DIM_2], axis=-1)
    return (q.reshape(b, n, N_KV_HEADS, Q_PER_KV, HEAD_DIM_2),
            k.reshape(b, n, N_KV_HEADS, HEAD_DIM_2),
            v.reshape(b, n, N_KV_HEADS, HEAD_DIM_2))

def _sink_column(sink, lead_shape):
    return jnp.broadcast_to(sink.astype(jnp.float32).reshape(1, N_KV_HEADS, Q_PER_KV, 1, 1), lead_shape + (1,))

def _joint_softmax(s_lat, s_ctx, sink):
    parts = [s_lat, s_ctx]
    if sink is not None:
        parts.append(_sink_column(sink, s_lat.shape[:-1]))
    p = jax.nn.softmax(jnp.concatenate(parts, axis=-1), axis=-1)
    k1 = s_lat.shape[-1]
    c = s_ctx.shape[-1]
    return p[..., :k1], p[..., k1:k1 + c]

def _ctx_self_attention(qc, kc, vc, sink):
    b, n = qc.shape[:2]
    s = jnp.einsum('bqhgd,bkhd->bhgqk', qc, kc).astype(jnp.float32)
    if sink is not None:
        s = jnp.concatenate([s, _sink_column(sink, s.shape[:-1])], axis=-1)
    p = jax.nn.softmax(s, axis=-1)[..., :kc.shape[1]]
    o = jnp.einsum('bhgqk,bkhd->bqhgd', p.astype(vc.dtype), vc)
    return o.reshape(b, n, N_HEADS * HEAD_DIM_2)

def _mixer_window(q, k, v, kc, vc, sink, cos, sin):
    b, n = q.shape[:2]
    nb = n // BLOCK_Q
    span = BLOCK_Q + 2 * WINDOW
    q_rot = _apply_rope(q, cos, sin)
    pad = ((0, 0), (WINDOW, WINDOW), (0, 0), (0, 0))
    k_pad = jnp.pad(_apply_rope(k, cos, sin), pad)
    v_pad = jnp.pad(v, pad)

    def block(i):
        start = i * BLOCK_Q
        qb = lax.dynamic_slice_in_dim(q_rot, start, BLOCK_Q, 1)
        qpb = lax.dynamic_slice_in_dim(q, start, BLOCK_Q, 1)
        kb = lax.dynamic_slice_in_dim(k_pad, start, span, 1)
        vb = lax.dynamic_slice_in_dim(v_pad, start, span, 1)
        qpos = start + jnp.arange(BLOCK_Q)
        kpos = start - WINDOW + jnp.arange(span)
        mask = ((jnp.abs(kpos[None, :] - qpos[:, None]) <= WINDOW)
                & (kpos >= 0)[None, :] & (kpos < n)[None, :])
        s_lat = jnp.einsum('bqhgd,bkhd->bhgqk', qb, kb).astype(jnp.float32)
        s_lat = jnp.where(mask, s_lat, NEG_INF_2)
        s_ctx = jnp.einsum('bqhgd,bkhd->bhgqk', qpb, kc).astype(jnp.float32)
        p_lat, p_ctx = _joint_softmax(s_lat, s_ctx, sink)
        return (jnp.einsum('bhgqk,bkhd->bqhgd', p_lat.astype(v.dtype), vb)
                + jnp.einsum('bhgqk,bkhd->bqhgd', p_ctx.astype(vc.dtype), vc))

    o = lax.map(block, jnp.arange(nb))
    return jnp.moveaxis(o, 0, 1).reshape(b, n, N_HEADS * HEAD_DIM_2)

def _mixer_global(q, k, v, kc, vc, cos, sin):
    b, n = q.shape[:2]
    nb = n // BLOCK_Q
    q_rot = _apply_rope(q, cos, sin)
    k_rot = _apply_rope(k, cos, sin)

    def block(i):
        start = i * BLOCK_Q
        qb = lax.dynamic_slice_in_dim(q_rot, start, BLOCK_Q, 1)
        qpb = lax.dynamic_slice_in_dim(q, start, BLOCK_Q, 1)
        s_lat = jnp.einsum('bqhgd,bkhd->bhgqk', qb, k_rot).astype(jnp.float32)
        s_ctx = jnp.einsum('bqhgd,bkhd->bhgqk', qpb, kc).astype(jnp.float32)
        p_lat, p_ctx = _joint_softmax(s_lat, s_ctx, None)
        return (jnp.einsum('bhgqk,bkhd->bqhgd', p_lat.astype(v.dtype), v)
                + jnp.einsum('bhgqk,bkhd->bqhgd', p_ctx.astype(vc.dtype), vc))

    o = lax.map(block, jnp.arange(nb))
    return jnp.moveaxis(o, 0, 1).reshape(b, n, N_HEADS * HEAD_DIM_2)

def _na_tables(n):
    rows = n // GRID_W
    wh = min(NA_WIN_H, rows)
    ww = min(NA_WIN_W, GRID_W)
    t = np.arange(n)
    r = t // GRID_W
    cl = t % GRID_W
    rs = np.clip(r - wh // 2, 0, rows - wh)
    cs = np.clip(cl - ww // 2, 0, GRID_W - ww)
    kr = rs[:, None, None] + np.arange(wh)[None, :, None]
    kcol = cs[:, None, None] + np.arange(ww)[None, None, :]
    idx = (kr * GRID_W + kcol).reshape(n, wh * ww)
    rel = ((kr - r[:, None, None] + NA_WIN_H - 1) * (2 * NA_WIN_W - 1)
           + (kcol - cl[:, None, None] + NA_WIN_W - 1)).reshape(n, wh * ww)
    return idx.astype(np.int32), rel.astype(np.int32)

def _mixer_neighbourhood(q, k, v, kc, vc, rpb):
    b, n = q.shape[:2]
    nb = n // BLOCK_Q
    idx, rel = _na_tables(n)
    n_keys = idx.shape[1]
    idx_blocks = jnp.asarray(idx).reshape(nb, BLOCK_Q, n_keys)
    rel_blocks = jnp.asarray(rel).reshape(nb, BLOCK_Q, n_keys)
    rpb_flat = rpb.reshape(N_HEADS, -1)

    def block(args):
        i, idx_b, rel_b = args
        qb = lax.dynamic_slice_in_dim(q, i * BLOCK_Q, BLOCK_Q, 1)
        kg = k[:, idx_b]
        vg = v[:, idx_b]
        bias = rpb_flat[:, rel_b].reshape(N_KV_HEADS, Q_PER_KV, BLOCK_Q, n_keys).astype(jnp.float32)
        s_lat = jnp.einsum('bqhgd,bqkhd->bhgqk', qb, kg).astype(jnp.float32) + bias
        s_ctx = jnp.einsum('bqhgd,bkhd->bhgqk', qb, kc).astype(jnp.float32)
        p_lat, p_ctx = _joint_softmax(s_lat, s_ctx, None)
        return (jnp.einsum('bhgqk,bqkhd->bqhgd', p_lat.astype(v.dtype), vg)
                + jnp.einsum('bhgqk,bkhd->bqhgd', p_ctx.astype(vc.dtype), vc))

    o = lax.map(block, (jnp.arange(nb), idx_blocks, rel_blocks))
    return jnp.moveaxis(o, 0, 1).reshape(b, n, N_HEADS * HEAD_DIM_2)

def _hier_moe(h, w_group, b_group, w_router, b_router, w_gate, w_up, w_down):
    t, d = h.shape
    p_grp = jax.nn.softmax((h @ w_group + b_group).astype(jnp.float32), axis=-1)
    grp = jnp.argmax(p_grp, axis=-1)
    p_top = jnp.take_along_axis(p_grp, grp[:, None], axis=-1)
    lg = (h @ w_router + b_router).astype(jnp.float32).reshape(t, N_GROUPS, EXPERTS_PER_GROUP)
    lg = jnp.take_along_axis(lg, grp[:, None, None], axis=1)[:, 0]
    p_in, e_in = lax.top_k(jax.nn.softmax(lg, axis=-1), TOP_K_IN_GROUP)
    wts = (p_top * p_in / jnp.sum(p_in, axis=-1, keepdims=True)).reshape(-1)
    eid = (grp[:, None] * EXPERTS_PER_GROUP + e_in).reshape(-1).astype(jnp.int32)
    tok = jnp.repeat(jnp.arange(t, dtype=jnp.int32), TOP_K_IN_GROUP)
    n_asg = t * TOP_K_IN_GROUP
    cap = -(-n_asg // MOE_BLOCK) * MOE_BLOCK + N_EXPERTS * MOE_BLOCK
    n_blocks = cap // MOE_BLOCK
    order = jnp.argsort(eid)
    eid_s = eid[order]
    tok_s = tok[order]
    wts_s = wts[order]
    counts = jnp.bincount(eid, length=N_EXPERTS).astype(jnp.int32)
    padded = (counts + MOE_BLOCK - 1) // MOE_BLOCK * MOE_BLOCK
    pad_end = jnp.cumsum(padded)
    pad_start = pad_end - padded
    start = jnp.cumsum(counts) - counts
    dest = pad_start[eid_s] + jnp.arange(n_asg, dtype=jnp.int32) - start[eid_s]
    tok_buf = jnp.full((cap,), t, jnp.int32).at[dest].set(tok_s)
    w_buf = jnp.zeros((cap,), jnp.float32).at[dest].set(wts_s)
    blk_e = jnp.minimum(jnp.searchsorted(pad_end, jnp.arange(n_blocks, dtype=jnp.int32) * MOE_BLOCK, side='right'),
                        N_EXPERTS - 1)
    h_pad = jnp.concatenate([h, jnp.zeros((1, d), h.dtype)], axis=0)
    xb = h_pad[tok_buf].reshape(n_blocks, MOE_BLOCK, d)

    def expert_block(args):
        xe, e = args
        return (jax.nn.silu(xe @ w_gate[e]) * (xe @ w_up[e])) @ w_down[e]

    y = lax.map(expert_block, (xb, blk_e)).reshape(cap, d)
    out = jax.ops.segment_sum(y.astype(jnp.float32) * w_buf[:, None], tok_buf, num_segments=t + 1)
    return out[:t]

def second_inputs(seed: int = 0) -> dict:
    key = jax.random.key(seed)
    ks = jax.random.split(key, 24)

    def nrm(k, shape, s):
        return jax.random.normal(k, shape, jnp.float32) * s

    d, f, hd = D_MODEL, EXPERT_HIDDEN, N_HEADS * HEAD_DIM_2
    return {
        'x': nrm(ks[0], (BATCH, SEQ, d), 1.0),
        'c': nrm(ks[1], (BATCH, d), 1.0),
        'ctx': nrm(ks[2], (BATCH, CTX_LEN, d), 1.0),
        'c_ctx': nrm(ks[3], (d,), 1.0),
        'w_ada': nrm(ks[4], (DEPTH, d, 6 * d), 0.5 * d ** -0.5),
        'b_ada': nrm(ks[5], (DEPTH, 6 * d), 0.02),
        'g_attn': 1.0 + nrm(ks[6], (DEPTH, d), 0.05),
        'w_qkv': nrm(ks[7], (DEPTH, d, QKV_DIM), d ** -0.5),
        'w_o': nrm(ks[8], (DEPTH, hd, d), hd ** -0.5),
        'sink_a': nrm(ks[9], (N_A_LAYERS, N_HEADS), 1.0),
        'gq_b': 1.0 + nrm(ks[10], (N_B_LAYERS, HEAD_DIM_2), 0.05),
        'gk_b': 1.0 + nrm(ks[11], (N_B_LAYERS, HEAD_DIM_2), 0.05),
        'rpb_c': nrm(ks[12], (N_C_LAYERS, N_HEADS, 2 * NA_WIN_H - 1, 2 * NA_WIN_W - 1), 0.5),
        'g_ffn': 1.0 + nrm(ks[13], (DEPTH, d), 0.05),
        'w_group': nrm(ks[14], (DEPTH, d, N_GROUPS), d ** -0.5),
        'b_group': nrm(ks[15], (DEPTH, N_GROUPS), 0.01),
        'w_router': nrm(ks[16], (DEPTH, d, N_EXPERTS), d ** -0.5),
        'b_router': nrm(ks[17], (DEPTH, N_EXPERTS), 0.01),
        'w_gate': nrm(ks[18], (DEPTH, N_EXPERTS, d, f), d ** -0.5),
        'w_up': nrm(ks[19], (DEPTH, N_EXPERTS, d, f), d ** -0.5),
        'w_down': nrm(ks[20], (DEPTH, N_EXPERTS, f, d), f ** -0.5),
        'g_final': 1.0 + nrm(ks[21], (d,), 0.05),
    }

def second_block(x, c, ctx, c_ctx, w_ada, b_ada, g_attn, w_qkv, w_o, sink_a, gq_b, gk_b, rpb_c, g_ffn,
              w_group, b_group, w_router, b_router, w_gate, w_up, w_down, g_final):
    b, n, d = x.shape
    cos, sin = _axial_rope_tables(n, x.dtype)
    silu_c = jax.nn.silu(c)
    silu_cc = jax.nn.silu(c_ctx)
    xc = ctx
    for i in range(DEPTH):
        m = i % N_MIXERS
        j = i // N_MIXERS
        last = i == DEPTH - 1
        mod = (silu_c @ w_ada[i] + b_ada[i])[:, None, :]
        modc = (silu_cc @ w_ada[i] + b_ada[i])[None, None, :]
        sh_a, sc_a, gt_a, sh_f, sc_f, gt_f = jnp.split(mod, 6, axis=-1)
        shc_a, scc_a, gtc_a, shc_f, scc_f, gtc_f = jnp.split(modc, 6, axis=-1)

        h = _modulate(_rmsnorm(x, g_attn[i]), sh_a, sc_a)
        hc = _modulate(_rmsnorm(xc, g_attn[i]), shc_a, scc_a)
        q, k, v = _split_qkv(h, w_qkv[i])
        qc, kc, vc = _split_qkv(hc, w_qkv[i])
        sink = None
        if m == 0:
            sink = sink_a[j]
        elif m == 1:
            q, k = _rmsnorm(q, gq_b[j]), _rmsnorm(k, gk_b[j])
            qc, kc = _rmsnorm(qc, gq_b[j]), _rmsnorm(kc, gk_b[j])
        q = q * ATTN_SCALE
        qc = qc * ATTN_SCALE
        if m == 0:
            o = _mixer_window(q, k, v, kc, vc, sink, cos, sin)
        elif m == 1:
            o = _mixer_global(q, k, v, kc, vc, cos, sin)
        else:
            o = _mixer_neighbourhood(q, k, v, kc, vc, rpb_c[j])
        x = x + gt_a * (o @ w_o[i])
        if not last:
            oc = _ctx_self_attention(qc, kc, vc, sink)
            xc = xc + gtc_a * (oc @ w_o[i])

        hf = _modulate(_rmsnorm(x, g_ffn[i]), sh_f, sc_f).reshape(b * n, d)
        if last:
            tokens = hf
        else:
            hfc = _modulate(_rmsnorm(xc, g_ffn[i]), shc_f, scc_f).reshape(-1, d)
            tokens = jnp.concatenate([hf, hfc], axis=0)
        y = _hier_moe(tokens, w_group[i], b_group[i], w_router[i], b_router[i],
                      w_gate[i], w_up[i], w_down[i]).astype(x.dtype)
        x = x + gt_f * y[:b * n].reshape(b, n, d)
        if not last:
            xc = xc + gtc_f * y[b * n:].reshape(xc.shape)
    return _rmsnorm(x, g_final)


def setup_inputs(seed=0):
    out = dict(first_inputs(seed))
    for name, value in second_inputs(seed + 1).items():
        if name != "x":
            out[name + "_2"] = value
    return out


def reference(
    x, mem, positions, norm_mix, norm_mem_q, norm_mem_kv, norm_ffn, ev_w_in, ev_q_gain,
    ev_k_gain, ev_w_s, ev_b_s, ev_ln_g, ev_ln_b, ev_w_out, od_w_in, od_w_g1, od_w_g2, od_b_g,
    od_o_gain, od_w_out, xa_w_q, xa_w_kv, xa_q_gain, xa_k_gain, xa_w_out, ffn_w_gu, ffn_w_down,
    c_2, ctx_2, c_ctx_2, w_ada_2, b_ada_2, g_attn_2, w_qkv_2, w_o_2, sink_a_2, gq_b_2, gk_b_2,
    rpb_c_2, g_ffn_2, w_group_2, b_group_2, w_router_2, b_router_2, w_gate_2, w_up_2, w_down_2,
    g_final_2,
):
    x = first_block(
        x, mem, positions, norm_mix, norm_mem_q, norm_mem_kv, norm_ffn, ev_w_in, ev_q_gain,
        ev_k_gain, ev_w_s, ev_b_s, ev_ln_g, ev_ln_b, ev_w_out, od_w_in, od_w_g1, od_w_g2,
        od_b_g, od_o_gain, od_w_out, xa_w_q, xa_w_kv, xa_q_gain, xa_k_gain, xa_w_out, ffn_w_gu,
        ffn_w_down,
    )
    return second_block(
        x, c_2, ctx_2, c_ctx_2, w_ada_2, b_ada_2, g_attn_2, w_qkv_2, w_o_2, sink_a_2, gq_b_2,
        gk_b_2, rpb_c_2, g_ffn_2, w_group_2, b_group_2, w_router_2, b_router_2, w_gate_2,
        w_up_2, w_down_2, g_final_2,
    )


_drawn_inputs = setup_inputs


def setup_inputs(seed=0):
    import zlib

    import numpy as np

    out = dict(_drawn_inputs(seed))
    spreads = {}
    factors = {'norm_mem_q': 6.74,
     'norm_mem_kv': 5.951,
     'ev_q_gain': 8.0,
     'ev_k_gain': 8.0,
     'ev_b_s': 3.166,
     'ev_ln_g': 4.764,
     'ev_ln_b': 8.0,
     'od_b_g': 8.0,
     'od_o_gain': 3.105,
     'xa_q_gain': 5.734,
     'xa_k_gain': 6.839,
     'b_ada_2': 2.804,
     'g_attn_2': 8.0,
     'sink_a_2': 8.0,
     'gq_b_2': 8.0,
     'gk_b_2': 8.0,
     'b_group_2': 21.111,
     'b_router_2': 7.339}
    for name, (base, spread) in spreads.items():
        noise = np.random.default_rng([zlib.crc32(name.encode()), seed]).standard_normal(out[name].shape)
        drawn = base * np.exp(spread * noise) if base else spread * noise
        out[name] = jnp.asarray(drawn.astype(out[name].dtype))
    for name, factor in factors.items():
        out[name] = (out[name] * factor).astype(out[name].dtype)
    return out
```

```python
from contextlib import ExitStack

import numpy as np

import concourse.bass as bass
from concourse import mybir

F32 = mybir.dt.float32
I32 = mybir.dt.int32
U32 = mybir.dt.uint32
ALU = mybir.AluOpType
ACT = mybir.ActivationFunctionType
AX = mybir.AxisListType.X

P = 128
D = 1024
KD = D // P
NB = 512
EPS = 1e-6
MASKED = -1e30
SLOTS = 6
SLOT = KD * NB

EV_HEADS, HD = 8, 64
GL_HEADS, GL_DK, GL_DV, GL_CHUNK, GL_TAU = 4, 128, 256, 64, 16.0
X_HEADS, X_HD = 4, 256
D_FF = 2816
FF_K = D_FF // P
FF_W = 256
FF_SLOTS = D_FF // FF_W
Q_HEADS, KV_HEADS = 16, 4
QKV = (Q_HEADS + 2 * KV_HEADS) * HD
N_EXP, N_GRP, EXP_H = 32, 4, 512
CAP = 512
EMPTY = 4096
MODW = 6 * D

C_IDENT, C_TRIL, C_CHUNK, C_SAME, C_BEFORE, C_ONES = (P * i for i in range(6))
C_WIN0 = 6 * P
C_WIN1 = C_WIN0 + NB
C_HALF = C_WIN1 + NB
C_IOTA = C_HALF + 2
C_GROUP = C_IOTA + N_EXP
C_ASG = C_GROUP + N_EXP
C_COS = C_ASG + 8
C_SIN = C_COS + 2 * HD
C_FREQ = C_SIN + 2 * HD
C_POW = C_FREQ + 8
C_ALL = C_POW + 20


def shape_constants():
    c = np.zeros((P, C_ALL), np.float32)
    i = np.arange(P)
    row, col = i[:, None], i[None, :]
    chunk = (row // GL_CHUNK) == (col // GL_CHUNK)
    c[:, C_IDENT:C_IDENT + P] = row == col
    c[:, C_TRIL:C_TRIL + P] = col <= row
    c[:, C_CHUNK:C_CHUNK + P] = chunk & (row <= col)
    c[:, C_SAME:C_SAME + P] = chunk
    c[:, C_BEFORE:C_BEFORE + P] = row < col
    c[:, C_ONES:C_ONES + P] = 1.0
    c[:, C_WIN0 + P:C_WIN0 + 2 * P] = np.where(col <= row, 0.0, MASKED)
    c[:, C_WIN1:C_WIN1 + P] = np.where(col >= row, 0.0, MASKED)
    c[:, C_HALF] = i < GL_CHUNK
    c[:, C_HALF + 1] = i >= GL_CHUNK
    c[:, C_IOTA:C_IOTA + N_EXP] = np.arange(N_EXP)
    c[:, C_GROUP:C_GROUP + N_EXP] = np.arange(N_EXP) // (N_EXP // N_GRP) - 100
    for t in range(4):
        for j in range(2):
            c[:, C_ASG + 2 * t + j] = 2 * (P * t + i) + j
    inv = (np.float32(10000.0) ** (-np.arange(16, dtype=np.float32) / np.float32(16))).astype(np.float32)
    for t in range(2):
        tok = P * t + i
        ar = (tok // 64).astype(np.float32)[:, None] * inv
        ac = (tok % 64).astype(np.float32)[:, None] * inv
        c[:, C_COS + HD * t:C_COS + HD * (t + 1)] = np.cos(np.concatenate([ar, ar, ac, ac], -1))
        c[:, C_SIN + HD * t:C_SIN + HD * (t + 1)] = np.concatenate(
            [-np.sin(ar), np.sin(ar), -np.sin(ac), np.sin(ac)], -1)
    c[:, C_FREQ:C_FREQ + 8] = np.float32(500000.0) ** (-np.arange(8, dtype=np.float32) * np.float32(2.0) / np.float32(16))
    c[:, C_POW:C_POW + 20] = -0.5
    return c


class Tally:

    def __init__(self):
        self.made, self.seen, self.latest = {}, {}, None

    def up(self, sem, by=1):
        self.made[id(sem)] = self.made.get(id(sem), 0) + by
        self.latest = (sem, self.made[id(sem)])
        return sem, by

    def last(self):
        return self.latest

    def count(self, sem):
        return self.seen.get(id(sem), 0)

    def next(self, sem, n=1):
        self.seen[id(sem)] = self.seen.get(id(sem), 0) + n
        return sem, self.seen[id(sem)]


def build_program(nc, I, out, upto="all", dbg=None):
    with ExitStack() as ctx:
        def sb(name, shape, dt=F32):
            return ctx.enter_context(nc.sbuf_tensor("sb_" + name, shape, dt))

        def sem(name):
            return ctx.enter_context(nc.semaphore(name))

        bank = [ctx.enter_context(nc.psum_tensor(f"bank{b}", [P, NB], F32)) for b in range(8)]
        T0, T1, S0, S1 = 4, 5, 6, 7

        ring = sb("ring", [P, SLOTS, SLOT])
        xs = sb("xs", [P, 4, D])
        hb = sb("hb", [P, 2, D])
        hT = sb("hT", [P, KD, 4 * P])
        A = sb("arena", [P, 12288])
        bc = sb("bc", [P, 3, D])
        cst = sb("cst", [P, C_ALL])
        st = sb("st", [P, 256])
        ropec = sb("ropec", [P, 2, 2, 8])
        posi = sb("posi", [P, 2], I32)
        idx = sb("idx", [P, 2, N_EXP * 4 + 2], U32)
        pick = sb("pick", [P, 2, 2], U32)
        rounds_i = sb("rounds_i", [P, 1], I32)

        ident = cst[:, C_IDENT:C_IDENT + P]
        hTf = hT[:].rearrange("p a b -> p (a b)")

        DR = {"mod": nc.dram_tensor("scratch_mod", [2, 2, MODW], F32, kind="Internal").ap(),
              "tok": nc.dram_tensor("scratch_tokens", [512, D], F32, kind="Internal").ap(),
              "tab": [nc.dram_tensor(f"scratch_table{l}", [N_EXP * CAP, 1], F32, kind="Internal").ap() for l in range(2)],
              "y": [nc.dram_tensor(f"scratch_y{l}", [1024, D], F32, kind="Internal").ap() for l in range(2)]}

        s = {n: sem(n) for n in (
            "act_back", "act_done", "act_go", "act_step", "ctx_loaded", "dest_ready", "dve_step", "e_ready",
            "es_ready", "fin_ready", "gla_dve", "h_ready", "idx_ready", "in_loaded", "loop_done_a", "loop_done_d",
            "marks_ready", "mod_rows", "mod_stored", "ms_ready", "mul_ready", "nmax_ready", "out_done",
            "pool_step", "pool_passed", "prep_ready", "proj_act", "rounds_ready", "rows_loaded", "rstd_ready", "sil_ready",
            "small_l", "small_loaded", "stat_ready", "stat_rstd", "tab_done", "tab_loaded", "w_used", "x_loaded",
            "y_loaded", "bc0", "bc1", "bc2", "tok_stored0", "tok_stored1",
        )}
        landed = [sem(f"landed{i}") for i in range(SLOTS)]
        readers = [("a", b) for b in (0, 1, 2, 3, T0, S0)] + [("d", b) for b in range(8)]
        full, free = ({r: {b: sem(f"{what}_{r}{b}") for q, b in readers if q == r} for r in "ad"} for what in ("full", "free"))

        def loop_sems(l):
            names = ["landed%d" % q for q in range(SLOTS)]
            for j in range(2):
                names += [f"{n}{j}" for n in (
                    "pe_gate", "pe_up", "pe_xT", "pe_aT", "pe_y_lo", "pe_y_hi", "silu", "xT_lo", "y_lo",
                    "acted", "xT_hi", "aT", "y_hi", "rows", "stored", "my_free")]
            names.append("picked")
            return {n: sem(f"moe{l}_{n}") for n in names}

        moe = [loop_sems(l) for l in range(2)]

        stream = []
        first = {}

        def dense(name, w, rows, cols, widths=None):
            first[name] = len(stream)
            kr = rows // P
            for n in range(cols // NB):
                for k0 in range(0, kr, KD):
                    k1 = min(k0 + KD, kr)
                    src = w[k0 * P:k1 * P, n * NB:(n + 1) * NB].rearrange("(k p) n -> p k n", p=P)
                    stream.append((k1 - k0, NB, src))

        def gate_up(name, w):
            first[name] = len(stream)
            v = w.rearrange("(k p) (two n) -> p k two n", p=P, two=2)
            for n in range(FF_SLOTS):
                stream.append((KD, "gu", v[:, :, :, n * FF_W:(n + 1) * FF_W]))

        for l in range(2):
            dense(f"ada{l}", I["w_ada_2"][l], D, MODW)
        for l in range(2):
            if l == 0:
                dense("ev_in", I["ev_w_in"][0], D, 5 * NB)
                dense("ev_out", I["ev_w_out"][0], D, D)
            else:
                dense("od_in", I["od_w_in"][0], D, 6 * NB)
                dense("od_out", I["od_w_out"][0], D, D)
            dense(f"xa_kv{l}", I["xa_w_kv"][l], D, 2 * D)
            dense(f"xa_q{l}", I["xa_w_q"][l], D, D)
            dense(f"xa_out{l}", I["xa_w_out"][l], D, D)
            gate_up(f"ff_in{l}", I["ffn_w_gu"][l])
            dense(f"ff_out{l}", I["ffn_w_down"][l], D_FF, D)
        moe_at = {}
        for l in range(2):
            dense(f"qkv{l}", I["w_qkv_2"][l], D, QKV)
            dense(f"w_o{l}", I["w_o_2"][l], D, D)
            moe_at[l] = len(stream)

        SLOT_USED = ["pe_gate0", "pe_up0", "pe_y_hi0", "pe_gate1", "pe_up1", "pe_y_hi1"]

        def slot_of_gu(n):
            return ring[:, n % SLOTS, :].rearrange("p (k n) -> p k n", k=KD)

        def slot_of(n):
            k, cols, _ = stream[n]
            v = ring[:, n % SLOTS, 0:k * NB]
            return v.rearrange("p (k n) -> p k n", k=k)

        STAGES = ["mod", "mix0", "xa0", "ffn0", "mix1", "xa1", "ffn1", "att0", "route0", "moe0", "att1", "route1", "moe1", "all"]
        LIM = STAGES.index(upto)

        def on(stage):
            return STAGES.index(stage) <= LIM

        ends = {"mod": first["ev_in"], "mix0": first["xa_kv0"], "xa0": first["ff_in0"], "ffn0": first["od_in"],
                "mix1": first["xa_kv1"], "xa1": first["ff_in1"], "ffn1": first["qkv0"], "att0": moe_at[0],
                "route0": moe_at[0], "moe0": moe_at[0]}
        n_stream = ends.get(upto, len(stream))

        def view(at, *dims):
            n = int(np.prod(dims))
            v = A[:, at:at + n]
            if len(dims) == 1:
                return v
            names = "abcde"[:len(dims)]
            return v.rearrange(f"p ({' '.join(names)}) -> p {' '.join(names)}", **dict(zip(names, dims)))

        modrow = view(0, 2, MODW)
        ev_p = view(0, 2, 5 * NB)
        ev_T = view(5120, 16, 2 * P)
        ev_o = view(9216, 2, D)
        ev_ws = view(11264, 8, P)
        ev_wsT = hTf[:, 3072:4096].rearrange("p (g i) -> p g i", g=8)
        xa_q, xa_k, xa_v = view(0, 2, D), view(2048, 2, D), view(4096, 2, D)
        xa_qT, xa_kT, xa_o = view(6144, KD, 2 * P), view(8192, KD, 2 * P), view(10240, 2, D)
        at_s = hTf[:, 0:1024].rearrange("p (b n) -> p b n", b=2)
        at_e = hTf[:, 1024:2048].rearrange("p (b n) -> p b n", b=2)
        at_eT = hTf[:, 2048:3072].rearrange("p (b k n) -> p b k n", b=2, k=4)
        ff_T = view(0, FF_K, 2 * P)
        ff_sil = view(5632, 2, FF_W)
        ff_act = view(6144, 2, FF_W)
        gl_p = view(0, 2, 6 * NB)
        gl_b = view(6144, 2, NB)
        gl_qT = view(7168, 2, GL_HEADS, 2 * P)
        gl_kT = view(9216, GL_HEADS, 2 * P)
        gl_ks = view(10240, 2, 2, NB)
        gl_S = hTf[:, 0:3072].rearrange("p (h n v) -> p h n v", h=GL_HEADS, n=3)
        gl_att = hTf[:, 3072:3584].rearrange("p (b i) -> p b i", b=4)
        gl_o = gl_p[:, :, 0:D]
        jq = view(0, 4, QKV)
        j_kT = view(6144, KV_HEADS, 4 * P)
        j_qT = view(8192, 2, Q_HEADS, P)
        mx = view(0, 2, D)
        mxT = view(2048, 2, KD, P)
        mact = view(4096, 2, EXP_H)
        mactT = view(5120, 2, EXP_H // P, P)
        my = view(6144, 2, D)
        msil = view(8192, 2, EXP_H)
        mw = view(9216, KD, 36)
        mlog = view(9504, 4, 36)
        monehot = view(9648, 4, 2, N_EXP)
        mtab = view(9904, P)
        mtmp = view(10032, 4, 4 * N_EXP)
        mdest = sb("mdest", [P, 8], U32)
        mwt = st[:, 152:160]

        g1, g2 = view(9216, KD, 16), A[0:16, 9344:9344 + NB]
        z1, z1T = view(9856, 2, 16), A[0:16, 9888:10144].rearrange("p (t i) -> p t i", t=2)
        dec = st[:, 160:176].rearrange("p (t h c) -> p t h c", t=2, h=GL_HEADS)
        sink8, sink1 = st[:, 176:192], st[:, 192:208]
        rb = st[:, 208:244]
        silu_c = st[:, 208:224].rearrange("p (k c) -> p k c", c=2)
        cond = st[:, 224:240].rearrange("p (k c) -> p k c", c=2)

        dr_mod = DR["mod"]

        def heads_T(v, h, t0, n):
            return v[0:HD, h, t0 * P:t0 * P + n]

        ev_jobs = []
        for t in range(2):
            for h in range(EV_HEADS):
                nk = (t + 1) * P
                ev_jobs.append(dict(
                    scores=[(0, nk, [(heads_T(ev_T, h, t, P), heads_T(ev_T, EV_HEADS + h, 0, nk))])], nk=nk,
                    mask=cst[:, C_WIN0 + (1 - t) * P:C_WIN0 + 2 * P], scale=HD ** -0.5, sink=None,
                    values=[ev_p[:, k, 2 * NB + h * HD:2 * NB + (h + 1) * HD] for k in range(t + 1)],
                    out=ev_o[:, t, h * HD:(h + 1) * HD]))
        xa_jobs = []
        for t in range(2):
            for h in range(X_HEADS):
                xa_jobs.append(dict(
                    scores=[(0, 2 * P, [(xa_qT[:, 2 * h + k, t * P:(t + 1) * P], xa_kT[:, 2 * h + k, :]) for k in range(2)])],
                    nk=2 * P, mask=None, scale=X_HD ** -0.5, sink=None,
                    values=[xa_v[:, k, h * X_HD:(h + 1) * X_HD] for k in range(2)],
                    out=xa_o[:, t, h * X_HD:(h + 1) * X_HD]))

        def joint_jobs(l, t):
            jobs = []
            for h in range(Q_HEADS):
                g = h // (Q_HEADS // KV_HEADS)
                rot, plain = j_qT[0:HD, 0, h, :], j_qT[0:HD, 1, h, :]
                parts = [(2 * P, 2 * P, [(plain, heads_T(j_kT, g, 2, 2 * P))])]
                tiles = [2, 3]
                if t < 2:
                    parts.insert(0, (0, 2 * P, [(rot, heads_T(j_kT, g, 0, 2 * P))]))
                    tiles = [0, 1, 2, 3]
                else:
                    parts = [(0, 2 * P, parts[0][2])]
                jobs.append(dict(
                    scores=parts, nk=P * len(tiles), mask=cst[:, (C_WIN0, C_WIN1)[t]:][:, 0:NB] if l == 0 and t < 2 else None,
                    scale=HD ** -0.5, sink=h if l == 0 else None,
                    values=[jq[:, k, D + (KV_HEADS + g) * HD:D + (KV_HEADS + g + 1) * HD] for k in tiles],
                    out=jq[:, t, h * HD:(h + 1) * HD]))
            return jobs

        block = ctx.enter_context(nc.Block(no_gpsimd_drain=False))

        @block.sync
        def _(sp):
            c = Tally()
            sp.dma_start(xs[:, 0:2, :], I["x"][0].rearrange("(t p) d -> p t d", p=P)).then_inc(s["x_loaded"], 16)
            sp.dma_start(xs[:, 2:4, :], I["mem"][0].rearrange("(t p) d -> p t d", p=P)).then_inc(s["x_loaded"], 16)

            def load(n):
                k, cols, src = stream[n]
                dst = slot_of(n)
                if cols == "gu":
                    dst = ring[:, n % SLOTS, :].rearrange("p (k two n) -> p k two n", k=KD, two=2)
                if n >= SLOTS:
                    sp.wait_ge(s["w_used"], n - SLOTS + 1)
                if cols == "gu":
                    for half in range(2):
                        sp.dma_start(dst[:, :, half, :], src[:, :, half, :]).then_inc(landed[n % SLOTS], 16)
                else:
                    h = max(1, k // 2)
                    sp.dma_start(dst[:, 0:h, :], src[:, 0:h, :]).then_inc(landed[n % SLOTS], 16)
                    sp.dma_start(dst[:, h:k, :], src[:, h:k, :]).then_inc(landed[n % SLOTS], 16)

            def experts(l):
                wg, wu, wd = I["w_gate_2"][l], I["w_up_2"][l], I["w_down_2"][l]

                def pair(e, step=None):
                    for j in range(2):
                        for m, w in enumerate((wg, wu, wd)):
                            q = 3 * j + m
                            if step is not None:
                                sp.wait_ge(moe[l][SLOT_USED[q]], step)
                            src = w[bass.ds(e + j, 1), :, :] if step is not None else w[e + j:e + j + 1, :, :]
                            src = src.rearrange("o (k p) n -> p (o k) n", p=P)
                            dst = ring[:, q, :].rearrange("p (k n) -> p k n", k=src.shape[1])
                            sp.dma_start(dst, src).then_inc(moe[l][f"landed{q}"], 16)

                sp.wait_ge(s["w_used"], moe_at[l])
                pair(0)
                sp.wait_ge(s["rounds_ready"], l + 1)
                rounds = sp.value_load(rounds_i[0:1, 0:1], min_val=1, max_val=4)
                with sp.Fori(1, rounds * (N_EXP // 2)) as i:
                    pair((i % (N_EXP // 2)) * 2, i)

            at = 0
            for l in range(2):
                for n in range(at, min(moe_at[l], n_stream)):
                    load(n)
                at = moe_at[l]
                if l == 0 and on("att0"):
                    pass
                if on(f"moe{l}"):
                    experts(l)
                    sp.wait_ge(s["loop_done_d"], l + 1)
            if on("all"):
                sp.wait_ge(*c.next(s["fin_ready"]))
                sp.dma_start(out[0].rearrange("(t p) d -> p t d", p=P), hb[:, 0:2, :]).then_inc(s["out_done"], 16)
            else:
                sp.wait_ge(*c.next(s["fin_ready"]))
                sp.dma_start(out[0].rearrange("(t p) d -> p t d", p=P), xs[:, 0:2, :]).then_inc(s["out_done"], 16)
                if dbg is not None:
                    sp.dma_start(dbg.rearrange("(t p) d -> p t d", p=P), xs[:, 2:4, :]).then_inc(s["out_done"], 16)
            sp.wait_ge(s["out_done"], 16 if dbg is None else 32)


        @block.tensor
        def _(pe):
            c = Tally()
            busy = {}

            def claim(b):
                if b in busy:
                    pe.wait_ge(*busy[b])

            def publish(ins, b, reader, until=None):
                ins.then_inc(*c.up(full[reader][b]))
                busy[b] = until or c.next(free[reader][b])

            pending = [0]

            def using(ins, n):
                if n > pending[0]:
                    pending[0] = n
                    ins.then_inc(*c.up(s["w_used"]))

            def weights(n):
                pe.wait_ge(landed[n % SLOTS], 32 * (n // SLOTS + 1))

            def transpose_tile(src, readers="ad", chunks=KD, hi=True):
                for half in range(chunks // 4):
                    b = (T0, T1)[half]
                    claim(b)
                    for k in range(4):
                        ins = pe.transpose(bank[b][:, k * P:(k + 1) * P],
                                           src[:, (4 * half + k) * P:(4 * half + k + 1) * P], ident)
                    publish(ins, b, readers[half])

            def norm(n_tiles, at=0):
                for i in range(n_tiles):
                    pe.wait_ge(*c.next(s["h_ready"]))
                    transpose_tile(hb[:, i % 2, :])

            def hT_settled():
                claim(T0)
                claim(T1)

            def gemm(n0, slots, tiles, reader, lhs=None, rows=P):
                u = 0
                for i in range(slots):
                    w = slot_of(n0 + i)
                    weights(n0 + i)
                    for t in tiles:
                        b = u % 4
                        claim(b)
                        for k in range(KD):
                            src = lhs(k, t) if lhs else hT[:, k, t * P:(t + 1) * P]
                            ins = pe.matmul(bank[b][0:rows, :], src, w[:, k, :], start=k == 0, stop=k == KD - 1)
                            if k == 0 and t == tiles[0] and n0 + i > 0:
                                using(ins, n0 + i)
                        who = reader(i, t)
                        publish(ins, b, who)
                        u += 1

            copy_by = lambda i, t: "ad"[t % 2]

            pe.wait_ge(s["in_loaded"], 64)
            pe.wait_ge(*c.next(s["act_done"]))
            gemm(0, 24, [0], lambda i, t: "d", lhs=lambda k, t: silu_c[:, k, :], rows=2)

            def attention(jobs):
                n = len(jobs)
                e0 = c.count(s["e_ready"])
                for j in range(n + 2):
                    if j < n:
                        sc = S0 + j % 2
                        claim(sc)
                        for col, width, pairs in jobs[j]["scores"]:
                            for m, (a, b) in enumerate(pairs):
                                ins = pe.matmul(bank[sc][:, col:col + width], a, b, start=m == 0, stop=m == len(pairs) - 1)
                        publish(ins, sc, "d", None if jobs[j]["mask"] is not None else (s["e_ready"], e0 + j + 1))
                    if 1 <= j <= n:
                        i = j - 1
                        pe.wait_ge(*c.next(s["e_ready"]))
                        b = T0 + i % 2
                        claim(b)
                        for k in range(jobs[i]["nk"] // P):
                            ins = pe.transpose(bank[b][:, k * P:(k + 1) * P], at_e[:, i % 2, k * P:(k + 1) * P], ident)
                        publish(ins, b, "ad"[i % 2])
                    if j >= 2:
                        i = j - 2
                        pe.wait_ge(*eT_copied[i])
                        claim(i % 2)
                        v = jobs[i]["values"]
                        for k in range(len(v)):
                            ins = pe.matmul(bank[i % 2][:, 0:v[k].shape[-1]], at_eT[:, i % 2, k, :], v[k],
                                            start=k == 0, stop=k == len(v) - 1)
                        publish(ins, i % 2, "d")
                    if 1 <= j <= n:
                        eT_copied[j - 1] = busy[T0 + (j - 1) % 2]

            eT_copied = {}

            def transpose_heads(src, heads, n_b=0):
                for g in range(heads // 4):
                    b = (T0, T1)[(g + n_b) % 2]
                    claim(b)
                    for k in range(4):
                        ins = pe.transpose(bank[b][0:HD, k * P:(k + 1) * P], src(4 * g + k), ident)
                    publish(ins, b, "ad"[(g + n_b) % 2])

            def out_tiles(src, tiles):
                for b in (0, 1):
                    claim(b)
                for t in tiles:
                    transpose_tile(src[:, t, :])

            def even_mixer():
                norm(2)
                hT_settled()
                gemm(first["ev_in"], 5, [0, 1], lambda i, t: "a" if i >= 3 else copy_by(i, t))
                for t in (1, 0):
                    pe.wait_ge(*c.next(s["prep_ready"]))
                    transpose_heads(lambda h: ev_p[:, t, h * HD:(h + 1) * HD], 16)
                pe.wait_ge(*c.next(s["prep_ready"]))
                transpose_tile(ev_ws.rearrange("p g j -> p (g j)"))
                hT_settled()
                for t in range(2):
                    pe.wait_ge(*c.next(s["prep_ready"]))
                    claim(2 + t)
                    for g in range(EV_HEADS):
                        ins = pe.matmul(bank[2 + t][:, g * HD:(g + 1) * HD], ev_wsT[:, g, :],
                                        ev_p[:, t, 4 * NB + g * HD:4 * NB + (g + 1) * HD], start=True, stop=True)
                    publish(ins, 2 + t, "d")
                attention(ev_jobs)
                for b in (2, 3):
                    claim(b)
                out_tiles(ev_o, [0, 1])
                hT_settled()
                gemm(first["ev_out"], 2, [0, 1], lambda i, t: "d")

            def cross(l):
                norm(4)
                hT_settled()
                gemm(first[f"xa_kv{l}"], 4, [2, 3], copy_by)
                gemm(first[f"xa_q{l}"], 2, [0, 1], copy_by)
                for src in (xa_k, xa_q):
                    for t in range(2):
                        pe.wait_ge(*c.next(s["prep_ready"]))
                        transpose_tile(src[:, t, :])
                hT_settled()
                attention(xa_jobs)
                out_tiles(xa_o, [0, 1])
                hT_settled()
                gemm(first[f"xa_out{l}"], 2, [0, 1], lambda i, t: "d")

            def feed_forward(l):
                norm(2)
                hT_settled()
                n0 = first[f"ff_in{l}"]
                units = [(i, t) for i in range(FF_SLOTS) for t in range(2)]
                m0 = c.count(s["mul_ready"])

                def turn(u):
                    pe.wait_ge(*c.next(s["mul_ready"]))
                    b = T0 + u % 2
                    claim(b)
                    for k in range(2):
                        ins = pe.transpose(bank[b][:, k * P:(k + 1) * P], ff_act[:, u % 2, k * P:(k + 1) * P], ident)
                    publish(ins, b, "ad"[u % 2])

                for u, (i, t) in enumerate(units):
                    if t == 0:
                        weights(n0 + i)
                    w = slot_of_gu(n0 + i)
                    claim(u % 4)
                    for k in range(KD):
                        ins = pe.matmul(bank[u % 4][:, :], hT[:, k, t * P:(t + 1) * P], w[:, k, :], start=k == 0, stop=k == KD - 1)
                        if k == 0 and t == 0:
                            using(ins, n0 + i)
                    publish(ins, u % 4, "a", (s["mul_ready"], m0 + u + 1))
                    if u >= 1:
                        turn(u - 1)
                turn(len(units) - 1)
                hT_settled()
                n0 = first[f"ff_out{l}"]
                q = 0
                for n in range(2):
                    for k0 in range(0, FF_K, KD):
                        weights(n0 + q)
                        w = slot_of(n0 + q)
                        nk = min(KD, FF_K - k0)
                        for t in range(2):
                            b = 2 * n + t
                            if k0 == 0:
                                claim(b)
                            for k in range(nk):
                                ins = pe.matmul(bank[b][:, :], ff_T[:, k0 + k, t * P:(t + 1) * P], w[:, k, :],
                                                start=k0 + k == 0, stop=k0 + k == FF_K - 1)
                                if k == 0 and t == 0:
                                    using(ins, n0 + q)
                            if k0 + nk == FF_K:
                                publish(ins, b, "d")
                        q += 1

            def linear_attention():
                norm(2)
                hT_settled()
                pe.wait_ge(s["small_loaded"], 64)
                for t in range(2):
                    claim(S0 + t)
                    for k in range(KD):
                        ins = pe.matmul(bank[S0 + t][:, 0:16], hT[:, k, t * P:(t + 1) * P], g1[:, k, :], start=k == 0, stop=k == KD - 1)
                    publish(ins, S0 + t, "d")
                gemm(first["od_in"], 2, [0, 1], copy_by)
                for t in range(2):
                    claim(S0 + t)
                    ins = pe.transpose(bank[S0 + t][0:16, 0:P], z1[:, t, :], ident)
                    publish(ins, S0 + t, "d")
                gemm(first["od_in"] + 2, 2, [0, 1], copy_by)
                for t in range(2):
                    claim(S0 + t)
                    ins = pe.matmul(bank[S0 + t][:, :], z1T[:, t, :], g2, start=True, stop=True)
                    publish(ins, S0 + t, "d")
                gemm(first["od_in"] + 4, 2, [0, 1], lambda i, t: "a")
                for t in range(2):
                    pe.wait_ge(*c.next(s["gla_dve"]))
                    la = hb[:, t, 0:NB]
                    claim(S0)
                    publish(pe.matmul(bank[S0][:, :], cst[:, C_CHUNK:C_CHUNK + P], la, start=True, stop=True), S0, "a")
                    claim(S1)
                    publish(pe.matmul(bank[S1][:, :], cst[:, C_SAME:C_SAME + P], la, start=True, stop=True), S1, "d")
                    claim(T0)
                    for h in range(GL_HEADS):
                        ins = pe.matmul(bank[T0][:, 2 * h:2 * h + 2], la[:, h * P:(h + 1) * P], cst[:, C_HALF:C_HALF + 2], start=True, stop=True)
                    publish(ins, T0, "a")
                for t in range(2):
                    pe.wait_ge(*c.next(s["prep_ready"]))
                    transpose_tile(gl_p[:, t, 0:D])
                hT_settled()
                n = 0
                d0 = c.count(s["gla_dve"])
                for t in range(2):
                    for h in range(GL_HEADS):
                        b = S0 + n % 2
                        claim(b)
                        for half in range(2):
                            i0 = t * P + half * GL_CHUNK
                            ins = pe.matmul(bank[b][:, half * GL_CHUNK:(half + 1) * GL_CHUNK], gl_kT[:, h, t * P:(t + 1) * P],
                                            gl_qT[:, half, h, i0:i0 + GL_CHUNK], start=True, stop=True)
                        publish(ins, b, "d", (s["gla_dve"], d0 + n + 1))
                        if t == 0:
                            v = lambda tt: gl_p[:, tt, D + h * GL_DV:D + (h + 1) * GL_DV]
                            claim(T0)
                            for m in range(2):
                                ins = pe.matmul(bank[T0][:, m * GL_DV:(m + 1) * GL_DV], gl_ks[:, 0, m, h * P:(h + 1) * P], v(0), start=True, stop=True)
                            publish(ins, T0, "d")
                            claim(T1)
                            publish(pe.matmul(bank[T1][:, 0:GL_DV], gl_ks[:, 1, 0, h * P:(h + 1) * P], v(1), start=True, stop=True), T1, "d")
                        n += 1
                        if n >= 2:
                            gla_out(n - 2)
                gla_out(7)
                for t in range(2):
                    pe.wait_ge(*c.next(s["prep_ready"]))
                    transpose_tile(gl_p[:, t, 0:D])
                hT_settled()
                gemm(first["od_out"], 2, [0, 1], lambda i, t: "d")

            def gla_out(n):
                t, h = n // GL_HEADS, n % GL_HEADS
                pe.wait_ge(*c.next(s["gla_dve"]))
                b = n % 4
                claim(b)
                o = bank[b][:, 0:GL_DV]
                parts = [(gl_att[:, n % 4, :], gl_p[:, t, D + h * GL_DV:D + (h + 1) * GL_DV])]
                for half in range(2):
                    chunk = 2 * t + half
                    if chunk:
                        parts.append((gl_qT[:, half, h, t * P:(t + 1) * P], gl_S[:, h, chunk - 1, :]))
                for m, (x, y) in enumerate(parts):
                    ins = pe.matmul(o, x, y, start=m == 0, stop=m == len(parts) - 1)
                publish(ins, b, "d")

            def joint(l):
                norm(2)
                norm(2)
                hT_settled()
                n0 = first[f"qkv{l}"]
                if l == 0:
                    gemm(n0, 3, [0, 1, 2, 3], copy_by)
                else:
                    gemm(n0, 2, [0, 1], copy_by)
                    gemm(n0 + 2, 1, [0, 1, 2, 3], copy_by)
                nb = 0
                for t in range(4):
                    pe.wait_ge(*c.next(s["prep_ready"]))
                    transpose_heads(lambda h: jq[:, t, D + h * HD:D + (h + 1) * HD], KV_HEADS, nb)
                    nb += 1
                for t in range(4 if l == 0 else 2):
                    if t < 2:
                        pe.wait_ge(*c.next(s["prep_ready"]))
                        transpose_heads(lambda h: hb[:, 0, h * HD:(h + 1) * HD], Q_HEADS)
                    else:
                        pe.wait_ge(*c.next(s["prep_ready"]))
                    transpose_heads(lambda h: jq[:, t, h * HD:(h + 1) * HD], Q_HEADS)
                    hT_settled()
                    attention(joint_jobs(l, t))
                out_tiles(jq[:, :, 0:D], range(4 if l == 0 else 2))
                hT_settled()
                gemm(first[f"w_o{l}"], 2, [0, 1, 2, 3] if l == 0 else [0, 1], lambda i, t: "d")

            def route(l, tiles):
                norm(2)
                if tiles == 4:
                    norm(2)
                hT_settled()
                pe.wait_ge(*c.next(s["small_l"], 64))
                for t in range(tiles):
                    claim(t)
                    for k in range(KD):
                        ins = pe.matmul(bank[t][:, 0:36], hT[:, k, t * P:(t + 1) * P], mw[:, k, :], start=k == 0, stop=k == KD - 1)
                        if t == 0 and k == 0:
                            using(ins, moe_at[l])
                    publish(ins, t, "d")
                pe.wait_ge(*c.next(s["marks_ready"]))
                claim(S0)
                for t in range(tiles):
                    marks = lambda q: mtmp[:, q, 0:N_EXP]
                    for q in range(t + 1):
                        pe.matmul(bank[S0][:, t * N_EXP:(t + 1) * N_EXP],
                                  cst[:, (C_BEFORE if q == t else C_ONES):][:, 0:P], marks(q), start=q == 0, stop=q == t)
                for q in range(tiles):
                    ins = pe.matmul(bank[S0][:, 4 * N_EXP:5 * N_EXP], cst[:, C_ONES:C_ONES + P], mtmp[:, q, 0:N_EXP],
                                    start=q == 0, stop=q == tiles - 1)
                publish(ins, S0, "d")
                pe.wait_ge(*c.next(s["tab_loaded"], 64))
                claim(S1)
                publish(pe.transpose(bank[S1][:, 0:P], mtab, ident), S1, "d")

            def experts(l):
                m = moe[l]
                pe.wait_ge(*c.next(s["rounds_ready"]))
                rounds = pe.value_load(rounds_i[0:1, 0:1], min_val=1, max_val=4)
                for b in range(8):
                    claim(b)

                def turn_rows(j, count):
                    pe.wait_ge(m[f"rows{j}"], count * 16)
                    for half, b in enumerate((T0, T1)):
                        for k in range(4):
                            ins = pe.transpose(bank[b][:, k * P:(k + 1) * P], mx[:, j, (4 * half + k) * P:(4 * half + k + 1) * P], ident)
                    ins.then_inc(m[f"pe_xT{j}"], 1)

                turn_rows(0, 1)
                with pe.Fori(0, rounds * (N_EXP // 2)) as i:
                    for j in range(2):
                        slots = [ring[:, 3 * j + q, :].rearrange("p (k n) -> p k n", k=(KD, KD, 4)[q]) for q in range(3)]
                        pe.wait_ge(m[f"xT_lo{j}"], i + 1)
                        pe.wait_ge(m[f"xT_hi{j}"], i + 1)
                        for q, name in enumerate(("pe_gate", "pe_up")):
                            pe.wait_ge(m[f"landed{3 * j + q}"], i * 16 + 16)
                            for k in range(KD):
                                ins = pe.matmul(bank[2 * j + q][:, :], mxT[:, j, k, :], slots[q][:, k, :], start=k == 0, stop=k == KD - 1)
                            ins.then_inc(m[f"{name}{j}"], 1)
                        turn_rows(1 - j, i + 1 + j)
                        pe.wait_ge(m[f"acted{j}"], i + 2)
                        for k in range(4):
                            ins = pe.transpose(bank[2 * j][:, k * P:(k + 1) * P], mact[:, j, k * P:(k + 1) * P], ident)
                        ins.then_inc(m[f"pe_aT{j}"], 1)
                        pe.wait_ge(m[f"aT{j}"], i + 1)
                        pe.wait_ge(m[f"landed{3 * j + 2}"], i * 16 + 16)
                        pe.wait_ge(m[f"y_lo{1 - j}"], i + 1)
                        pe.wait_ge(m[f"y_hi{1 - j}"], i + 1)
                        for n in range(2):
                            for k in range(4):
                                ins = pe.matmul(bank[S0 + n][:, :], mactT[:, j, k, :], slots[2][:, k, n * NB:(n + 1) * NB], start=k == 0, stop=k == 3)
                            ins.then_inc(m[f"pe_y_{('lo', 'hi')[n]}{j}"], 1)
                pe.wait_ge(s["loop_done_a"], l + 1)
                pe.wait_ge(s["loop_done_d"], l + 1)

            if on("mix0"):
                even_mixer()
            if on("xa0"):
                cross(0)
            if on("ffn0"):
                feed_forward(0)
            if on("mix1"):
                linear_attention()
            if on("xa1"):
                cross(1)
            if on("ffn1"):
                feed_forward(1)
            for l in range(2):
                if on(f"att{l}"):
                    joint(l)
                if on(f"route{l}"):
                    route(l, 4 - 2 * l)
                if on(f"moe{l}"):
                    experts(l)

        @block.scalar
        def _(act):
            c = Tally()

            def take(b):
                act.wait_ge(*c.next(full["a"][b]))

            def release(ins, b):
                ins.then_inc(*c.up(free["a"][b]))

            def copy_out(b, dst, src=None):
                take(b)
                release(act.activation(dst, bank[b][:, :] if src is None else src, ACT.Copy), b)

            def lo_chunks(dst):
                copy_out(T0, dst, bank[T0][:, :].rearrange("p (k n) -> p k n", k=4))

            def flag(sem_):
                act.wait_ge(*c.last())
                act.activation(st[:, 60:61], cst[:, 0:1], ACT.Copy).then_inc(*c.up(sem_))

            def turned(cols):
                for t in cols:
                    lo_chunks(hT[:, 0:4, t * P:(t + 1) * P])

            def norm(cols):
                c.next(s["h_ready"], len(cols))
                turned(cols)

            def attention(jobs):
                n = len(jobs)
                for j in range(n + 1):
                    if j < n:
                        job = jobs[j]
                        nk, sc = job["nk"], S0 + j % 2
                        act.wait_ge(*c.next(s["nmax_ready"]))
                        src = at_s[:, j % 2, 0:nk]
                        if job["mask"] is None:
                            src = bank[sc][:, 0:nk]
                        nm = st[:, 16 + j % 4:17 + j % 4]
                        ins = act.activation(at_e[:, j % 2, 0:nk], src, ACT.Exp, bias=nm, scale=job["scale"],
                                             accum_out=st[:, 20 + j % 4:21 + j % 4])
                        ins.then_inc(*c.up(s["e_ready"]))
                        if job["sink"] is not None:
                            h = job["sink"]
                            act.activation(st[:, 24 + j % 4:25 + j % 4], sink1[:, h:h + 1], ACT.Exp, bias=nm).then_inc(*c.up(s["es_ready"]))
                    if j >= 1 and (j - 1) % 2 == 0:
                        i = j - 1
                        k = jobs[i]["nk"] // P
                        copy_out(T0, at_eT[:, i % 2, 0:k, :], bank[T0][:, 0:k * P].rearrange("p (k n) -> p k n", k=k))

            def heads_out(dst, heads, n_b=0):
                for g in range(heads // 4):
                    if (g + n_b) % 2 == 0:
                        copy_out(T0, dst(4 * g), bank[T0][0:HD, :].rearrange("p (k n) -> p k n", k=4))

            act.wait_ge(s["in_loaded"], 64)
            act.activation(silu_c, cond, ACT.Silu).then_inc(*c.up(s["act_done"]))
            act.wait_ge(*c.next(s["act_go"]))
            act.activation(ropec[:].rearrange("p t c j -> p (t c j)"), st[:, 64:96], ACT.Sin).then_inc(*c.up(s["act_back"]))

            def even_mixer():
                norm([0, 1])
                act.wait_ge(s["mod_stored"], 32)
                for i in range(5):
                    for t in range(2):
                        b = (2 * i + t) % 4
                        dst = ev_p[:, t, i * NB:(i + 1) * NB]
                        if i >= 3:
                            take(b)
                            release(act.activation(dst, bank[b][:, :], ACT.Gelu), b)
                        elif t == 0:
                            copy_out(b, dst)
                    if i in (1, 4):
                        flag(s["proj_act"])
                for t in (1, 0):
                    heads_out(lambda h: ev_T[0:HD, h:h + 4, t * P:(t + 1) * P], 16)
                lo_chunks(ev_wsT[:, 0:4, :])
                attention(ev_jobs)
                turned([0, 1])

            def cross():
                norm([2, 3])
                norm([0, 1])
                for i in range(4):
                    for t in range(2):
                        if t == 0:
                            copy_out((2 * i + t) % 4, (xa_k, xa_v)[i // 2][:, t, (i % 2) * NB:(i % 2 + 1) * NB])
                flag(s["proj_act"])
                for i in range(2):
                    copy_out((2 * i) % 4, xa_q[:, 0, i * NB:(i + 1) * NB])
                flag(s["proj_act"])
                for dst in (xa_kT, xa_qT):
                    for t in range(2):
                        lo_chunks(dst[:, 0:4, t * P:(t + 1) * P])
                attention(xa_jobs)
                turned([0, 1])

            def feed_forward():
                norm([0, 1])
                n = 2 * FF_SLOTS
                for u in range(n + 2):
                    if u < n:
                        take(u % 4)
                        if u >= 2:
                            act.wait_ge(*c.next(s["mul_ready"]))
                        act.activation(ff_sil[:, u % 2, :], bank[u % 4][:, 0:FF_W], ACT.Silu).then_inc(*c.up(s["sil_ready"]))
                    if u >= 2 and (u - 2) % 2 == 0:
                        i, t = (u - 2) // 2, 0
                        copy_out(T0, ff_T[:, 2 * i:2 * i + 2, 0:P], bank[T0][:, 0:2 * P].rearrange("p (k n) -> p k n", k=2))
                c.next(s["mul_ready"], 2)

            def linear_attention():
                norm([0, 1])
                for i in range(6):
                    for t in range(2):
                        b = (2 * (i % 2) + t) % 4
                        dst = gl_p[:, t, i * NB:(i + 1) * NB]
                        if i >= 4:
                            take(b)
                            release(act.activation(dst, bank[b][:, :], ACT.Silu), b)
                        elif t == 0:
                            copy_out(b, dst)
                flag(s["proj_act"])
                for t in range(2):
                    act.wait_ge(*c.next(s["act_go"]))
                    v = hb[:, t, NB:2 * NB]
                    act.activation(v, v, ACT.Exp, scale=-1.0).then_inc(*c.up(s["act_step"]))
                    act.wait_ge(*c.last())
                    act.activation(v, v, ACT.Ln, bias=1.0).then_inc(*c.up(s["act_back"]))
                k = 1.0 / GL_TAU
                for t in range(2):
                    take(S0)
                    act.activation(gl_b[:, t, :], bank[S0][:, :], ACT.Copy).then_inc(*c.up(s["act_back"]))
                    take(T0)
                    release(act.activation(dec[:, t, :, :].rearrange("p h c -> p (h c)"), bank[T0][:, 0:8], ACT.Exp, scale=k), T0)
                    act.wait_ge(*c.next(s["act_go"]))
                    act.wait_ge(*c.last())
                    act.activation(gl_b[:, t, :], bank[S0][:, :], ACT.Exp, scale=-k).then_inc(*c.up(s["act_step"]))
                    release(act.activation(hb[:, t, 0:NB], bank[S0][:, :], ACT.Exp, scale=k), S0)
                    v = hb[:, t, NB:2 * NB]
                    act.activation(v, v, ACT.Exp, scale=k).then_inc(*c.up(s["act_back"]))
                for t in range(2):
                    take(T0)
                    for half in range(2):
                        i0 = half * GL_CHUNK
                        ins = act.activation(gl_qT[:, half, :, t * P + i0:t * P + i0 + GL_CHUNK],
                                             bank[T0][:, :].rearrange("p (h n) -> p h n", h=GL_HEADS)[:, :, i0:i0 + GL_CHUNK], ACT.Copy)
                        if half == 0:
                            ins.then_inc(*c.up(s["act_step"]))
                    release(ins, T0)
                turned([0, 1])

            def joint(l):
                norm([0, 1])
                norm([2, 3])
                if l == 0:
                    for i in range(3):
                        for t in (0, 2):
                            copy_out((4 * i + t) % 4, jq[:, t, i * NB:(i + 1) * NB])
                else:
                    for i in range(2):
                        copy_out((2 * i) % 4, jq[:, 0, i * NB:(i + 1) * NB])
                    for t in (0, 2):
                        copy_out(t, jq[:, t, 2 * NB:3 * NB])
                flag(s["proj_act"])
                for t in range(4):
                    heads_out(lambda h: j_kT[0:HD, h:h + 4, t * P:(t + 1) * P], KV_HEADS, t)
                for t in range(4 if l == 0 else 2):
                    if t < 2:
                        heads_out(lambda h: j_qT[0:HD, 0, h:h + 4, :], Q_HEADS)
                    heads_out(lambda h: j_qT[0:HD, 1, h:h + 4, :], Q_HEADS)
                    attention(joint_jobs(l, t))
                turned(range(4 if l == 0 else 2))

            def route(l, tiles):
                for t in range(tiles):
                    act.wait_ge(*c.next(s["h_ready"]))
                    act.dma_start(DR["tok"][t * P:(t + 1) * P, :], hb[:, t % 2, :]).then_inc(s[f"tok_stored{t % 2}"], 16)
                    turned([t])
                for _ in range(2):
                    act.wait_ge(*c.next(s["act_go"]))
                    n = 4 * tiles if _ == 0 else tiles
                    v = st[:, (32, 48)[_]:(32, 48)[_] + n]
                    act.activation(v, v, ACT.Exp).then_inc(*c.up(s["act_back"]))

            def experts(l):
                m = moe[l]
                act.wait_ge(*c.next(s["rounds_ready"]))
                rounds = act.value_load(rounds_i[0:1, 0:1], min_val=1, max_val=4)

                def rows_T(j, count):
                    act.wait_ge(m[f"pe_xT{j}"], count)
                    act.activation(mxT[:, j, 0:4, :], bank[T0][:, :].rearrange("p (k n) -> p k n", k=4), ACT.Copy).then_inc(m[f"xT_lo{j}"], 1)

                rows_T(0, 1)
                act.sem_inc(m["y_lo1"], 1)
                with act.Fori(0, rounds * (N_EXP // 2)) as i:
                    for j in range(2):
                        act.wait_ge(m[f"pe_gate{j}"], i + 1)
                        act.wait_ge(m[f"acted{j}"], i + 1)
                        act.activation(msil[:, j, :], bank[2 * j][:, :], ACT.Silu).then_inc(m[f"silu{j}"], 1)
                        rows_T(1 - j, i + 1 + j)
                        act.wait_ge(m[f"pe_y_lo{j}"], i + 1)
                        act.wait_ge(m[f"my_free{j}"], i + 1)
                        act.activation(my[:, j, 0:NB], bank[S0][:, :], ACT.Copy).then_inc(m[f"y_lo{j}"], 1)
                act.activation(st[:, 60:61], cst[:, 0:1], ACT.Copy).then_inc(s["loop_done_a"], 1)

            if on("mix0"):
                even_mixer()
            if on("xa0"):
                cross()
            if on("ffn0"):
                feed_forward()
            if on("mix1"):
                linear_attention()
            if on("xa1"):
                cross()
            if on("ffn1"):
                feed_forward()
            for l in range(2):
                if on(f"att{l}"):
                    joint(l)
                if on(f"route{l}"):
                    route(l, 4 - 2 * l)
                if on(f"moe{l}"):
                    experts(l)

        @block.vector
        def _(dve):
            c = Tally()

            def step(ins):
                ins.then_inc(*c.up(s["dve_step"]))
                dve.wait_ge(*c.last())

            def settle():
                dve.wait_ge(*c.last())

            def take(b):
                dve.wait_ge(*c.next(full["d"][b]))

            def release(ins, b):
                ins.then_inc(*c.up(free["d"][b]))

            def flag(sem_):
                step(dve.tensor_copy(st[:, 61:62], cst[:, 0:1]))
                dve.tensor_copy(st[:, 62:63], cst[:, 0:1]).then_inc(*c.up(sem_))
                settle()

            def copy_out(b, dst, src=None):
                take(b)
                release(dve.tensor_copy(dst, bank[b][:, :] if src is None else src), b)

            def hi_chunks(dst):
                copy_out(T1, dst, bank[T1][:, :].rearrange("p (k n) -> p k n", k=4))

            def filled(slot, n=1):
                dve.wait_ge(*c.next(s[f"bc{slot}"], 16 * n))

            def inv_rms(tiles):
                for i, t in enumerate(tiles):
                    step(dve.tensor_tensor_reduce(hb[:, i, :], xs[:, t, :], xs[:, t, :], 1.0, 0.0, ALU.mult, ALU.add, st[:, i:i + 1]))
                    dve.tensor_scalar(st[:, 4 + i:5 + i], st[:, i:i + 1], 1.0 / D, EPS, ALU.mult, ALU.add).then_inc(*c.up(s["ms_ready"]))

            def norm(tiles, gain, shift=None, stored=None):
                settle()
                for i, t in enumerate(tiles):
                    if stored:
                        dve.wait_ge(s[f"tok_stored{i}"], stored)
                inv_rms(tiles)
                filled(gain)
                if shift is not None:
                    filled(shift)
                for i, t in enumerate(tiles):
                    dve.wait_ge(*c.next(s["rstd_ready"]))
                    ins = dve.scalar_tensor_tensor(hb[:, i, :], xs[:, t, :], st[:, 8 + i:9 + i], bc[:, gain, :], ALU.mult, ALU.mult)
                    if shift is not None:
                        step(ins)
                        ins = dve.tensor_tensor(hb[:, i, :], hb[:, i, :], bc[:, shift, :], ALU.add)
                    ins.then_inc(*c.up(s["h_ready"]))
                for t in tiles:
                    hi_chunks(hT[:, 4:8, t * P:(t + 1) * P])

            def turned(tiles):
                for t in tiles:
                    hi_chunks(hT[:, 4:8, t * P:(t + 1) * P])

            def group_norm(src, groups, width, gains):
                n = groups * width
                sq = hb[:].rearrange("p a b -> p (a b)")[:, 0:n]
                g3 = lambda v: v.rearrange("p (g w) -> p g w", w=width)
                step(dve.tensor_tensor(sq, src, src, ALU.mult))
                step(dve.tensor_reduce(st[:, 104:104 + groups], g3(sq), AX, ALU.add))
                dve.tensor_scalar(st[:, 104:104 + groups], st[:, 104:104 + groups], 1.0 / width, EPS, ALU.mult, ALU.add).then_inc(*c.up(s["stat_ready"]))
                dve.wait_ge(*c.next(s["stat_rstd"]))
                r = st[:, 124:124 + groups].unsqueeze(2).to_broadcast([P, groups, width])
                step(dve.tensor_tensor(g3(src), g3(src), r, ALU.mult))
                for g0, g, row in gains:
                    v = g3(src[:, g0 * width:(g0 + g) * width])
                    step(dve.tensor_tensor(v, v, row.unsqueeze(1).to_broadcast([P, g, width]), ALU.mult))

            def residual(units, gates=None, count=4):
                for u, (n, t) in enumerate(units):
                    b = u % count
                    x = xs[:, t, n * NB:(n + 1) * NB]
                    take(b)
                    if gates is None:
                        release(dve.tensor_tensor(x, x, bank[b][:, :], ALU.add), b)
                    else:
                        tmp = hb[:, u % 2, 0:NB]
                        release(dve.tensor_tensor(tmp, bank[b][:, :], bc[:, gates[t // 2], n * NB:(n + 1) * NB], ALU.mult), b)
                        settle()
                        step(dve.tensor_tensor(x, x, tmp, ALU.add))

            def attention(jobs):
                n = len(jobs)
                for j in range(n + 2):
                    if j < n:
                        job = jobs[j]
                        nk, sc, q = job["nk"], S0 + j % 2, j % 4
                        top, nm = st[:, 12 + q:13 + q], st[:, 16 + q:17 + q]
                        take(sc)
                        if job["mask"] is not None:
                            release(dve.tensor_tensor_reduce(at_s[:, j % 2, 0:nk], bank[sc][:, 0:nk], job["mask"], 1.0, -3.0e38,
                                                             ALU.add, ALU.max, top), sc)
                            settle()
                        else:
                            step(dve.tensor_reduce(top, bank[sc][:, 0:nk], AX, ALU.max))
                        if job["sink"] is not None:
                            h = job["sink"]
                            step(dve.tensor_tensor(top, top, sink8[:, h:h + 1], ALU.max))
                        dve.tensor_scalar(nm, top, -job["scale"], None, ALU.mult).then_inc(*c.up(s["nmax_ready"]))
                    if 1 <= j <= n:
                        i = j - 1
                        q = i % 4
                        total, inv = st[:, 20 + q:21 + q], st[:, 28 + q:29 + q]
                        dve.wait_ge(*c.next(s["e_ready"]))
                        if jobs[i]["sink"] is not None:
                            dve.wait_ge(*c.next(s["es_ready"]))
                            step(dve.tensor_tensor(total, total, st[:, 24 + q:25 + q], ALU.add))
                        step(dve.reciprocal(inv, total))
                        if i % 2 == 1:
                            k = jobs[i]["nk"] // P
                            copy_out(T1, at_eT[:, 1, 0:k, :], bank[T1][:, 0:k * P].rearrange("p (k n) -> p k n", k=k))
                    if j >= 2:
                        i = j - 2
                        take(i % 2)
                        out_ = jobs[i]["out"]
                        release(dve.tensor_scalar(out_, bank[i % 2][:, 0:out_.shape[-1]], st[:, 28 + i % 4:29 + i % 4], None, ALU.mult), i % 2)
                settle()

            def heads_out(dst, heads, n_b=0):
                for g in range(heads // 4):
                    if (g + n_b) % 2 == 1:
                        copy_out(T1, dst(4 * g), bank[T1][0:HD, :].rearrange("p (k n) -> p k n", k=4))

            def rope_angles():
                dve.wait_ge(s["in_loaded"], 64)
                pos, ang, k = st[:, 96:98], st[:, 32:48], st[:, 48:64]
                step(dve.tensor_copy(pos, posi[:]))
                for t in range(2):
                    step(dve.tensor_scalar(ang[:, 8 * t:8 * t + 8], cst[:, C_FREQ:C_FREQ + 8], pos[:, t:t + 1], None, ALU.mult))
                big = float(3 << 22)
                step(dve.tensor_scalar(k, ang, 1.0 / (2.0 * np.pi), big, ALU.mult, ALU.add))
                step(dve.tensor_scalar(k, k, big, None, ALU.subtract))
                c1 = 6.28125
                c2 = float(np.float32(round((2 * np.pi - c1) * 2 ** 22) / 2 ** 22))
                c3 = 2 * np.pi - c1 - c2
                for part in (c1, c2, c3):
                    step(dve.scalar_tensor_tensor(ang, k, -part, ang, ALU.mult, ALU.add))
                v = st[:, 64:96].rearrange("p (t c j) -> p t c j", t=2, c=2)
                a3, k3 = ang.rearrange("p (t j) -> p t j", t=2), k.rearrange("p (t j) -> p t j", t=2)
                step(dve.tensor_scalar(k, ang, np.pi / 2, -2 * np.pi, ALU.is_gt, ALU.mult))
                step(dve.scalar_tensor_tensor(v[:, :, 0, :], a3, np.pi / 2, k3, ALU.add, ALU.add))
                step(dve.tensor_copy(v[:, :, 1, :], a3))
                dve.tensor_scalar(st[:, 64:96], st[:, 64:96], 3.1415925, -3.1415925, ALU.min, ALU.max).then_inc(*c.up(s["act_go"]))

            def modulation():
                dve.wait_ge(s["rows_loaded"], 128)
                for l in range(2):
                    for n in range(12):
                        b = (12 * l + n) % 4
                        v = modrow[0:2, l, n * NB:(n + 1) * NB]
                        take(b)
                        release(dve.tensor_tensor(v, v, bank[b][0:2, :], ALU.add), b)
                    settle()
                    for q, k in enumerate((1, 4)):
                        gain = hb[0:2, q, :] if l == 0 else bc[0:2, 1 + q, :]
                        v = modrow[0:2, l, k * D:(k + 1) * D]
                        ins = dve.scalar_tensor_tensor(v, v, 1.0, gain, ALU.add, ALU.mult)
                        if q == 0:
                            step(ins)
                    ins.then_inc(*c.up(s["mod_rows"]))

            def even_mixer():
                norm([0, 1], 0)
                dve.wait_ge(s["mod_stored"], 32)
                filled(1, 2)
                filled(2, 2)
                dve.wait_ge(*c.next(s["act_back"]))
                col = lambda i: ev_p[:, 1, i * NB:(i + 1) * NB]

                def prepare(t):
                    qk = ev_p[:, t, 0:2 * NB]
                    group_norm(qk, 16, HD, [(0, 8, bc[:, 2, 0:HD]), (8, 8, bc[:, 2, HD:2 * HD])])
                    v = qk.rearrange("p (h d) -> p h d", d=HD)
                    x1, x2 = v[:, :, 0:8], v[:, :, 8:16]
                    cos, sin = (ropec[:, t, i, :].unsqueeze(1).to_broadcast([P, 16, 8]) for i in range(2))
                    w = hb[:, 0, 0:4 * 128].rearrange("p (q h j) -> p q h j", q=4, h=16)
                    for q, (a, b) in enumerate(((x1, cos), (x2, sin), (x2, cos), (x1, sin))):
                        dve.tensor_tensor(w[:, q], a, b, ALU.mult).then_inc(*c.up(s["dve_step"]))
                    settle()
                    step(dve.tensor_tensor(x1, w[:, 0], w[:, 1], ALU.subtract))
                    dve.tensor_tensor(x2, w[:, 2], w[:, 3], ALU.add).then_inc(*c.up(s["prep_ready"]))
                    settle()

                for i in range(2):
                    copy_out((2 * i + 1) % 4, col(i))
                settle()
                prepare(1)
                copy_out(1, col(2))
                dve.wait_ge(*c.next(s["proj_act"]))
                prepare(0)
                dve.wait_ge(s["small_loaded"], 32)
                tril = cst[:, C_TRIL:C_TRIL + P].unsqueeze(1).to_broadcast([P, 8, P])
                dve.tensor_tensor(ev_ws, ev_ws, tril, ALU.mult).then_inc(*c.up(s["prep_ready"]))
                dve.wait_ge(*c.next(s["proj_act"]))
                for t in range(2):
                    settle()
                    v = ev_p[:, t, 4 * NB:5 * NB].rearrange("p (g d) -> p g d", g=8)
                    sq = hb[:, 0, 0:NB].rearrange("p (g d) -> p g d", g=8)
                    wide = lambda x: x.unsqueeze(2).to_broadcast([P, 8, HD])
                    mean, ms, rs = st[:, 96:104], st[:, 104:112], st[:, 124:132]
                    step(dve.tensor_reduce(mean, v, AX, ALU.add))
                    step(dve.tensor_scalar(mean, mean, 1.0 / HD, None, ALU.mult))
                    step(dve.tensor_tensor(v, v, wide(mean), ALU.subtract))
                    step(dve.tensor_tensor(sq, v, v, ALU.mult))
                    step(dve.tensor_reduce(ms, sq, AX, ALU.add))
                    dve.tensor_scalar(ms, ms, 1.0 / HD, EPS, ALU.mult, ALU.add).then_inc(*c.up(s["stat_ready"]))
                    dve.wait_ge(*c.next(s["stat_rstd"]))
                    step(dve.tensor_tensor(v, v, wide(rs), ALU.mult))
                    vf = ev_p[:, t, 4 * NB:5 * NB]
                    step(dve.tensor_tensor(vf, vf, bc[:, 1, 0:NB], ALU.mult))
                    dve.tensor_tensor(vf, vf, bc[:, 1, NB:2 * NB], ALU.add).then_inc(*c.up(s["prep_ready"]))
                settle()
                for t in (1, 0):
                    heads_out(lambda h: ev_T[0:HD, h:h + 4, t * P:(t + 1) * P], 16)
                hi_chunks(ev_wsT[:, 4:8, :])
                for t in range(2):
                    take(2 + t)
                    for g in range(EV_HEADS):
                        ins = dve.scalar_tensor_tensor(ev_o[:, t, NB + g * HD:NB + (g + 1) * HD], bank[2 + t][:, g * HD:(g + 1) * HD],
                                                       st[:, 144 + g:145 + g], ev_p[:, t, 3 * NB + g * HD:3 * NB + (g + 1) * HD],
                                                       ALU.add, ALU.mult)
                        if g < EV_HEADS - 1:
                            ins.then_inc(*c.up(s["dve_step"]))
                    release(ins, 2 + t)
                attention(ev_jobs)
                turned([0, 1])
                residual([(n, t) for n in range(2) for t in range(2)])

            def cross():
                norm([2, 3], 0)
                norm([0, 1], 1)
                filled(2, 2)
                for i in range(4):
                    copy_out((2 * i + 1) % 4, (xa_k, xa_v)[i // 2][:, 1, (i % 2) * NB:(i % 2 + 1) * NB])
                settle()
                dve.wait_ge(*c.next(s["proj_act"]))
                for t in range(2):
                    group_norm(xa_k[:, t, :], X_HEADS, X_HD, [(0, X_HEADS, bc[:, 2, X_HD:2 * X_HD])])
                    flag(s["prep_ready"])
                for i in range(2):
                    copy_out((2 * i + 1) % 4, xa_q[:, 1, i * NB:(i + 1) * NB])
                settle()
                dve.wait_ge(*c.next(s["proj_act"]))
                for t in range(2):
                    group_norm(xa_q[:, t, :], X_HEADS, X_HD, [(0, X_HEADS, bc[:, 2, 0:X_HD])])
                    flag(s["prep_ready"])
                for dst in (xa_kT, xa_qT):
                    for t in range(2):
                        hi_chunks(dst[:, 4:8, t * P:(t + 1) * P])
                attention(xa_jobs)
                turned([0, 1])
                residual([(n, t) for n in range(2) for t in range(2)])

            def feed_forward():
                norm([0, 1], 0)
                n = 2 * FF_SLOTS
                for u in range(n + 2):
                    if u < n:
                        dve.wait_ge(*c.next(s["sil_ready"]))
                        dve.tensor_tensor(ff_act[:, u % 2, :], ff_sil[:, u % 2, :], bank[u % 4][:, FF_W:2 * FF_W], ALU.mult).then_inc(*c.up(s["mul_ready"]))
                    if u >= 2 and (u - 2) % 2 == 1:
                        i = (u - 2) // 2
                        copy_out(T1, ff_T[:, 2 * i:2 * i + 2, P:2 * P], bank[T1][:, 0:2 * P].rearrange("p (k n) -> p k n", k=2))
                settle()
                residual([(n, t) for n in range(2) for t in range(2)])

            def linear_attention():
                norm([0, 1], 0)
                filled(1)
                filled(2)
                dve.memset(gl_qT.rearrange("p a b c -> p (a b c)"), 0.0).then_inc(*c.up(s["dve_step"]))
                for t in range(2):
                    copy_out(S0 + t, z1[:, t, :], bank[S0 + t][:, 0:16])
                for i in range(2):
                    copy_out((2 * i + 1) % 4, gl_p[:, 1, i * NB:(i + 1) * NB])
                for t in range(2):
                    copy_out(S0 + t, z1T[:, t, :], bank[S0 + t][0:16, 0:P])
                for i in range(2, 4):
                    copy_out((2 * i + 1) % 4, gl_p[:, 1, i * NB:(i + 1) * NB])
                z = lambda t: hb[:, t, 0:NB]
                w = lambda t: hb[:, t, NB:2 * NB]
                for t in range(2):
                    take(S0 + t)
                    release(dve.tensor_tensor(z(t), bank[S0 + t][:, :], bc[:, 2, 0:NB], ALU.add), S0 + t)
                    settle()
                    dve.scalar_tensor_tensor(w(t), z(t), -1.0, z(t), ALU.mult, ALU.max).then_inc(*c.up(s["act_go"]))
                dve.wait_ge(*c.next(s["proj_act"]))
                for t in range(2):
                    dve.wait_ge(*c.next(s["act_back"]))
                    dve.scalar_tensor_tensor(z(t), z(t), 0.0, w(t), ALU.min, ALU.subtract).then_inc(*c.up(s["gla_dve"]))
                for t in range(2):
                    copy_out(S1, w(t))
                    settle()
                    dve.wait_ge(*c.next(s["act_back"]))
                    dve.tensor_tensor(w(t), w(t), gl_b[:, t, :], ALU.subtract).then_inc(*c.up(s["act_go"]))
                    dve.wait_ge(*c.next(s["act_back"]))
                    q, k = gl_p[:, t, 0:NB], gl_p[:, t, NB:2 * NB]
                    for half in range(2):
                        dve.scalar_tensor_tensor(gl_ks[:, t, half, :], k, cst[:, C_HALF + half:C_HALF + half + 1], w(t), ALU.mult, ALU.mult)\
                           .then_inc(*c.up(s["dve_step"]))
                    step(dve.tensor_tensor(k, k, gl_b[:, t, :], ALU.mult))
                    dve.scalar_tensor_tensor(q, q, GL_DK ** -0.5, z(t), ALU.mult, ALU.mult).then_inc(*c.up(s["prep_ready"]))
                for t in range(2):
                    hi_chunks(gl_kT[:, :, t * P:(t + 1) * P])
                for n in range(9):
                    if n < 8:
                        h = n % GL_HEADS
                        if n < GL_HEADS:
                            take(T0)
                            step(dve.tensor_copy(gl_S[:, h, 0, :], bank[T0][:, 0:GL_DV]))
                            release(dve.scalar_tensor_tensor(gl_S[:, h, 1, :], gl_S[:, h, 0, :], dec[:, 0, h, 1:2], bank[T0][:, GL_DV:2 * GL_DV],
                                                             ALU.mult, ALU.add), T0)
                            settle()
                            take(T1)
                            release(dve.scalar_tensor_tensor(gl_S[:, h, 2, :], gl_S[:, h, 1, :], dec[:, 1, h, 0:1], bank[T1][:, 0:GL_DV],
                                                             ALU.mult, ALU.add), T1)
                        take(S0 + n % 2)
                        dve.tensor_tensor(gl_att[:, n % 4, :], bank[S0 + n % 2][:, 0:P], cst[:, C_CHUNK:C_CHUNK + P], ALU.mult).then_inc(*c.up(s["gla_dve"]))
                    if n >= 1:
                        t, h = (n - 1) // GL_HEADS, (n - 1) % GL_HEADS
                        copy_out((n - 1) % 4, gl_o[:, t, h * GL_DV:(h + 1) * GL_DV], bank[(n - 1) % 4][:, 0:GL_DV])
                settle()
                for t in range(2):
                    o = gl_o[:, t, :]
                    group_norm(o, GL_HEADS, GL_DV, [])
                    step(dve.tensor_tensor(o, o, bc[:, 1, :], ALU.mult))
                    dve.tensor_tensor(o, o, gl_p[:, t, 2 * D:3 * D], ALU.mult).then_inc(*c.up(s["prep_ready"]))
                    settle()
                turned([0, 1])
                residual([(n, t) for n in range(2) for t in range(2)])

            def rotate(x, cos, sin, dst, tmp, heads):
                wide = lambda v: v.unsqueeze(1).to_broadcast([P, heads, HD])
                h3 = lambda v: v.rearrange("p (h d) -> p h d", d=HD)
                h4 = lambda v: v.rearrange("p (h a b i) -> p h a b i", h=heads, a=2, b=2)
                dve.tensor_tensor(h3(dst), h3(x), wide(cos), ALU.mult).then_inc(*c.up(s["dve_step"]))
                s4 = sin.rearrange("p (a b i) -> p a b i", a=2, b=2)
                for b in range(2):
                    sw = s4[:, :, b, :].unsqueeze(1).to_broadcast([P, heads, 2, 16])
                    dve.tensor_tensor(h4(tmp)[:, :, :, b, :], h4(x)[:, :, :, 1 - b, :], sw, ALU.mult).then_inc(*c.up(s["dve_step"]))
                settle()

            def joint(l):
                if l == 0:
                    dve.wait_ge(s["ctx_loaded"], 32)
                norm([0, 1], 0, 1)
                norm([2, 3], 0, 1)
                if l == 0:
                    for i in range(3):
                        for t in (1, 3):
                            copy_out(t, jq[:, t, i * NB:(i + 1) * NB])
                else:
                    for i in range(2):
                        copy_out((2 * i + 1) % 4, jq[:, 1, i * NB:(i + 1) * NB])
                    for t in (1, 3):
                        copy_out(t, jq[:, t, 2 * NB:3 * NB])
                settle()
                dve.wait_ge(*c.next(s["proj_act"]))
                hbf = hb[:].rearrange("p a b -> p (a b)")
                if l == 1:
                    filled(0, 2)
                for t in range(4):
                    k = jq[:, t, D:D + KV_HEADS * HD]
                    if l == 1:
                        gk = bc[:, 0, HD:2 * HD]
                        if t < 2:
                            group_norm(jq[:, t, 0:20 * HD], 20, HD, [(0, 16, bc[:, 0, 0:HD]), (16, 4, gk)])
                        else:
                            group_norm(k, 4, HD, [(0, 4, gk)])
                    if t < 2:
                        rotate(k, cst[:, C_COS + HD * t:C_COS + HD * (t + 1)], cst[:, C_SIN + HD * t:C_SIN + HD * (t + 1)],
                               hbf[:, 0:256], hbf[:, 256:512], KV_HEADS)
                        dve.tensor_tensor(k, hbf[:, 0:256], hbf[:, 256:512], ALU.add).then_inc(*c.up(s["prep_ready"]))
                        settle()
                    else:
                        flag(s["prep_ready"])
                for t in range(4):
                    heads_out(lambda h: j_kT[0:HD, h:h + 4, t * P:(t + 1) * P], KV_HEADS, t)
                for t in range(4 if l == 0 else 2):
                    settle()
                    if t < 2:
                        rotate(jq[:, t, 0:D], cst[:, C_COS + HD * t:C_COS + HD * (t + 1)], cst[:, C_SIN + HD * t:C_SIN + HD * (t + 1)],
                               hb[:, 0, :], hb[:, 1, :], Q_HEADS)
                        dve.tensor_tensor(hb[:, 0, :], hb[:, 0, :], hb[:, 1, :], ALU.add).then_inc(*c.up(s["prep_ready"]))
                        heads_out(lambda h: j_qT[0:HD, 0, h:h + 4, :], Q_HEADS)
                    else:
                        flag(s["prep_ready"])
                    heads_out(lambda h: j_qT[0:HD, 1, h:h + 4, :], Q_HEADS)
                    if l == 0 and t == 0:
                        step(dve.tensor_scalar(sink8, sink1, float(HD ** 0.5), None, ALU.mult))
                    attention(joint_jobs(l, t))
                tiles = range(4 if l == 0 else 2)
                turned(tiles)
                filled(2)
                if l == 0:
                    filled(0)
                residual([(n, t) for n in range(2) for t in tiles], gates=(2, 0))

            def route(l, tiles):
                norm([0, 1], 0, 1)
                if tiles == 4:
                    norm([2, 3], 0, 1, stored=16)
                T = tiles
                dve.wait_ge(*c.next(s["small_l"], 64))
                for t in range(T):
                    take(t)
                    release(dve.tensor_tensor(mlog[:, t, :], bank[t][:, 0:36], rb, ALU.add), t)
                settle()
                lg, lr = mlog[:, 0:T, 0:4], mlog[:, 0:T, 4:36]
                wide = lambda v, n: v.unsqueeze(2).to_broadcast([P, T, n])
                gmax, e4 = st[:, 0:T], st[:, 32:32 + 4 * T].rearrange("p (t g) -> p t g", g=4)
                step(dve.tensor_reduce(gmax, lg, AX, ALU.max))
                dve.tensor_tensor(e4, lg, wide(gmax, 4), ALU.subtract).then_inc(*c.up(s["act_go"]))
                w4 = mtmp[:, 0, 0:4 * T].rearrange("p (t g) -> p t g", g=4)
                grp = st[:, 4:4 + T]
                step(dve.tensor_tensor(w4, lg, wide(gmax, 4), ALU.is_equal))
                iota4 = cst[:, C_IOTA:C_IOTA + 4].unsqueeze(1).to_broadcast([P, T, 4])
                step(dve.scalar_tensor_tensor(w4, w4, -100.0, iota4, ALU.mult, ALU.add))
                step(dve.tensor_reduce(grp, w4, AX, ALU.min))
                m32 = mtmp[:, 1, 0:N_EXP * T].rearrange("p (t e) -> p t e", e=N_EXP)
                n32 = mtmp[:, 2, 0:N_EXP * T].rearrange("p (t e) -> p t e", e=N_EXP)
                group = cst[:, C_GROUP:C_GROUP + N_EXP].unsqueeze(1).to_broadcast([P, T, N_EXP])
                step(dve.tensor_tensor(m32, group, wide(grp, N_EXP), ALU.is_equal))
                step(dve.tensor_tensor(lr, lr, m32, ALU.mult))
                step(dve.tensor_scalar(n32, m32, 1.0, -MASKED, ALU.subtract, ALU.mult))
                step(dve.tensor_tensor(n32, n32, lr, ALU.add))
                best = mtmp[:, 3, 0:8 * T].rearrange("p (t e) -> p t e", e=8)
                where = mtmp[:, 3, 32:32 + 8 * T].bitcast(U32).rearrange("p (t e) -> p t e", e=8)
                for t in range(T):
                    step(dve.max(best[:, t, :], n32[:, t, :]))
                    step(dve.max_index(where[:, t, :], best[:, t, :], n32[:, t, :]))
                eid = mtmp[:, 3, 64:64 + 2 * T].rearrange("p (t j) -> p t j", j=2)
                step(dve.tensor_copy(eid, where[:, :, 0:2]))
                dve.tensor_tensor(st[:, 48:48 + T], best[:, :, 1], best[:, :, 0], ALU.subtract).then_inc(*c.up(s["act_go"]))
                hot = monehot[:, 0:T, :, :]
                iota = cst[:, C_IOTA:C_IOTA + N_EXP].unsqueeze(1).to_broadcast([P, T, N_EXP])
                for j in range(2):
                    step(dve.tensor_tensor(hot[:, :, j, :], iota, wide(eid[:, :, j], N_EXP), ALU.is_equal))
                dve.tensor_tensor(mtmp[:, 0:T, 0:N_EXP], hot[:, :, 0, :], hot[:, :, 1, :], ALU.add).then_inc(*c.up(s["marks_ready"]))
                dve.wait_ge(*c.next(s["act_back"], 2))
                total, e21, p, q = st[:, 0:T], st[:, 48:48 + T], st[:, 4:4 + T], st[:, 8:8 + T]
                settle()
                step(dve.tensor_reduce(total, e4, AX, ALU.add))
                step(dve.tensor_scalar(q, e21, 1.0, None, ALU.add))
                step(dve.tensor_tensor(total, total, q, ALU.mult))
                step(dve.reciprocal(p, total))
                w2 = mwt[:, 0:2 * T].rearrange("p (t j) -> p t j", j=2)
                step(dve.tensor_copy(w2[:, :, 0], p))
                step(dve.tensor_tensor(w2[:, :, 1], p, e21, ALU.mult))
                take(S0)
                rank = bank[S0][:, 0:N_EXP * T].rearrange("p (t e) -> p t e", e=N_EXP)
                r = st[:, 32:32 + 2 * T].rearrange("p (t j) -> p t j", j=2)
                prod = mtmp[:, 1, 0:N_EXP * T].rearrange("p (t e) -> p t e", e=N_EXP)
                for j in range(2):
                    step(dve.tensor_tensor(prod, hot[:, :, j, :], rank, ALU.mult))
                    step(dve.tensor_reduce(r[:, :, j], prod, AX, ALU.add))
                step(dve.scalar_tensor_tensor(r, eid, float(CAP), r, ALU.mult, ALU.add))
                dve.tensor_copy(mdest[:, 0:2 * T], st[:, 32:32 + 2 * T]).then_inc(*c.up(s["dest_ready"]))
                most, n = st[:, 0:1], st[:, 1:2]
                release(dve.tensor_reduce(most, bank[S0][:, 4 * N_EXP:5 * N_EXP], AX, ALU.max), S0)
                settle()
                step(dve.tensor_scalar(n, most, float(P), 1.0, ALU.is_gt, ALU.add))
                for k in (2, 3):
                    step(dve.scalar_tensor_tensor(n, most, float(k * P), n, ALU.is_gt, ALU.add))
                dve.tensor_copy(rounds_i[:], n).then_inc(*c.up(s["rounds_ready"]))
                take(S1)
                release(dve.tensor_copy(idx[:, 0, 0:P], bank[S1][:, 0:P]), S1)
                settle()
                dve.tensor_scalar(idx[:, 1, 0:P], idx[:, 0, 0:P], 1, None, ALU.logical_shift_right).then_inc(*c.up(s["idx_ready"]))
                settle()

            def experts(l):
                m = moe[l]
                rounds = dve.value_load(rounds_i[0:1, 0:1], min_val=1, max_val=4)

                def rows_T(j, count):
                    dve.wait_ge(m[f"pe_xT{j}"], count)
                    dve.tensor_copy(mxT[:, j, 4:8, :], bank[T1][:, :].rearrange("p (k n) -> p k n", k=4)).then_inc(m[f"xT_hi{j}"], 1)

                rows_T(0, 1)
                dve.sem_inc(m["acted0"], 1)
                dve.sem_inc(m["acted1"], 1)
                dve.sem_inc(m["y_hi1"], 1)
                with dve.Fori(0, rounds * (N_EXP // 2)) as i:
                    for j in range(2):
                        dve.wait_ge(m[f"pe_up{j}"], i + 1)
                        dve.wait_ge(m[f"silu{j}"], i + 1)
                        dve.tensor_tensor(mact[:, j, :], msil[:, j, :], bank[2 * j + 1][:, :], ALU.mult).then_inc(m[f"acted{j}"], 1)
                        rows_T(1 - j, i + 1 + j)
                        dve.wait_ge(m[f"pe_aT{j}"], i + 1)
                        dve.tensor_copy(mactT[:, j, :, :], bank[2 * j][:, :].rearrange("p (k n) -> p k n", k=4)).then_inc(m[f"aT{j}"], 1)
                        dve.wait_ge(m[f"pe_y_hi{j}"], i + 1)
                        dve.wait_ge(m[f"my_free{j}"], i + 1)
                        dve.tensor_copy(my[:, j, NB:2 * NB], bank[S1][:, :]).then_inc(m[f"y_hi{j}"], 1)
                dve.tensor_copy(st[:, 63:64], cst[:, 0:1]).then_inc(*c.up(s["loop_done_d"]))
                settle()
                tiles = 4 - 2 * l
                y = view(0, 4, 2, D)
                filled(2)
                if l == 0:
                    filled(0)
                dve.wait_ge(*c.next(s["y_loaded"], 16 * tiles))
                for t in range(tiles):
                    a, b = y[:, t, 0, :], y[:, t, 1, :]
                    step(dve.tensor_scalar(a, a, mwt[:, 2 * t:2 * t + 1], None, ALU.mult))
                    step(dve.scalar_tensor_tensor(a, b, mwt[:, 2 * t + 1:2 * t + 2], a, ALU.mult, ALU.add))
                    step(dve.tensor_tensor(a, a, bc[:, 2 if t < 2 else 0, :], ALU.mult))
                    step(dve.tensor_tensor(xs[:, t, :], xs[:, t, :], a, ALU.add))

            rope_angles()
            modulation()
            dve.wait_ge(s["x_loaded"], 32)
            if on("mix0"):
                even_mixer()
            if on("xa0"):
                cross()
            if on("ffn0"):
                feed_forward()
            if on("mix1"):
                linear_attention()
            if on("xa1"):
                cross()
            if on("ffn1"):
                feed_forward()
            for l in range(2):
                if on(f"att{l}"):
                    joint(l)
                if on(f"route{l}"):
                    route(l, 4 - 2 * l)
                if on(f"moe{l}"):
                    experts(l)
            settle()
            if on("all"):
                inv_rms([0, 1])
                filled(0)
                for i in range(2):
                    dve.wait_ge(*c.next(s["rstd_ready"]))
                    step(dve.scalar_tensor_tensor(hb[:, i, :], xs[:, i, :], st[:, 8 + i:9 + i], bc[:, 0, :], ALU.mult, ALU.mult))
            flag(s["fin_ready"])

        def experts(pool, c, step, l):
            m = moe[l]
            tiles = 4 - 2 * l
            pool.wait_ge(*c.next(s["idx_ready"]))
            pool.wait_ge(*c.next(s["rounds_ready"]))
            for q in range(2):
                pool.wait_ge(*c.next(s[f"tok_stored{q}"], 16 * tiles // 2))
            rounds = pool.value_load(rounds_i[0:1, 0:1], min_val=1, max_val=4)
            step(pool.memset(view(0, 2 * D), 0.0))

            def apart():
                pool.sem_inc(s["pool_passed"], 1)

            def gather(j, col, before, picks):
                if before is not None:
                    pool.wait_ge(m[f"rows{j}"], before * 16)
                    pool.wait_ge(m[f"pe_xT{j}"], before)
                    apart()
                pool.tensor_copy(pick[:, 0, j:j + 1], idx[:, 1, bass.ds(col, 1)]).then_inc(m["picked"], 1)
                pool.wait_ge(m["picked"], picks)
                apart()
                pool.indirect_dma_start(out=mx[:, j, :], out_offset=None, in_=DR["tok"],
                                        in_offset=bass.IndirectOffsetOnAxis(ap=pick[:, 0, j:j + 1], axis=0),
                                        bounds_check=tiles * P - 1, oob_is_err=False).then_inc(m[f"rows{j}"], 16)

            def store(j, col, i):
                pool.tensor_copy(pick[:, 1, j:j + 1], idx[:, 0, bass.ds(col, 1)]).then_inc(m["picked"], 1)
                pool.wait_ge(m["picked"], i * 4 + 3 + 2 * j)
                pool.wait_ge(m[f"y_lo{j}"], i + 1 + j)
                pool.wait_ge(m[f"y_hi{j}"], i + 1 + j)
                apart()
                pool.indirect_dma_start(out=DR["y"][l], out_offset=bass.IndirectOffsetOnAxis(ap=pick[:, 1, j:j + 1], axis=0),
                                        in_=my[:, j, :], in_offset=None,
                                        bounds_check=2 * tiles * P - 1, oob_is_err=False).then_inc(m[f"stored{j}"], 16)

            for j in range(2):
                gather(j, j, None, j + 1)
                pool.sem_inc(m[f"my_free{j}"], 1)
            steps = rounds * (N_EXP // 2)
            with pool.Fori(0, steps) as i:
                for j in range(2):
                    store(j, i * 2 + j, i)
                    gather(j, i * 2 + 2 + j, i + 1, i * 4 + 4 + 2 * j)
                    pool.wait_ge(m[f"stored{j}"], (i + 1) * 16)
                    pool.sem_inc(m[f"my_free{j}"], 1)
            for j in range(2):
                pool.wait_ge(m[f"rows{j}"], (steps + 1) * 16)
            apart()
            y = view(0, 4, 2, D)
            for t in range(tiles):
                pool.dma_start(y[:, t, :, :], DR["y"][l][2 * t * P:2 * (t + 1) * P, :].rearrange("(p j) d -> p j d", j=2)).then_inc(s["y_loaded"], 16)

        @block.gpsimd
        def _(pool):
            c = Tally()

            def step(ins):
                ins.then_inc(*c.up(s["pool_step"]))
                pool.wait_ge(*c.last())

            def fill(slot, *rows):
                at = 0
                for row in rows:
                    n = row.shape[-1]
                    pool.dma_start(bc[:, slot, at:at + n], row.partition_broadcast(P)).then_inc(s[f"bc{slot}"], 16)
                    at += n

            def norms(n=2):
                for i in range(n):
                    pool.wait_ge(*c.next(s["ms_ready"]))
                    pool.tensor_tensor(st[:, 8 + i:9 + i], st[:, 4 + i:5 + i], cst[:, C_POW:C_POW + 1], ALU.pow).then_inc(*c.up(s["rstd_ready"]))

            def normed(n=2):
                pool.wait_ge(*c.next(s["h_ready"], n))

            def stats(*groups):
                for g in groups:
                    pool.wait_ge(*c.next(s["stat_ready"]))
                    pool.tensor_tensor(st[:, 124:124 + g], st[:, 104:104 + g], cst[:, C_POW:C_POW + g], ALU.pow).then_inc(*c.up(s["stat_rstd"]))

            def mod(l, which, k):
                return dr_mod[l, which, k * D:(k + 1) * D]

            pool.dma_start(cst[:], I["shape_constants"]).then_inc(s["in_loaded"], 16)
            with nc.allow_non_contiguous_dma(reason="features of the condition rows by partition"):
                for q, v in enumerate((I["c_2"][0], I["c_ctx_2"])):
                    pool.dma_start(cond[:, :, q], v.rearrange("(k p) -> p k", p=P)).then_inc(s["in_loaded"], 16)
                pool.dma_start(posi[:], I["positions"][0].rearrange("(t p) -> p t", p=P)).then_inc(s["in_loaded"], 16)
            for l in range(2):
                for q in range(2):
                    pool.dma_start(modrow[q:q + 1, l, :], I["b_ada_2"][l:l + 1, :]).then_inc(s["rows_loaded"], 16)
            for l in range(2):
                for q, name in enumerate(("g_attn_2", "g_ffn_2")):
                    dst = hb[0:2, q, :] if l == 0 else bc[0:2, 1 + q, :]
                    pool.dma_start(dst, I[name][l].partition_broadcast(2)).then_inc(s["rows_loaded"], 16)
            fill(0, I["norm_mix"][0])
            step(pool.memset(idx[:, 0, P:P + 2], EMPTY))
            step(pool.memset(idx[:, 1, P:P + 2], EMPTY // 2))
            pool.wait_ge(s["in_loaded"], 64)
            for l in range(2):
                pool.wait_ge(*c.next(s["mod_rows"]))
                pool.dma_start(dr_mod[l], modrow[0:2, l, :]).then_inc(s["mod_stored"], 16)
            pool.wait_ge(s["mod_stored"], 32)

            def cross(l):
                fill(2, I["xa_q_gain"][l], I["xa_k_gain"][l])
                norms()
                normed()
                if l == 1:
                    pool.dma_start(xs[:, 2:4, :], I["ctx_2"][0].rearrange("(t p) d -> p t d", p=P)).then_inc(s["ctx_loaded"], 16)
                norms()
                normed()
                fill(0, I["norm_ffn"][l])
                stats(X_HEADS, X_HEADS, X_HEADS, X_HEADS)

            if on("mix0"):
                fill(1, I["ev_ln_g"][0].rearrange("g d -> (g d)"), I["ev_ln_b"][0].rearrange("g d -> (g d)"))
                fill(2, I["ev_q_gain"][0], I["ev_k_gain"][0])
                pool.dma_start(ev_ws, I["ev_w_s"][0].rearrange("g i j -> i g j")).then_inc(s["small_loaded"], 16)
                with nc.allow_non_contiguous_dma(reason="spatial biases by token"):
                    pool.dma_start(st[:, 144:152], I["ev_b_s"][0].rearrange("g i -> i g")).then_inc(s["small_loaded"], 16)
                norms()
                normed()
                fill(0, I["norm_mem_kv"][0])
                stats(16, 16, 8, 8)
            if on("xa0"):
                pool.wait_ge(s["ms_ready"], c.count(s["ms_ready"]) + 1)
                fill(1, I["norm_mem_q"][0])
                cross(0)
            if on("ffn0"):
                norms()
                normed()
            if on("mix1"):
                fill(0, I["norm_mix"][1])
                fill(1, I["od_o_gain"][0].rearrange("h v -> (h v)"))
                fill(2, I["od_b_g"][0])
                pool.wait_ge(s["ms_ready"], c.count(s["ms_ready"]) + 1)
                pool.dma_start(g1, I["od_w_g1"][0].rearrange("(k p) n -> p k n", p=P)).then_inc(s["small_loaded"], 16)
                pool.dma_start(g2, I["od_w_g2"][0]).then_inc(s["small_loaded"], 16)
                norms()
                normed()
                fill(0, I["norm_mem_kv"][1])
                stats(GL_HEADS, GL_HEADS)
            if on("xa1"):
                pool.wait_ge(s["ms_ready"], c.count(s["ms_ready"]) + 1)
                fill(1, I["norm_mem_q"][1])
                cross(1)
            if on("ffn1"):
                norms()
                normed()
            for l in range(2):
                if on(f"att{l}"):
                    if l == 1:
                        pool.wait_ge(s["ms_ready"], c.count(s["ms_ready"]) + 1)
                    fill(0, mod(l, 0, 1))
                    fill(1, mod(l, 0, 0))
                    if l == 0:
                        with nc.allow_non_contiguous_dma(reason="a short row"):
                            pool.dma_start(sink1, I["sink_a_2"][0].partition_broadcast(P)).then_inc(s["ctx_loaded"], 16)
                    fill(2, mod(l, 0, 2))
                    norms()
                    normed()
                    fill(0, mod(l, 1, 1))
                    fill(1, mod(l, 1, 0))
                    norms()
                    normed()
                    if l == 0:
                        fill(0, mod(l, 1, 2))
                    else:
                        fill(0, I["gq_b_2"][0], I["gk_b_2"][0])
                        stats(20, 20, 4, 4)
                if on(f"route{l}"):
                    tiles = 4 - 2 * l
                    pool.wait_ge(s["ms_ready"], c.count(s["ms_ready"]) + 1)
                    fill(0, mod(l, 0, 4))
                    fill(1, mod(l, 0, 3))
                    fill(2, mod(l, 0, 5))
                    with nc.allow_non_contiguous_dma(reason="router's narrow weights"):
                        for n0, n1, w, b in ((0, 4, "w_group_2", "b_group_2"), (4, 36, "w_router_2", "b_router_2")):
                            pool.dma_start(mw[:, :, n0:n1], I[w][l].rearrange("(k p) n -> p k n", p=P)).then_inc(s["small_l"], 16)
                            pool.dma_start(rb[:, n0:n1], I[b][l].partition_broadcast(P)).then_inc(s["small_l"], 16)
                    norms()
                    normed()
                    if tiles == 4:
                        fill(0, mod(l, 1, 4))
                        fill(1, mod(l, 1, 3))
                        norms()
                        normed()
                        fill(0, mod(l, 1, 5))
                    tab = DR["tab"][l]
                    step(pool.memset(mtab, float(EMPTY)))
                    pool.dma_start(tab.rearrange("(p s) o -> p (s o)", p=P), mtab).then_inc(s["tab_done"], 16)
                    pool.wait_ge(*c.next(s["tab_done"], 16))
                    pool.wait_ge(*c.next(s["dest_ready"]))
                    for q in range(2 * tiles):
                        pool.indirect_dma_start(out=tab, out_offset=bass.IndirectOffsetOnAxis(ap=mdest[:, q:q + 1], axis=0),
                                                in_=cst[:, C_ASG + q:C_ASG + q + 1], in_offset=None).then_inc(s["tab_done"], 16)
                    pool.wait_ge(*c.next(s["tab_done"], 32 * tiles))
                    rows = tab.rearrange("(e r s) o -> r e (s o)", e=N_EXP, r=4)
                    for r in range(4):
                        pool.dma_start(mtab[r * N_EXP:(r + 1) * N_EXP, :], rows[r]).then_inc(s["tab_loaded"], 16)
                if on(f"moe{l}"):
                    experts(pool, c, step, l)
            if on("all"):
                pool.wait_ge(s["ms_ready"], c.count(s["ms_ready"]) + 1)
                fill(0, I["g_final_2"])
                norms()


INPUTS = [
    "x", "mem", "positions", "norm_mix", "norm_mem_q", "norm_mem_kv", "norm_ffn", "ev_w_in", "ev_q_gain",
    "ev_k_gain", "ev_w_s", "ev_b_s", "ev_ln_g", "ev_ln_b", "ev_w_out", "od_w_in", "od_w_g1", "od_w_g2", "od_b_g",
    "od_o_gain", "od_w_out", "xa_w_q", "xa_w_kv", "xa_q_gain", "xa_k_gain", "xa_w_out", "ffn_w_gu", "ffn_w_down",
    "c_2", "ctx_2", "c_ctx_2", "w_ada_2", "b_ada_2", "g_attn_2", "w_qkv_2", "w_o_2", "sink_a_2", "gq_b_2", "gk_b_2",
    "g_ffn_2", "w_group_2", "b_group_2", "w_router_2", "b_router_2", "w_gate_2", "w_up_2", "w_down_2",
    "g_final_2",
]


def kernel(**inputs):
    from concourse import bacc
    from concourse.bass_utils import run_bass_kernel_spmd

    nc = bacc.Bacc("TRN2", target_bir_lowering=False, num_devices=1)
    arrays, aps = {}, {}
    for name in INPUTS:
        arrays["in_" + name] = np.ascontiguousarray(inputs[name])
    arrays["in_shape_constants"] = shape_constants()
    for key, a in arrays.items():
        aps[key[3:]] = nc.dram_tensor(key, a.shape, mybir.dt.from_np(a.dtype), kind="ExternalInput").ap()
    shape = tuple(np.shape(inputs["x"]))
    out = nc.dram_tensor("out_0", shape, F32, kind="ExternalOutput").ap()
    build_program(nc, aps, out)
    r = run_bass_kernel_spmd(nc, [arrays], core_ids=[0])
    return r.results[0]["out_0"]
```

```python
from contextlib import ExitStack

import numpy as np

import concourse.bass as bass
from concourse import mybir

F32 = mybir.dt.float32
F32R = mybir.dt.float32r
I32 = mybir.dt.int32
U32 = mybir.dt.uint32
ALU = mybir.AluOpType
ACT = mybir.ActivationFunctionType
AX = mybir.AxisListType.X

P = 128
D = 1024
KD = D // P
NB = 512
EPS = 1e-6
MASKED = -1e30
SLOTS = 6
LAND = 4
SLOT = KD * NB

EV_HEADS, HD = 8, 64
GL_HEADS, GL_DK, GL_DV, GL_CHUNK, GL_TAU = 4, 128, 256, 64, 16.0
X_HEADS, X_HD = 4, 256
D_FF = 2816
FF_K = D_FF // P
FF_W = 256
FF_SLOTS = D_FF // FF_W
Q_HEADS, KV_HEADS = 16, 4
QKV = (Q_HEADS + 2 * KV_HEADS) * HD
N_EXP, N_GRP, EXP_H = 32, 4, 512
ROWS = 64
CAP = 512
EMPTY = 4096
MODW = 6 * D

C_IDENT, C_TRIL, C_CHUNK, C_SAME, C_BEFORE, C_ONES = (P * i for i in range(6))
C_WIN0 = 6 * P
C_WIN1 = C_WIN0 + NB
C_HALF = C_WIN1 + NB
C_IOTA = C_HALF + 2
C_GROUP = C_IOTA + N_EXP
C_ASG = C_GROUP + N_EXP
C_COS = C_ASG + 8
C_SIN = C_COS + 2 * HD
C_FREQ = C_SIN + 2 * HD
C_POW = C_FREQ + 8
C_ALL = C_POW + 20


def shape_constants():
    c = np.zeros((P, C_ALL), np.float32)
    i = np.arange(P)
    row, col = i[:, None], i[None, :]
    chunk = (row // GL_CHUNK) == (col // GL_CHUNK)
    c[:, C_IDENT:C_IDENT + P] = row == col
    c[:, C_TRIL:C_TRIL + P] = col <= row
    c[:, C_CHUNK:C_CHUNK + P] = chunk & (row <= col)
    c[:, C_SAME:C_SAME + P] = chunk
    c[:, C_BEFORE:C_BEFORE + P] = row < col
    c[:, C_ONES:C_ONES + P] = 1.0
    c[:, C_WIN0 + P:C_WIN0 + 2 * P] = np.where(col <= row, 0.0, MASKED)
    c[:, C_WIN1:C_WIN1 + P] = np.where(col >= row, 0.0, MASKED)
    c[:, C_HALF] = i < GL_CHUNK
    c[:, C_HALF + 1] = i >= GL_CHUNK
    c[:, C_IOTA:C_IOTA + N_EXP] = np.arange(N_EXP)
    c[:, C_GROUP:C_GROUP + N_EXP] = np.arange(N_EXP) // (N_EXP // N_GRP) - 100
    for t in range(4):
        for j in range(2):
            c[:, C_ASG + 2 * t + j] = 2 * (P * t + i) + j
    inv = (np.float32(10000.0) ** (-np.arange(16, dtype=np.float32) / np.float32(16))).astype(np.float32)
    for t in range(2):
        tok = P * t + i
        ar = (tok // 64).astype(np.float32)[:, None] * inv
        ac = (tok % 64).astype(np.float32)[:, None] * inv
        c[:, C_COS + HD * t:C_COS + HD * (t + 1)] = np.cos(np.concatenate([ar, ar, ac, ac], -1))
        c[:, C_SIN + HD * t:C_SIN + HD * (t + 1)] = np.concatenate(
            [-np.sin(ar), np.sin(ar), -np.sin(ac), np.sin(ac)], -1)
    c[:, C_FREQ:C_FREQ + 8] = np.float32(500000.0) ** (-np.arange(8, dtype=np.float32) * np.float32(2.0) / np.float32(16))
    c[:, C_POW:C_POW + 20] = -0.5
    return c


class Tally:

    def __init__(self):
        self.made, self.seen, self.latest = {}, {}, None

    def up(self, sem, by=1):
        self.made[id(sem)] = self.made.get(id(sem), 0) + by
        self.latest = (sem, self.made[id(sem)])
        return sem, by

    def last(self):
        return self.latest

    def count(self, sem):
        return self.seen.get(id(sem), 0)

    def next(self, sem, n=1):
        self.seen[id(sem)] = self.seen.get(id(sem), 0) + n
        return sem, self.seen[id(sem)]


def build_program(nc, I, out):
    with ExitStack() as ctx:
        def sb(name, shape, dt=F32):
            return ctx.enter_context(nc.sbuf_tensor("sb_" + name, shape, dt))

        def sem(name):
            return ctx.enter_context(nc.semaphore(name))

        bank = [ctx.enter_context(nc.psum_tensor(f"bank{b}", [P, NB], F32)) for b in range(8)]
        T0, T1, S0, S1 = 4, 5, 6, 7

        shapes = {f"ring{q}": [P, SLOT] for q in range(SLOTS)}
        shapes |= {"hb": [P, 2, D],
                   "hT": [P, KD, 4 * P],
                   "arena": [P, 12288]}
        with ExitStack() as plain:
            *ring, hb, hT, A = (plain.enter_context(nc.sbuf_tensor("sb_" + n, shapes[n], F32)) for n in shapes)
        rounded = {"sb_" + n: ctx.enter_context(nc.sbuf_tensor(f"sb_{n}_rounded", shapes[n], F32R)) for n in shapes}

        def rnd(ap):
            return bass.AP(rounded[ap.tensor.name], ap.offset, ap.ap)

        def whole(ap):
            return rnd(ap).bitcast(F32)

        xs = sb("xs", [P, 4, D])
        bc = sb("bc", [P, 3, D])
        cst = sb("cst", [P, C_ALL])
        st = sb("st", [P, 256])
        ropec = sb("ropec", [P, 2, 2, 8])
        posi = sb("posi", [P, 2], I32)
        idx = sb("idx", [ROWS, 2, N_EXP * (CAP // ROWS)], U32)
        pick = sb("pick", [ROWS, 2, 2], U32)
        steps_i = sb("steps_i", [P, 1], I32)

        ident = cst[:, C_IDENT:C_IDENT + P]
        hTf = hT[:].rearrange("p a b -> p (a b)")

        DR = {"mod": nc.dram_tensor("scratch_mod", [2, 2, MODW], F32, kind="Internal").ap(),
              "tok": nc.dram_tensor("scratch_tokens", [512, D], F32, kind="Internal").ap(),
              "tab": [nc.dram_tensor(f"scratch_table{l}", [N_EXP * CAP, 1], F32, kind="Internal").ap() for l in range(2)],
              "y": [nc.dram_tensor(f"scratch_y{l}", [1024, D], F32, kind="Internal").ap() for l in range(2)]}

        s = {n: sem(n) for n in (
            "act_back", "act_done", "act_go", "act_step", "ctx_loaded", "dest_ready", "dve_step", "e_ready",
            "es_ready", "fin_ready", "gla_dve", "h_ready", "idx_ready", "in_loaded",
            "marks_ready", "mod_rows", "mod_stored", "ms_ready", "mul_ready", "nmax_ready", "out_done",
            "pool_step", "pool_passed", "pe_passed", "prep_ready", "proj_act", "steps_ready", "rows_loaded", "rstd_ready", "sil_ready",
            "small_l", "small_loaded", "stat_ready", "stat_rstd", "tab_done", "tab_loaded", "w_used", "x_loaded",
            "y_loaded0", "y_loaded1", "y_scaled", "w_hi", "w_lo", "x_hi", "p_ready", "bc0", "bc1", "bc2", "tok_stored0", "tok_stored1",
        )}
        landed = [sem(f"landed{i}") for i in range(LAND)]
        readers = [("a", b) for b in (0, 1, 2, 3, T0, T1, S0)] + [("d", b) for b in range(8)]
        full, free = ({r: {b: sem(f"{what}_{r}{b}") for q, b in readers if q == r} for r in "ad"} for what in ("full", "free"))

        def loop_sems(l):
            names = ["landed%d" % q for q in range(SLOTS)] + [
                "rows0", "rows1", "stored0", "stored1", "pe_gate", "pe_up", "pe_xT", "pe_aT", "pe_y_lo", "pe_y_hi", "w_hi", "w_lo",
                "x_hi", "x_lo", "gate_low", "gate_sum", "silu", "up_low", "up_sum", "acted", "aT", "y_lo", "y_hi",
                "my_free", "picked_in", "picked_out"]
            return {n: sem(f"moe{l}_{n}") for n in names}

        moe = [loop_sems(l) for l in range(2)]

        stream = []
        first = {}

        def dense(name, w, rows, cols):
            first[name] = len(stream)
            kr = rows // P
            for n in range(cols // NB):
                for k0 in range(0, kr, KD):
                    k1 = min(k0 + KD, kr)
                    src = w[k0 * P:k1 * P, n * NB:(n + 1) * NB].rearrange("(k p) n -> p k n", p=P)
                    stream.append((k1 - k0, NB, src))

        def gate_up(name, w):
            first[name] = len(stream)
            v = w.rearrange("(k p) (two n) -> p k two n", p=P, two=2)
            for n in range(FF_SLOTS):
                stream.append((KD, "gu", v[:, :, :, n * FF_W:(n + 1) * FF_W]))

        for l in range(2):
            dense(f"ada{l}", I["w_ada_2"][l], D, MODW)
        for l in range(2):
            if l == 0:
                dense("ev_in", I["ev_w_in"][0], D, 5 * NB)
                dense("ev_out", I["ev_w_out"][0], D, D)
            else:
                dense("od_in", I["od_w_in"][0], D, 6 * NB)
                dense("od_out", I["od_w_out"][0], D, D)
            dense(f"xa_q{l}", I["xa_w_q"][l], D, D)
            dense(f"xa_kv{l}", I["xa_w_kv"][l], D, 2 * D)
            dense(f"xa_out{l}", I["xa_w_out"][l], D, D)
            gate_up(f"ff_in{l}", I["ffn_w_gu"][l])
            dense(f"ff_out{l}", I["ffn_w_down"][l], D_FF, D)
        moe_at = {}
        for l in range(2):
            dense(f"qkv{l}", I["w_qkv_2"][l], D, QKV)
            dense(f"w_o{l}", I["w_o_2"][l], D, D)
            moe_at[l] = len(stream)

        def since(engine, signal, n):
            if not (isinstance(n, int) and n <= 0):
                engine.wait_ge(signal, n)

        def steps_less_2(engine):
            return engine.value_load(steps_i[0:1, 0:1], min_val=N_EXP // 2 - 2, max_val=CAP // ROWS * (N_EXP // 2) - 2)

        def expert_steps(engine, v, body, first=True):
            if first:
                body(0, False)
            with engine.Fori(1, v + 1) as i:
                body(i, False)
            body(v + 1, True)

        def slot_of(n):
            return ring[n % LAND][:].rearrange("p (k n) -> p k n", k=KD)

        def high_of(n):
            return ring[LAND + n % 2][:].rearrange("p (k n) -> p k n", k=KD)

        def halves(n):
            k = stream[n][0]
            return (0, k // 2), (k // 2, k)

        def view(at, *dims):
            n = int(np.prod(dims))
            v = A[:, at:at + n]
            if len(dims) == 1:
                return v
            names = "abcde"[:len(dims)]
            return v.rearrange(f"p ({' '.join(names)}) -> p {' '.join(names)}", **dict(zip(names, dims)))

        modrow = view(0, 2, MODW)
        ev_p = view(0, 2, 5 * NB)
        ev_T = view(5120, 16, 2 * P)
        ev_o = view(9216, 2, D)
        ev_ws = view(11264, 8, P)
        ev_wsT = hTf[:, 3072:4096].rearrange("p (g i) -> p g i", g=8)
        xa_q, xa_k, xa_v = view(0, 2, D), view(2048, 2, D), view(4096, 2, D)
        xa_qT, xa_kT, xa_o = view(6144, KD, 2 * P), view(8192, KD, 2 * P), view(10240, 2, D)
        at_s = hTf[:, 0:1024].rearrange("p (b n) -> p b n", b=2)
        at_e = hTf[:, 1024:2048].rearrange("p (b n) -> p b n", b=2)
        at_eT = hTf[:, 2048:3072].rearrange("p (b k n) -> p b k n", b=2, k=4)
        ff_T = view(0, 2, FF_K, 2 * P)
        ff_sil = view(11264, 2, FF_W)
        ff_act = view(11776, 2, FF_W)
        gl_p = view(0, 2, 6 * NB)
        gl_b = view(6144, 2, NB)
        gl_qT = view(7168, 2, GL_HEADS, 2 * P)
        gl_kT = view(9216, GL_HEADS, 2 * P)
        gl_ks = view(10240, 2, 2, NB)
        gl_S = hTf[:, 0:3072].rearrange("p (h n v) -> p h n v", h=GL_HEADS, n=3)
        gl_att = hTf[:, 3072:3584].rearrange("p (b i) -> p b i", b=4)
        gl_o = gl_p[:, :, 0:D]
        jq = view(0, 4, QKV)
        j_kT = view(6144, KV_HEADS, 4 * P)
        j_qT = view(8192, 2, Q_HEADS, P)
        G = Q_HEADS // KV_HEADS
        j_pT = [v.rearrange("p (k n) -> p k n", k=4) for v in (hb[:].rearrange("p a b -> p (a b)"), hTf[:, 2048:4096])]
        j_e = hTf[:, 0:2048].rearrange("p (b n) -> p b n", b=4)
        j_oT = jq[:, :, 0:D].rearrange("p t (k n) -> p t k n", k=KD)
        LO2 = (hT, 2)
        LO_X = (view(6144, KD, 4 * P), 0)
        LO_J = (view(8192, KD, 4 * P), 0)

        def low(lo, t, k0=0, k1=KD):
            v, off = lo
            return v[:, k0:k1, (off + t) * P:(off + t + 1) * P]

        mx = view(0, 2, D)
        mxT = view(2048, 2, KD, P)
        mact = view(4096, 2, EXP_H)
        mactT = view(5120, 2, EXP_H // P, ROWS)
        mup = view(5632, EXP_H)
        my = view(6144, 2, D)
        msil = view(8192, 2, EXP_H)
        half = KD // 2 * NB
        mwh = [v.rearrange("p (k n) -> p k n", k=KD // 2) for v in (
            hTf[:, 0:half], hTf[:, half:2 * half], hb[:].rearrange("p a b -> p (a b)"), view(9216, half))]
        mw = view(9216, KD, 36)
        mlog = view(9504, 4, 36)
        monehot = view(9648, 4, 2, N_EXP)
        mtab = view(9904, 2, ROWS)
        mtmp = view(10032, 4, 4 * N_EXP)
        mdest = sb("mdest", [P, 8], U32)
        mwt = st[:, 152:160]

        g1, g2 = view(9216, KD, 16), A[0:16, 9344:9344 + NB]
        z1, z1T = view(9856, 2, 16), A[0:16, 9888:10144].rearrange("p (t i) -> p t i", t=2)
        dec = st[:, 160:176].rearrange("p (t h c) -> p t h c", t=2, h=GL_HEADS)
        sink8, sink1 = st[:, 176:192], st[:, 192:208]
        STAT, RSTD = (104, 176), (124, 64)
        rb = st[:, 208:244]
        silu_c = st[:, 208:224].rearrange("p (k c) -> p k c", c=2)
        silu_s = hTf[:, 0:KD * 64].rearrange("p (k c) -> p k c", c=64)
        cond = st[:, 224:240].rearrange("p (k c) -> p k c", c=2)

        dr_mod = DR["mod"]

        def heads_T(v, h, t0, n):
            return v[0:HD, h, t0 * P:t0 * P + n]

        ev_jobs = []
        for t in range(2):
            for h in range(EV_HEADS):
                nk = (t + 1) * P
                ev_jobs.append(dict(
                    scores=[(0, nk, [(heads_T(ev_T, h, t, P), heads_T(ev_T, EV_HEADS + h, 0, nk))])], nk=nk,
                    mask=cst[:, C_WIN0 + (1 - t) * P:C_WIN0 + 2 * P], scale=HD ** -0.5, sink=None,
                    values=[ev_p[:, k, 2 * NB + h * HD:2 * NB + (h + 1) * HD] for k in range(t + 1)],
                    out=ev_o[:, t, h * HD:(h + 1) * HD]))
        xa_jobs = []
        for t in range(2):
            for h in range(X_HEADS):
                xa_jobs.append(dict(
                    scores=[(0, 2 * P, [(xa_qT[:, 2 * h + k, t * P:(t + 1) * P], xa_kT[:, 2 * h + k, :]) for k in range(2)])],
                    nk=2 * P, mask=None, scale=X_HD ** -0.5, sink=None,
                    values=[xa_v[:, k, h * X_HD:(h + 1) * X_HD] for k in range(2)],
                    out=xa_o[:, t, h * X_HD:(h + 1) * X_HD]))

        def joint_jobs(l, t):
            jobs = []
            for h in range(Q_HEADS):
                g = h // (Q_HEADS // KV_HEADS)
                rot, plain = j_qT[0:HD, 0, h, :], j_qT[0:HD, 1, h, :]
                parts = [(2 * P, 2 * P, [(plain, heads_T(j_kT, g, 2, 2 * P))])]
                tiles = [2, 3]
                if t < 2:
                    parts.insert(0, (0, 2 * P, [(rot, heads_T(j_kT, g, 0, 2 * P))]))
                    tiles = [0, 1, 2, 3]
                else:
                    parts = [(0, 2 * P, parts[0][2])]
                jobs.append(dict(
                    scores=parts, nk=P * len(tiles), mask=cst[:, (C_WIN0, C_WIN1)[t]:][:, 0:NB] if l == 0 and t < 2 else None,
                    scale=HD ** -0.5, sink=h if l == 0 else None,
                    values=[jq[:, k, D + (KV_HEADS + g) * HD:D + (KV_HEADS + g + 1) * HD] for k in tiles]))
            return jobs

        block = ctx.enter_context(nc.Block(no_gpsimd_drain=False))

        @block.sync
        def _(sp):
            c = Tally()
            with nc.allow_non_contiguous_dma(reason="features of the condition rows by partition"):
                for q, v in enumerate((I["c_2"][0], I["c_ctx_2"])):
                    sp.dma_start(cond[:, :, q], v.rearrange("(k p) -> p k", p=P)).then_inc(s["in_loaded"], 16)
                sp.dma_start(posi[:], I["positions"][0].rearrange("(t p) -> p t", p=P)).then_inc(s["in_loaded"], 16)
            sp.dma_start(cst[:], I["shape_constants"]).then_inc(s["in_loaded"], 16)

            def load(n):
                k, cols, src = stream[n]
                dst = slot_of(n)
                if cols == "gu":
                    dst = ring[n % LAND][:].rearrange("p (k two n) -> p k two n", k=KD, two=2)
                if n >= LAND:
                    sp.wait_ge(s["w_used"], n - LAND + 1)
                if cols == "gu":
                    for half in range(2):
                        sp.dma_start(dst[:, :, half, :], src[:, :, half, :]).then_inc(landed[n % LAND], 16)
                else:
                    for k0, k1 in halves(n):
                        sp.dma_start(dst[:, k0:k1, :], src[:, k0:k1, :]).then_inc(landed[n % LAND], 16)

            def experts(l):
                m = moe[l]
                w3 = I["w_gate_2"][l], I["w_up_2"][l], I["w_down_2"][l]

                def fetch(part, j, e):
                    q = 3 * j + part
                    src = w3[part][e:e + 1, :, :] if isinstance(e, int) else w3[part][bass.ds(e, 1), :, :]
                    src = src.rearrange("o (k p) n -> p (o k) n", p=P)
                    dst = ring[q][:].rearrange("p (k n) -> p k n", k=src.shape[1])
                    sp.dma_start(dst, src).then_inc(m[f"landed{q}"], 16)

                def pair(i, last):
                    for j in range(2):
                        e = i * 2 + j
                        of = lambda n: n if isinstance(n, int) else n % N_EXP
                        if not (last and j == 1):
                            since(sp, m["pe_gate"], e)
                            fetch(0, 1 - j, of(e + 1))
                            since(sp, m["pe_up"], e)
                            fetch(1, 1 - j, of(e + 1))
                        since(sp, m["pe_y_hi"], e - 1)
                        fetch(2, j, of(e))

                sp.wait_ge(s["w_used"], moe_at[l])
                fetch(0, 0, 0)
                fetch(1, 0, 0)
                pair(0, False)
                sp.wait_ge(s["steps_ready"], l + 1)
                less_2 = steps_less_2(sp)
                steps = less_2 + 2
                expert_steps(sp, less_2, pair, first=False)
                sp.wait_ge(m["pe_y_hi"], steps * 2)
                if l == 0:
                    for q in range(2):
                        sp.wait_ge(s[f"y_loaded{q}"], 32)

            at = 0
            for l in range(2):
                for n in range(at, moe_at[l]):
                    if n == LAND:
                        for t, name in ((0, "x"), (2, "mem")):
                            sp.dma_start(xs[:, t:t + 2, :], I[name][0].rearrange("(t p) d -> p t d", p=P)).then_inc(s["x_loaded"], 16)
                    load(n)
                at = moe_at[l]
                experts(l)
            sp.wait_ge(*c.next(s["fin_ready"]))
            sp.dma_start(out[0].rearrange("(t p) d -> p t d", p=P), hb[:, 0:2, :]).then_inc(s["out_done"], 16)
            sp.wait_ge(s["out_done"], 16)

        @block.tensor
        def _(pe):
            c = Tally()
            busy = {}

            def claim(b):
                if b in busy:
                    pe.wait_ge(*busy[b])

            def publish(ins, b, reader, until=None):
                ins.then_inc(*c.up(full[reader][b]))
                busy[b] = until or c.next(free[reader][b])

            pending = [0]

            def using(ins, n):
                if n > pending[0]:
                    pending[0] = n
                    ins.then_inc(*c.up(s["w_used"]))

            def products(b, n, part, xs_of, lo_of, start, stop, rows=P):
                pe.wait_ge(s["w_lo"], 2 * n + part + 1)
                k0, k1 = halves(n)[part]
                wh, wl = high_of(n), slot_of(n)
                for k in range(k0, k1):
                    trio = [(xs_of(k), wh), (xs_of(k), wl)] + ([(lo_of(k), wh)] if lo_of else [])
                    for q, (x, w) in enumerate(trio):
                        ins = pe.matmul(bank[b][0:rows, :], rnd(x), rnd(w[:, k, :]), start=start and k == k0 and q == 0,
                                        stop=stop and k == k1 - 1 and q == len(trio) - 1)
                        if k == 0 and q == 0:
                            using(ins, n)
                return ins

            def transpose_tile(src, split=False):
                for half in range(2):
                    b = (T0, T1)[half]
                    claim(b)
                    for k in range(4):
                        ins = pe.transpose(bank[b][:, k * P:(k + 1) * P],
                                           src[:, (4 * half + k) * P:(4 * half + k + 1) * P], ident)
                    if split:
                        publish(ins, b, "a", c.next(free["d"][b]))
                    else:
                        publish(ins, b, "ad"[half])

            def norm(n_tiles, split=True):
                for i in range(n_tiles):
                    pe.wait_ge(*c.next(s["h_ready"]))
                    transpose_tile(hb[:, i % 2, :], split)

            def hT_settled():
                claim(T0)
                claim(T1)

            def gemm(n0, slots, tiles, reader, lo=LO2):
                u = 0
                for i in range(slots):
                    for t in tiles:
                        b = u % 4
                        claim(b)
                        for part in range(2):
                            ins = products(b, n0 + i, part, lambda k: hT[:, k, t * P:(t + 1) * P],
                                           lambda k: low(lo, t)[:, k, :], part == 0, part == 1)
                        publish(ins, b, reader(i, t))
                        u += 1

            copy_by = lambda i, t: "ad"[t % 2]

            pe.wait_ge(s["in_loaded"], 64)
            pe.wait_ge(*c.next(s["prep_ready"]))
            for n in range(24):
                claim(n % 4)
                for part in range(2):
                    ins = products(n % 4, n, part, lambda k: silu_s[:, k, :], None, part == 0, part == 1, rows=64)
                publish(ins, n % 4, "d")

            def attention(jobs):
                n = len(jobs)
                e0 = c.count(s["e_ready"])
                for j in range(n + 2):
                    if j < n:
                        sc = S0 + j % 2
                        claim(sc)
                        for col, width, pairs in jobs[j]["scores"]:
                            for m, (a, b) in enumerate(pairs):
                                ins = pe.matmul(bank[sc][:, col:col + width], a, b, start=m == 0, stop=m == len(pairs) - 1)
                        publish(ins, sc, "d", None if jobs[j]["mask"] is not None else (s["e_ready"], e0 + j + 1))
                    if 1 <= j <= n:
                        i = j - 1
                        pe.wait_ge(*c.next(s["e_ready"]))
                        b = T0 + i % 2
                        claim(b)
                        for k in range(jobs[i]["nk"] // P):
                            ins = pe.transpose(bank[b][:, k * P:(k + 1) * P], at_e[:, i % 2, k * P:(k + 1) * P], ident)
                        publish(ins, b, "ad"[i % 2])
                    if j >= 2:
                        i = j - 2
                        pe.wait_ge(*eT_copied[i])
                        claim(i % 2)
                        v = jobs[i]["values"]
                        for k in range(len(v)):
                            ins = pe.matmul(bank[i % 2][:, 0:v[k].shape[-1]], at_eT[:, i % 2, k, :], v[k],
                                            start=k == 0, stop=k == len(v) - 1)
                        publish(ins, i % 2, "d")
                    if 1 <= j <= n:
                        eT_copied[j - 1] = busy[T0 + (j - 1) % 2]

            eT_copied = {}

            def group_attention(jobs):
                n = len(jobs)
                e0 = c.count(s["e_ready"])
                c.next(s["e_ready"], n)
                copied = {}
                for j in range(n + 5):
                    if j < n:
                        sc = S0 + j % 2
                        claim(sc)
                        for col, width, pairs in jobs[j]["scores"]:
                            for a, b in pairs:
                                ins = pe.matmul(bank[sc][:, col:col + width], a, b, start=True, stop=True)
                        publish(ins, sc, "d", None if jobs[j]["mask"] is not None else (s["e_ready"], e0 + j + 1))
                    if 2 <= j <= n + 1:
                        i = j - 2
                        pe.wait_ge(*c.next(s["p_ready"]))
                        b = T0 + i % 2
                        claim(b)
                        for k in range(jobs[i]["nk"] // P):
                            ins = pe.transpose(bank[b][:, k * P:(k + 1) * P], j_e[:, i % 4, k * P:(k + 1) * P], ident)
                        publish(ins, b, "ad"[i % 2])
                        copied[i] = busy[b]
                    if j >= G + 4 and (j - 4) % G == 0:
                        g = (j - 4) // G - 1
                        pe.wait_ge(*copied[g * G + G - 2])
                        pe.wait_ge(*copied[g * G + G - 1])
                        claim(g % 2)
                        v = jobs[g * G]["values"]
                        for k in range(len(v)):
                            ins = pe.matmul(bank[g % 2][0:HD, :], v[k], j_pT[g % 2][:, k, :], start=k == 0, stop=k == len(v) - 1)
                        publish(ins, g % 2, "a")

            def transpose_heads(src, heads, n_b=0):
                for g in range(heads // 4):
                    b = (T0, T1)[(g + n_b) % 2]
                    claim(b)
                    for k in range(4):
                        ins = pe.transpose(bank[b][0:HD, k * P:(k + 1) * P], src(4 * g + k), ident)
                    publish(ins, b, "ad"[(g + n_b) % 2])

            def out_tiles(src, tiles):
                for b in (0, 1):
                    claim(b)
                for t in tiles:
                    transpose_tile(src[:, t, :], split=True)

            def even_mixer():
                norm(2)
                hT_settled()
                gemm(first["ev_in"], 5, [0, 1], lambda i, t: "a" if i >= 3 else copy_by(i, t))
                for t in (1, 0):
                    pe.wait_ge(*c.next(s["prep_ready"]))
                    transpose_heads(lambda h: ev_p[:, t, h * HD:(h + 1) * HD], 16)
                pe.wait_ge(*c.next(s["prep_ready"]))
                transpose_tile(ev_ws.rearrange("p g j -> p (g j)"))
                hT_settled()
                for t in range(2):
                    pe.wait_ge(*c.next(s["prep_ready"]))
                    claim(2 + t)
                    for g in range(EV_HEADS):
                        ins = pe.matmul(bank[2 + t][:, g * HD:(g + 1) * HD], ev_wsT[:, g, :],
                                        ev_p[:, t, 4 * NB + g * HD:4 * NB + (g + 1) * HD], start=True, stop=True)
                    publish(ins, 2 + t, "d")
                attention(ev_jobs)
                for b in (2, 3):
                    claim(b)
                out_tiles(ev_o, [0, 1])
                hT_settled()
                gemm(first["ev_out"], 2, [0, 1], lambda i, t: "d")

            def cross(l):
                norm(4)
                hT_settled()
                gemm(first[f"xa_q{l}"], 2, [0, 1], copy_by, LO_X)
                gemm(first[f"xa_kv{l}"], 4, [2, 3], copy_by, LO_X)
                for src in (xa_q, xa_k):
                    for t in range(2):
                        pe.wait_ge(*c.next(s["prep_ready"]))
                        transpose_tile(src[:, t, :])
                hT_settled()
                attention(xa_jobs)
                out_tiles(xa_o, [0, 1])
                hT_settled()
                gemm(first[f"xa_out{l}"], 2, [0, 1], lambda i, t: "d")

            def feed_forward(l):
                norm(2)
                hT_settled()
                n0 = first[f"ff_in{l}"]
                units = [(i, t) for i in range(FF_SLOTS) for t in range(2)]
                m0 = c.count(s["mul_ready"])

                def turn(u):
                    pe.wait_ge(*c.next(s["mul_ready"]))
                    b = T0 + u % 2
                    claim(b)
                    for k in range(2):
                        ins = pe.transpose(bank[b][:, k * P:(k + 1) * P], ff_act[:, u % 2, k * P:(k + 1) * P], ident)
                    publish(ins, b, "a", c.next(free["d"][b]))

                for u, (i, t) in enumerate(units):
                    claim(u % 4)
                    for part in range(2):
                        ins = products(u % 4, n0 + i, part, lambda k: hT[:, k, t * P:(t + 1) * P],
                                       lambda k: low(LO2, t)[:, k, :], part == 0, part == 1)
                    publish(ins, u % 4, "a", (s["mul_ready"], m0 + u + 1))
                    if u >= 1:
                        turn(u - 1)
                turn(len(units) - 1)
                hT_settled()
                n0 = first[f"ff_out{l}"]
                q = 0
                for n in range(2):
                    for k0 in range(0, FF_K, KD):
                        last = k0 + KD >= FF_K
                        for t in range(2):
                            b = 2 * n + t
                            if k0 == 0:
                                claim(b)
                            for part in range(2):
                                ins = products(b, n0 + q, part, lambda k: ff_T[:, 0, k0 + k, t * P:(t + 1) * P],
                                               lambda k: ff_T[:, 1, k0 + k, t * P:(t + 1) * P],
                                               k0 == 0 and part == 0, last and part == 1)
                            if last:
                                publish(ins, b, "d")
                        q += 1

            def linear_attention():
                norm(2)
                hT_settled()
                pe.wait_ge(s["small_loaded"], 64)
                for t in range(2):
                    claim(S0 + t)
                    for k in range(KD):
                        for q, x in enumerate((hT[:, k, t * P:(t + 1) * P], low(LO2, t)[:, k, :])):
                            ins = pe.matmul(bank[S0 + t][:, 0:16], whole(x), g1[:, k, :], start=k == 0 and q == 0, stop=k == KD - 1 and q == 1)
                    publish(ins, S0 + t, "d")
                gemm(first["od_in"], 2, [0, 1], copy_by)
                for t in range(2):
                    claim(S0 + t)
                    ins = pe.transpose(bank[S0 + t][0:16, 0:P], z1[:, t, :], ident)
                    publish(ins, S0 + t, "d")
                gemm(first["od_in"] + 2, 2, [0, 1], copy_by)
                for t in range(2):
                    claim(S0 + t)
                    ins = pe.matmul(bank[S0 + t][:, :], z1T[:, t, :], g2, start=True, stop=True)
                    publish(ins, S0 + t, "d")
                gemm(first["od_in"] + 4, 2, [0, 1], lambda i, t: "a")
                for t in range(2):
                    pe.wait_ge(*c.next(s["gla_dve"]))
                    la = hb[:, t, 0:NB]
                    claim(S0)
                    publish(pe.matmul(bank[S0][:, :], cst[:, C_CHUNK:C_CHUNK + P], la, start=True, stop=True), S0, "a")
                    claim(S1)
                    publish(pe.matmul(bank[S1][:, :], cst[:, C_SAME:C_SAME + P], la, start=True, stop=True), S1, "d")
                    claim(T0)
                    for h in range(GL_HEADS):
                        ins = pe.matmul(bank[T0][:, 2 * h:2 * h + 2], la[:, h * P:(h + 1) * P], cst[:, C_HALF:C_HALF + 2], start=True, stop=True)
                    publish(ins, T0, "a")
                for t in range(2):
                    pe.wait_ge(*c.next(s["prep_ready"]))
                    transpose_tile(gl_p[:, t, 0:D])
                hT_settled()
                n = 0
                d0 = c.count(s["gla_dve"])
                for t in range(2):
                    for h in range(GL_HEADS):
                        b = S0 + n % 2
                        claim(b)
                        for half in range(2):
                            i0 = t * P + half * GL_CHUNK
                            ins = pe.matmul(bank[b][:, half * GL_CHUNK:(half + 1) * GL_CHUNK], gl_kT[:, h, t * P:(t + 1) * P],
                                            gl_qT[:, half, h, i0:i0 + GL_CHUNK], start=True, stop=True)
                        publish(ins, b, "d", (s["gla_dve"], d0 + n + 1))
                        if t == 0:
                            v = lambda tt: gl_p[:, tt, D + h * GL_DV:D + (h + 1) * GL_DV]
                            claim(T0)
                            for m in range(2):
                                ins = pe.matmul(bank[T0][:, m * GL_DV:(m + 1) * GL_DV], gl_ks[:, 0, m, h * P:(h + 1) * P], v(0), start=True, stop=True)
                            publish(ins, T0, "d")
                            claim(T1)
                            publish(pe.matmul(bank[T1][:, 0:GL_DV], gl_ks[:, 1, 0, h * P:(h + 1) * P], v(1), start=True, stop=True), T1, "d")
                        n += 1
                        if n >= 2:
                            gla_out(n - 2)
                gla_out(7)
                for t in range(2):
                    pe.wait_ge(*c.next(s["prep_ready"]))
                    transpose_tile(gl_p[:, t, 0:D], split=True)
                hT_settled()
                gemm(first["od_out"], 2, [0, 1], lambda i, t: "d")

            def gla_out(n):
                t, h = n // GL_HEADS, n % GL_HEADS
                pe.wait_ge(*c.next(s["gla_dve"]))
                b = n % 4
                claim(b)
                o = bank[b][:, 0:GL_DV]
                parts = [(gl_att[:, n % 4, :], gl_p[:, t, D + h * GL_DV:D + (h + 1) * GL_DV])]
                for half in range(2):
                    chunk = 2 * t + half
                    if chunk:
                        parts.append((gl_qT[:, half, h, t * P:(t + 1) * P], gl_S[:, h, chunk - 1, :]))
                for m, (x, y) in enumerate(parts):
                    ins = pe.matmul(o, x, y, start=m == 0, stop=m == len(parts) - 1)
                publish(ins, b, "d")

            def joint(l):
                norm(2)
                norm(2)
                hT_settled()
                n0 = first[f"qkv{l}"]
                if l == 0:
                    gemm(n0, 3, [0, 1, 2, 3], copy_by, LO_J)
                else:
                    gemm(n0, 2, [0, 1], copy_by, LO_J)
                    gemm(n0 + 2, 1, [0, 1, 2, 3], copy_by, LO_J)
                nb = 0
                for t in range(4):
                    pe.wait_ge(*c.next(s["prep_ready"]))
                    transpose_heads(lambda h: jq[:, t, D + h * HD:D + (h + 1) * HD], KV_HEADS, nb)
                    nb += 1
                for t in range(4 if l == 0 else 2):
                    if t < 2:
                        pe.wait_ge(*c.next(s["prep_ready"]))
                        transpose_heads(lambda h: hb[:, 0, h * HD:(h + 1) * HD], Q_HEADS)
                    else:
                        pe.wait_ge(*c.next(s["prep_ready"]))
                    transpose_heads(lambda h: jq[:, t, h * HD:(h + 1) * HD], Q_HEADS)
                    hT_settled()
                    group_attention(joint_jobs(l, t))
                pe.wait_ge(*c.next(s["prep_ready"]))
                for b in (0, 1):
                    claim(b)
                gemm(first[f"w_o{l}"], 2, [0, 1, 2, 3] if l == 0 else [0, 1], lambda i, t: "d", LO_J)

            def route(l, tiles):
                norm(2, split=False)
                if tiles == 4:
                    norm(2, split=False)
                hT_settled()
                pe.wait_ge(*c.next(s["small_l"], 64))
                for t in range(tiles):
                    claim(t)
                    for k in range(KD):
                        ins = pe.matmul(bank[t][:, 0:36], hT[:, k, t * P:(t + 1) * P], mw[:, k, :], start=k == 0, stop=k == KD - 1)
                        if t == 0 and k == 0:
                            using(ins, moe_at[l])
                    publish(ins, t, "d")
                pe.wait_ge(*c.next(s["marks_ready"]))
                claim(S0)
                for t in range(tiles):
                    marks = lambda q: mtmp[:, q, 0:N_EXP]
                    for q in range(t + 1):
                        pe.matmul(bank[S0][:, t * N_EXP:(t + 1) * N_EXP],
                                  cst[:, (C_BEFORE if q == t else C_ONES):][:, 0:P], marks(q), start=q == 0, stop=q == t)
                for q in range(tiles):
                    ins = pe.matmul(bank[S0][:, 4 * N_EXP:5 * N_EXP], cst[:, C_ONES:C_ONES + P], mtmp[:, q, 0:N_EXP],
                                    start=q == 0, stop=q == tiles - 1)
                publish(ins, S0, "d")
                pe.wait_ge(*c.next(s["tab_loaded"], 64))
                claim(S1)
                for q in range(2):
                    ins = pe.transpose(bank[S1][0:ROWS, q * P:(q + 1) * P], mtab[:, q, :], ident)
                publish(ins, S1, "d")

            def experts(l):
                m = moe[l]
                pe.wait_ge(*c.next(s["steps_ready"]))
                less_2 = steps_less_2(pe)
                steps = less_2 + 2
                for b in range(8):
                    claim(b)

                def turn_rows(j, e, landed_rows):
                    pe.wait_ge(m[f"rows{j}"], landed_rows * 16)
                    pe.sem_inc(s["pe_passed"], 1)
                    for k in range(KD):
                        ins = pe.transpose(bank[T0 + j][:, k * ROWS:(k + 1) * ROWS], mx[0:ROWS, j, k * P:(k + 1) * P], ident[0:ROWS, 0:ROWS])
                    ins.then_inc(m["pe_xT"], 1)

                def hidden(j, e, part):
                    slot = ring[3 * j + part][:].rearrange("p (k n) -> p k n", k=KD)
                    for h in range(2):
                        pe.wait_ge(m["w_lo"], e * 4 + 2 * part + h + 1)
                        for k in range(KD // 2):
                            kk = h * (KD // 2) + k
                            for q, w in enumerate((mwh[2 * part + h][:, k, :], slot[:, kk, :])):
                                ins = pe.matmul(bank[2 * j + part][:, :], rnd(mxT[:, j, kk, :]), rnd(w), start=kk == 0 and q == 0,
                                                stop=kk == KD - 1 and q == 1)
                    ins.then_inc(m[("pe_gate", "pe_up")[part]], 1)

                def turn_act(j, e):
                    pe.wait_ge(m["acted"], e + 1)
                    pe.sem_inc(s["pe_passed"], 1)
                    for k in range(4):
                        ins = pe.transpose(bank[2 * j][:, k * ROWS:(k + 1) * ROWS], mact[0:ROWS, j, k * P:(k + 1) * P], ident[0:ROWS, 0:ROWS])
                    ins.then_inc(m["pe_aT"], 1)

                def down(j, e, landed_down):
                    pe.wait_ge(m["aT"], e + 1)
                    pe.wait_ge(m[f"landed{3 * j + 2}"], landed_down * 16)
                    w = ring[3 * j + 2][:].rearrange("p (k n) -> p k n", k=4)
                    for n, part in enumerate(("lo", "hi")):
                        since(pe, m[f"y_{part}"], e)
                        for k in range(4):
                            ins = pe.matmul(bank[S0 + n][0:ROWS, :], mactT[:, j, k, :], w[:, k, n * NB:(n + 1) * NB], start=k == 0, stop=k == 3)
                        ins.then_inc(m[f"pe_y_{part}"], 1)

                def pair(i, last):
                    for j in range(2):
                        e = i * 2 + j
                        before = not (isinstance(i, int) and j == 0)
                        pe.wait_ge(m["x_lo"], e + 1)
                        hidden(j, e, 0)
                        if before:
                            turn_act(1 - j, e - 1)
                        hidden(j, e, 1)
                        if not (last and j == 1):
                            turn_rows(1 - j, e + 1, i + 1 + j)
                        if before:
                            down(1 - j, e - 1, i + j)

                turn_rows(0, 0, 1)
                expert_steps(pe, less_2, pair)
                turn_act(1, less_2 * 2 + 3)
                down(1, less_2 * 2 + 3, steps)
                pe.wait_ge(m["y_lo"], steps * 2)
                pe.wait_ge(m["y_hi"], steps * 2)

            even_mixer()
            cross(0)
            feed_forward(0)
            linear_attention()
            cross(1)
            feed_forward(1)
            for l in range(2):
                joint(l)
                route(l, 4 - 2 * l)
                experts(l)

        @block.scalar
        def _(act):
            c = Tally()

            def take(b):
                act.wait_ge(*c.next(full["a"][b]))

            def release(ins, b):
                ins.then_inc(*c.up(free["a"][b]))

            def copy_out(b, dst, src=None):
                take(b)
                release(act.activation(dst, bank[b][:, :] if src is None else src, ACT.Copy), b)

            def lo_chunks(dst):
                copy_out(T0, dst, bank[T0][:, :].rearrange("p (k n) -> p k n", k=4))

            def flag(sem_):
                act.wait_ge(*c.last())
                act.activation(st[:, 60:61], cst[:, 0:1], ACT.Copy).then_inc(*c.up(sem_))

            def high(b, dst, n=4):
                take(b)
                act.activation(rnd(dst), bank[b][:, 0:n * P].rearrange("p (k n) -> p k n", k=n), ACT.Copy).then_inc(*c.up(s["x_hi"]))

            def turned(cols):
                for t in cols:
                    for half, b in enumerate((T0, T1)):
                        high(b, hT[:, 4 * half:4 * half + 4, t * P:(t + 1) * P])

            def split(n, used=True):
                if used and n >= 2:
                    act.wait_ge(s["w_used"], n - 1)
                act.wait_ge(landed[n % LAND], 32 * (n // LAND + 1))
                for k0, k1 in halves(n):
                    act.activation(rnd(high_of(n)[:, k0:k1, :]), slot_of(n)[:, k0:k1, :], ACT.Copy).then_inc(*c.up(s["w_hi"]))

            def ahead(n):
                if n + 1 not in moe_at.values():
                    split(n + 1)

            def norm(cols):
                c.next(s["h_ready"], len(cols))
                turned(cols)

            def attention(jobs):
                n = len(jobs)
                for j in range(n + 1):
                    if j < n:
                        exponentials(j, jobs[j], at_s[:, j % 2, :], at_e[:, j % 2, :])
                    if j >= 1 and (j - 1) % 2 == 0:
                        i = j - 1
                        k = jobs[i]["nk"] // P
                        copy_out(T0, at_eT[:, i % 2, 0:k, :], bank[T0][:, 0:k * P].rearrange("p (k n) -> p k n", k=k))

            def exponentials(j, job, scores, e):
                nk, sc = job["nk"], S0 + j % 2
                act.wait_ge(*c.next(s["nmax_ready"]))
                src = bank[sc][:, 0:nk] if job["mask"] is None else scores[:, 0:nk]
                nm = st[:, 16 + j % 4:17 + j % 4]
                act.activation(e[:, 0:nk], src, ACT.Exp, bias=nm, scale=job["scale"],
                               accum_out=st[:, 20 + j % 4:21 + j % 4]).then_inc(*c.up(s["e_ready"]))
                if job["sink"] is not None:
                    h = job["sink"]
                    act.activation(st[:, 24 + j % 4:25 + j % 4], sink1[:, h:h + 1], ACT.Exp, bias=nm).then_inc(*c.up(s["es_ready"]))

            def group_attention(jobs, t):
                n = len(jobs)
                for j in range(n + 6):
                    if j < n:
                        exponentials(j, jobs[j], j_e[:, j % 4, :], j_e[:, j % 4, :])
                    if 3 <= j < n + 3 and j % 2 == 1:
                        i = j - 3
                        k, h = jobs[i]["nk"] // P, i % G
                        copy_out(T0, j_pT[i // G % 2][:, 0:k, h * P:(h + 1) * P], bank[T0][:, 0:k * P].rearrange("p (k n) -> p k n", k=k))
                    if j >= G + 5 and (j - 5) % G == 0:
                        g = (j - 5) // G - 1
                        take(g % 2)
                        o = bank[g % 2][0:HD, :].rearrange("p (a b n) -> p a b n", a=2, b=2)
                        for b in range(2):
                            ins = act.activation(j_oT[b * HD:(b + 1) * HD, t, 2 * g:2 * g + 2, :], o[:, :, b, :], ACT.Copy)
                            if b == 0:
                                ins.then_inc(*c.up(s["act_step"]))
                        release(ins, g % 2)

            def heads_out(dst, heads, n_b=0):
                for g in range(heads // 4):
                    if (g + n_b) % 2 == 0:
                        copy_out(T0, dst(4 * g), bank[T0][0:HD, :].rearrange("p (k n) -> p k n", k=4))

            act.wait_ge(s["in_loaded"], 64)
            act.activation(silu_c, cond, ACT.Silu).then_inc(*c.up(s["act_done"]))
            act.wait_ge(*c.next(s["act_go"]))
            act.wait_ge(*c.last())
            act.activation(rnd(silu_s[:, :, 0:2]), silu_c, ACT.Copy).then_inc(*c.up(s["act_back"]))
            split(0)
            split(1)
            act.wait_ge(*c.next(s["act_go"]))
            act.activation(ropec[:].rearrange("p t c j -> p (t c j)"), st[:, 64:96], ACT.Sin).then_inc(*c.up(s["act_back"]))
            for n in range(2, 25):
                act.wait_ge(full["d"][(n - 2) % 4], (n - 2) // 4 + 1)
                split(n, used=False)

            def even_mixer():
                norm([0, 1])
                act.wait_ge(s["mod_stored"], 32)
                for i in range(5):
                    ahead(first["ev_in"] + i)
                    for t in range(2):
                        b = (2 * i + t) % 4
                        dst = ev_p[:, t, i * NB:(i + 1) * NB]
                        if i >= 3:
                            take(b)
                            release(act.activation(dst, bank[b][:, :], ACT.Gelu), b)
                        elif t == 0:
                            copy_out(b, dst)
                    if i in (1, 4):
                        flag(s["proj_act"])
                for t in (1, 0):
                    heads_out(lambda h: ev_T[0:HD, h:h + 4, t * P:(t + 1) * P], 16)
                lo_chunks(ev_wsT[:, 0:4, :])
                attention(ev_jobs)
                turned([0, 1])
                for i in range(2):
                    ahead(first["ev_out"] + i)

            def cross(l):
                norm([2, 3])
                norm([0, 1])
                for i in range(2):
                    ahead(first[f"xa_q{l}"] + i)
                    copy_out((2 * i) % 4, xa_q[:, 0, i * NB:(i + 1) * NB])
                flag(s["proj_act"])
                for i in range(4):
                    ahead(first[f"xa_kv{l}"] + i)
                    copy_out((2 * i) % 4, (xa_k, xa_v)[i // 2][:, 0, (i % 2) * NB:(i % 2 + 1) * NB])
                    if i == 1:
                        flag(s["proj_act"])
                for dst in (xa_qT, xa_kT):
                    for t in range(2):
                        lo_chunks(dst[:, 0:4, t * P:(t + 1) * P])
                attention(xa_jobs)
                turned([0, 1])
                for i in range(2):
                    ahead(first[f"xa_out{l}"] + i)

            def feed_forward(l):
                norm([0, 1])
                n = 2 * FF_SLOTS
                for u in range(n + 2):
                    if u < n:
                        if u % 2 == 0:
                            ahead(first[f"ff_in{l}"] + u // 2)
                        take(u % 4)
                        if u >= 2:
                            act.wait_ge(*c.next(s["mul_ready"]))
                        act.activation(ff_sil[:, u % 2, :], bank[u % 4][:, 0:FF_W], ACT.Silu).then_inc(*c.up(s["sil_ready"]))
                    if u >= 2:
                        i, t = (u - 2) // 2, (u - 2) % 2
                        high((T0, T1)[t], ff_T[:, 0, 2 * i:2 * i + 2, t * P:(t + 1) * P], 2)
                c.next(s["mul_ready"], 2)
                for q in range(6):
                    ahead(first[f"ff_out{l}"] + q)

            def linear_attention():
                norm([0, 1])
                for i in range(6):
                    ahead(first["od_in"] + i)
                    for t in range(2):
                        b = (2 * (i % 2) + t) % 4
                        dst = gl_p[:, t, i * NB:(i + 1) * NB]
                        if i >= 4:
                            take(b)
                            release(act.activation(dst, bank[b][:, :], ACT.Silu), b)
                        elif t == 0:
                            copy_out(b, dst)
                flag(s["proj_act"])
                for t in range(2):
                    act.wait_ge(*c.next(s["act_go"]))
                    v = hb[:, t, NB:2 * NB]
                    act.activation(v, v, ACT.Exp, scale=-1.0).then_inc(*c.up(s["act_step"]))
                    act.wait_ge(*c.last())
                    act.activation(v, v, ACT.Ln, bias=1.0).then_inc(*c.up(s["act_back"]))
                k = 1.0 / GL_TAU
                for t in range(2):
                    take(S0)
                    act.activation(gl_b[:, t, :], bank[S0][:, :], ACT.Copy).then_inc(*c.up(s["act_back"]))
                    take(T0)
                    release(act.activation(dec[:, t, :, :].rearrange("p h c -> p (h c)"), bank[T0][:, 0:8], ACT.Exp, scale=k), T0)
                    act.wait_ge(*c.next(s["act_go"]))
                    act.wait_ge(*c.last())
                    act.activation(gl_b[:, t, :], bank[S0][:, :], ACT.Exp, scale=-k).then_inc(*c.up(s["act_step"]))
                    release(act.activation(hb[:, t, 0:NB], bank[S0][:, :], ACT.Exp, scale=k), S0)
                    v = hb[:, t, NB:2 * NB]
                    act.activation(v, v, ACT.Exp, scale=k).then_inc(*c.up(s["act_back"]))
                for t in range(2):
                    take(T0)
                    for half in range(2):
                        i0 = half * GL_CHUNK
                        ins = act.activation(gl_qT[:, half, :, t * P + i0:t * P + i0 + GL_CHUNK],
                                             bank[T0][:, :].rearrange("p (h n) -> p h n", h=GL_HEADS)[:, :, i0:i0 + GL_CHUNK], ACT.Copy)
                        if half == 0:
                            ins.then_inc(*c.up(s["act_step"]))
                    release(ins, T0)
                turned([0, 1])
                for i in range(2):
                    ahead(first["od_out"] + i)

            def joint(l):
                if l == 1:
                    split(moe_at[0])
                norm([0, 1])
                norm([2, 3])
                if l == 0:
                    for i in range(3):
                        ahead(first["qkv0"] + i)
                        for t in (0, 2):
                            copy_out((4 * i + t) % 4, jq[:, t, i * NB:(i + 1) * NB])
                else:
                    for i in range(2):
                        ahead(first["qkv1"] + i)
                        copy_out((2 * i) % 4, jq[:, 0, i * NB:(i + 1) * NB])
                    ahead(first["qkv1"] + 2)
                    for t in (0, 2):
                        copy_out(t, jq[:, t, 2 * NB:3 * NB])
                flag(s["proj_act"])
                for t in range(4):
                    heads_out(lambda h: j_kT[0:HD, h:h + 4, t * P:(t + 1) * P], KV_HEADS, t)
                for t in range(4 if l == 0 else 2):
                    if t < 2:
                        heads_out(lambda h: j_qT[0:HD, 0, h:h + 4, :], Q_HEADS)
                    heads_out(lambda h: j_qT[0:HD, 1, h:h + 4, :], Q_HEADS)
                    group_attention(joint_jobs(l, t), t)
                act.wait_ge(*c.last())
                for t in range(4 if l == 0 else 2):
                    act.activation(rnd(hT[:, :, t * P:(t + 1) * P]), j_oT[:, t], ACT.Copy).then_inc(*c.up(s["x_hi"]))
                for i in range(2):
                    ahead(first[f"w_o{l}"] + i)

            def route(l, tiles):
                for t in range(tiles):
                    act.wait_ge(*c.next(s["h_ready"]))
                    act.dma_start(DR["tok"][t * P:(t + 1) * P, :], hb[:, t % 2, :]).then_inc(s[f"tok_stored{t % 2}"], 16)
                    lo_chunks(hT[:, 0:4, t * P:(t + 1) * P])
                for _ in range(2):
                    act.wait_ge(*c.next(s["act_go"]))
                    n = 4 * tiles if _ == 0 else tiles
                    v = st[:, (32, 48)[_]:(32, 48)[_] + n]
                    act.activation(v, v, ACT.Exp).then_inc(*c.up(s["act_back"]))

            def experts(l):
                m = moe[l]

                def high_w(j, part, landed_w, parts=(0, 1)):
                    act.wait_ge(m[f"landed{3 * j + part}"], landed_w * 16)
                    slot = ring[3 * j + part][:].rearrange("p (h k n) -> p h k n", h=2, k=KD // 2)
                    for h in parts:
                        act.activation(rnd(mwh[2 * part + h]), slot[:, h, :, :], ACT.Copy).then_inc(m["w_hi"], 1)

                def high_x(j, e):
                    act.wait_ge(m["pe_xT"], e + 1)
                    act.activation(rnd(mxT[:, j, :, 0:ROWS]), bank[T0 + j][:, :].rearrange("p (k n) -> p k n", k=KD), ACT.Copy).then_inc(m["x_hi"], 1)

                def y_lo(j, e):
                    act.wait_ge(m["pe_y_lo"], e + 1)
                    since(act, m["my_free"], e - 1)
                    act.activation(my[0:ROWS, j, 0:NB], bank[S0][0:ROWS, :], ACT.Copy).then_inc(m["y_lo"], 1)

                def pair(i, last):
                    for j in range(2):
                        e = i * 2 + j
                        more = not (last and j == 1)
                        act.wait_ge(m["pe_gate"], e + 1)
                        since(act, m["acted"], e - 1)
                        act.activation(msil[0:ROWS, j, :], bank[2 * j][ROWS:P, :], ACT.Copy).then_inc(m["gate_low"], 1)
                        act.wait_ge(m["gate_sum"], e + 1)
                        act.activation(msil[0:ROWS, j, :], msil[0:ROWS, j, :], ACT.Silu).then_inc(m["silu"], 1)
                        if more:
                            high_w(1 - j, 0, i + 1 + j)
                        act.wait_ge(m["pe_up"], e + 1)
                        since(act, m["acted"], e)
                        act.activation(mup[0:ROWS, :], bank[2 * j + 1][ROWS:P, :], ACT.Copy).then_inc(m["up_low"], 1)
                        if more:
                            high_x(1 - j, e + 1)
                            high_w(1 - j, 1, i + 1 + j)
                        if not (isinstance(i, int) and j == 0):
                            y_lo(1 - j, e - 1)

                high_w(0, 0, 1)
                for q in range(2):
                    act.wait_ge(*c.next(s[f"tok_stored{q}"], 16 * (2 - l)))
                high_w(0, 1, 1, parts=(0,))
                act.wait_ge(*c.next(s["idx_ready"]))
                high_w(0, 1, 1, parts=(1,))
                act.wait_ge(*c.next(s["steps_ready"]))
                less_2 = steps_less_2(act)
                steps = less_2 + 2
                high_x(0, 0)
                expert_steps(act, less_2, pair)
                y_lo(1, less_2 * 2 + 3)
                y = view(0, 4, 2, D)
                for t in range(4 - 2 * l):
                    if t % 2 == 0:
                        act.wait_ge(*c.next(s[f"y_loaded{t // 2}"], 32))
                    act.activation(y[:, t, 0, :], y[:, t, 0, :], ACT.Copy, scale=mwt[:, 2 * t:2 * t + 1]).then_inc(*c.up(s["y_scaled"]))

            even_mixer()
            cross(0)
            feed_forward(0)
            linear_attention()
            cross(1)
            feed_forward(1)
            for l in range(2):
                joint(l)
                route(l, 4 - 2 * l)
                experts(l)

        @block.vector
        def _(dve):
            c = Tally()

            def step(ins):
                ins.then_inc(*c.up(s["dve_step"]))
                dve.wait_ge(*c.last())

            def settle():
                dve.wait_ge(*c.last())

            def take(b):
                dve.wait_ge(*c.next(full["d"][b]))

            def release(ins, b):
                ins.then_inc(*c.up(free["d"][b]))

            def flag(sem_):
                step(dve.tensor_copy(st[:, 61:62], cst[:, 0:1]))
                dve.tensor_copy(st[:, 62:63], cst[:, 0:1]).then_inc(*c.up(sem_))
                settle()

            def copy_out(b, dst, src=None):
                take(b)
                release(dve.tensor_copy(dst, bank[b][:, :] if src is None else src), b)

            def hi_chunks(dst):
                copy_out(T1, dst, bank[T1][:, :].rearrange("p (k n) -> p k n", k=4))

            def filled(slot, n=1):
                dve.wait_ge(*c.next(s[f"bc{slot}"], 16 * n))

            def inv_rms(tiles):
                for i, t in enumerate(tiles):
                    step(dve.tensor_tensor_reduce(hb[:, i, :], xs[:, t, :], xs[:, t, :], 1.0, 0.0, ALU.mult, ALU.add, st[:, i:i + 1]))
                    dve.tensor_scalar(st[:, 4 + i:5 + i], st[:, i:i + 1], 1.0 / D, EPS, ALU.mult, ALU.add).then_inc(*c.up(s["ms_ready"]))

            def low_parts(b, lo_dst, hi_src, n=4):
                dve.wait_ge(*c.next(s["x_hi"]))
                release(dve.tensor_tensor(rnd(lo_dst), bank[b][:, 0:n * P].rearrange("p (k n) -> p k n", k=n), whole(hi_src), ALU.subtract), b)

            def turned(tiles, lo=LO2):
                for t in tiles:
                    for half, b in enumerate((T0, T1)):
                        low_parts(b, low(lo, t, 4 * half, 4 * half + 4), hT[:, 4 * half:4 * half + 4, t * P:(t + 1) * P])

            def split(n):
                for q, (k0, k1) in enumerate(halves(n)):
                    dve.wait_ge(s["w_hi"], 2 * n + q + 1)
                    w = slot_of(n)[:, k0:k1, :]
                    dve.tensor_tensor(rnd(w), w, whole(high_of(n)[:, k0:k1, :]), ALU.subtract).then_inc(*c.up(s["w_lo"]))

            def ahead(n):
                if n + 1 not in moe_at.values():
                    split(n + 1)

            def norm(tiles, gain, shift=None, stored=None, lo=LO2, turn=True, meanwhile=None):
                settle()
                for i, t in enumerate(tiles):
                    if stored:
                        dve.wait_ge(s[f"tok_stored{i}"], stored)
                inv_rms(tiles)
                if meanwhile:
                    meanwhile()
                filled(gain)
                if shift is not None:
                    filled(shift)
                for i, t in enumerate(tiles):
                    dve.wait_ge(*c.next(s["rstd_ready"]))
                    ins = dve.scalar_tensor_tensor(hb[:, i, :], xs[:, t, :], st[:, 8 + i:9 + i], bc[:, gain, :], ALU.mult, ALU.mult)
                    if shift is not None:
                        step(ins)
                        ins = dve.tensor_tensor(hb[:, i, :], hb[:, i, :], bc[:, shift, :], ALU.add)
                    ins.then_inc(*c.up(s["h_ready"]))
                if lo and turn:
                    turned(tiles, lo)
                elif turn:
                    for t in tiles:
                        hi_chunks(hT[:, 4:8, t * P:(t + 1) * P])

            def group_squares(src, groups, width, q=0):
                sq = hb[:].rearrange("p a b -> p (a b)")[:, 0:groups * width]
                ms = st[:, STAT[q]:STAT[q] + groups]
                step(dve.tensor_tensor(sq, src, src, ALU.mult))
                step(dve.tensor_reduce(ms, sq.rearrange("p (g w) -> p g w", w=width), AX, ALU.add))
                dve.tensor_scalar(ms, ms, 1.0 / width, EPS, ALU.mult, ALU.add).then_inc(*c.up(s["stat_ready"]))

            def group_norm(src, groups, width, gains, q=0, squared=False):
                g3 = lambda v: v.rearrange("p (g w) -> p g w", w=width)
                if not squared:
                    group_squares(src, groups, width, q)
                dve.wait_ge(*c.next(s["stat_rstd"]))
                r = st[:, RSTD[q]:RSTD[q] + groups].unsqueeze(2).to_broadcast([P, groups, width])
                step(dve.tensor_tensor(g3(src), g3(src), r, ALU.mult))
                for g0, g, row in gains:
                    v = g3(src[:, g0 * width:(g0 + g) * width])
                    step(dve.tensor_tensor(v, v, row.unsqueeze(1).to_broadcast([P, g, width]), ALU.mult))

            def residual(n0, units, gates=None, u0=0):
                for u, (n, t) in enumerate(units):
                    if n0 is not None and t == units[0][1]:
                        ahead(n0 + n)
                    b = (u0 + u) % 4
                    x = xs[:, t, n * NB:(n + 1) * NB]
                    take(b)
                    if gates is None:
                        release(dve.tensor_tensor(x, x, bank[b][:, :], ALU.add), b)
                    else:
                        tmp = hb[:, u % 2, 0:NB]
                        release(dve.tensor_tensor(tmp, bank[b][:, :], bc[:, gates[t // 2], n * NB:(n + 1) * NB], ALU.mult), b)
                        settle()
                        step(dve.tensor_tensor(x, x, tmp, ALU.add))

            def row_maximum(j, job, scores):
                nk, sc, q = job["nk"], S0 + j % 2, j % 4
                top, nm = st[:, 12 + q:13 + q], st[:, 16 + q:17 + q]
                take(sc)
                if job["mask"] is not None:
                    release(dve.tensor_tensor_reduce(scores[:, 0:nk], bank[sc][:, 0:nk], job["mask"], 1.0, -3.0e38,
                                                     ALU.add, ALU.max, top), sc)
                    settle()
                else:
                    step(dve.tensor_reduce(top, bank[sc][:, 0:nk], AX, ALU.max))
                if job["sink"] is not None:
                    h = job["sink"]
                    step(dve.tensor_tensor(top, top, sink8[:, h:h + 1], ALU.max))
                dve.tensor_scalar(nm, top, -job["scale"], None, ALU.mult).then_inc(*c.up(s["nmax_ready"]))

            def inverse_sum(i, job):
                q = i % 4
                total, inv = st[:, 20 + q:21 + q], st[:, 28 + q:29 + q]
                dve.wait_ge(*c.next(s["e_ready"]))
                if job["sink"] is not None:
                    dve.wait_ge(*c.next(s["es_ready"]))
                    step(dve.tensor_tensor(total, total, st[:, 24 + q:25 + q], ALU.add))
                step(dve.reciprocal(inv, total))
                return inv

            def attention(jobs):
                n = len(jobs)
                for j in range(n + 2):
                    if j < n:
                        row_maximum(j, jobs[j], at_s[:, j % 2, :])
                    if 1 <= j <= n:
                        i = j - 1
                        inverse_sum(i, jobs[i])
                        if i % 2 == 1:
                            k = jobs[i]["nk"] // P
                            copy_out(T1, at_eT[:, 1, 0:k, :], bank[T1][:, 0:k * P].rearrange("p (k n) -> p k n", k=k))
                    if j >= 2:
                        i = j - 2
                        take(i % 2)
                        out_ = jobs[i]["out"]
                        release(dve.tensor_scalar(out_, bank[i % 2][:, 0:out_.shape[-1]], st[:, 28 + i % 4:29 + i % 4], None, ALU.mult), i % 2)
                settle()

            def group_attention(jobs):
                n = len(jobs)
                for j in range(n + 3):
                    if j < n:
                        row_maximum(j, jobs[j], j_e[:, j % 4, :])
                    if 1 <= j <= n:
                        i = j - 1
                        inv = inverse_sum(i, jobs[i])
                        e = j_e[:, i % 4, 0:jobs[i]["nk"]]
                        dve.tensor_scalar(e, e, inv, None, ALU.mult).then_inc(*c.up(s["p_ready"]))
                    if j >= 4 and j % 2 == 0 and j - 3 < n:
                        i = j - 3
                        k, h = jobs[i]["nk"] // P, i % G
                        copy_out(T1, j_pT[i // G % 2][:, 0:k, h * P:(h + 1) * P], bank[T1][:, 0:k * P].rearrange("p (k n) -> p k n", k=k))
                settle()

            def heads_out(dst, heads, n_b=0):
                for g in range(heads // 4):
                    if (g + n_b) % 2 == 1:
                        copy_out(T1, dst(4 * g), bank[T1][0:HD, :].rearrange("p (k n) -> p k n", k=4))

            def rope_angles():
                dve.wait_ge(s["in_loaded"], 64)
                pos, ang, k = st[:, 96:98], st[:, 32:48], st[:, 48:64]
                step(dve.tensor_copy(pos, posi[:]))
                for t in range(2):
                    step(dve.tensor_scalar(ang[:, 8 * t:8 * t + 8], cst[:, C_FREQ:C_FREQ + 8], pos[:, t:t + 1], None, ALU.mult))
                big = float(3 << 22)
                step(dve.tensor_scalar(k, ang, 1.0 / (2.0 * np.pi), big, ALU.mult, ALU.add))
                step(dve.tensor_scalar(k, k, big, None, ALU.subtract))
                c1 = 6.28125
                c2 = float(np.float32(round((2 * np.pi - c1) * 2 ** 22) / 2 ** 22))
                c3 = 2 * np.pi - c1 - c2
                for part in (c1, c2, c3):
                    step(dve.scalar_tensor_tensor(ang, k, -part, ang, ALU.mult, ALU.add))
                v = st[:, 64:96].rearrange("p (t c j) -> p t c j", t=2, c=2)
                a3, k3 = ang.rearrange("p (t j) -> p t j", t=2), k.rearrange("p (t j) -> p t j", t=2)
                step(dve.tensor_scalar(k, ang, np.pi / 2, -2 * np.pi, ALU.is_gt, ALU.mult))
                step(dve.scalar_tensor_tensor(v[:, :, 0, :], a3, np.pi / 2, k3, ALU.add, ALU.add))
                step(dve.tensor_copy(v[:, :, 1, :], a3))
                dve.tensor_scalar(st[:, 64:96], st[:, 64:96], 3.1415925, -3.1415925, ALU.min, ALU.max).then_inc(*c.up(s["act_go"]))

            def modulation():
                split(0)
                split(1)
                dve.wait_ge(s["rows_loaded"], 128)
                for l in range(2):
                    for n in range(12):
                        m = 12 * l + n
                        b = m % 4
                        v = modrow[0:2, l, n * NB:(n + 1) * NB]
                        if m + 2 <= 24:
                            split(m + 2)
                        take(b)
                        step(dve.tensor_tensor(v, v, bank[b][0:2, :], ALU.add))
                        release(dve.tensor_tensor(v, v, bank[b][32:34, :], ALU.add), b)
                    settle()
                    for q, k in enumerate((1, 4)):
                        gain = hb[0:2, q, :] if l == 0 else bc[0:2, 1 + q, :]
                        v = modrow[0:2, l, k * D:(k + 1) * D]
                        ins = dve.scalar_tensor_tensor(v, v, 1.0, gain, ALU.add, ALU.mult)
                        if q == 0:
                            step(ins)
                    ins.then_inc(*c.up(s["mod_rows"]))
                    if l == 0:
                        dve.wait_ge(s["x_loaded"], 32)
                        norm([0, 1], 0, turn=False)

            def even_mixer():
                turned([0, 1])
                dve.wait_ge(s["mod_stored"], 32)
                filled(1, 2)
                filled(2, 2)
                dve.wait_ge(*c.next(s["act_back"]))
                col = lambda i: ev_p[:, 1, i * NB:(i + 1) * NB]

                def prepare(t):
                    qk = ev_p[:, t, 0:2 * NB]
                    group_norm(qk, 16, HD, [(0, 8, bc[:, 2, 0:HD]), (8, 8, bc[:, 2, HD:2 * HD])])
                    v = qk.rearrange("p (h d) -> p h d", d=HD)
                    x1, x2 = v[:, :, 0:8], v[:, :, 8:16]
                    cos, sin = (ropec[:, t, i, :].unsqueeze(1).to_broadcast([P, 16, 8]) for i in range(2))
                    w = hb[:, 0, 0:4 * 128].rearrange("p (q h j) -> p q h j", q=4, h=16)
                    for q, (a, b) in enumerate(((x1, cos), (x2, sin), (x2, cos), (x1, sin))):
                        dve.tensor_tensor(w[:, q], a, b, ALU.mult).then_inc(*c.up(s["dve_step"]))
                    settle()
                    step(dve.tensor_tensor(x1, w[:, 0], w[:, 1], ALU.subtract))
                    dve.tensor_tensor(x2, w[:, 2], w[:, 3], ALU.add).then_inc(*c.up(s["prep_ready"]))
                    settle()

                n0 = first["ev_in"]
                for i in range(2):
                    ahead(n0 + i)
                    copy_out((2 * i + 1) % 4, col(i))
                settle()
                ahead(n0 + 2)
                copy_out(1, col(2))
                prepare(1)
                ahead(n0 + 3)
                dve.wait_ge(*c.next(s["proj_act"]))
                prepare(0)
                ahead(n0 + 4)
                dve.wait_ge(s["small_loaded"], 32)
                tril = cst[:, C_TRIL:C_TRIL + P].unsqueeze(1).to_broadcast([P, 8, P])
                dve.tensor_tensor(ev_ws, ev_ws, tril, ALU.mult).then_inc(*c.up(s["prep_ready"]))
                dve.wait_ge(*c.next(s["proj_act"]))
                for t in range(2):
                    settle()
                    v = ev_p[:, t, 4 * NB:5 * NB].rearrange("p (g d) -> p g d", g=8)
                    sq = hb[:, 0, 0:NB].rearrange("p (g d) -> p g d", g=8)
                    wide = lambda x: x.unsqueeze(2).to_broadcast([P, 8, HD])
                    mean, ms, rs = st[:, 96:104], st[:, 104:112], st[:, 124:132]
                    step(dve.tensor_reduce(mean, v, AX, ALU.add))
                    step(dve.tensor_scalar(mean, mean, 1.0 / HD, None, ALU.mult))
                    step(dve.tensor_tensor(v, v, wide(mean), ALU.subtract))
                    step(dve.tensor_tensor(sq, v, v, ALU.mult))
                    step(dve.tensor_reduce(ms, sq, AX, ALU.add))
                    dve.tensor_scalar(ms, ms, 1.0 / HD, EPS, ALU.mult, ALU.add).then_inc(*c.up(s["stat_ready"]))
                    dve.wait_ge(*c.next(s["stat_rstd"]))
                    step(dve.tensor_tensor(v, v, wide(rs), ALU.mult))
                    vf = ev_p[:, t, 4 * NB:5 * NB]
                    step(dve.tensor_tensor(vf, vf, bc[:, 1, 0:NB], ALU.mult))
                    dve.tensor_tensor(vf, vf, bc[:, 1, NB:2 * NB], ALU.add).then_inc(*c.up(s["prep_ready"]))
                settle()
                for t in (1, 0):
                    heads_out(lambda h: ev_T[0:HD, h:h + 4, t * P:(t + 1) * P], 16)
                hi_chunks(ev_wsT[:, 4:8, :])
                for t in range(2):
                    take(2 + t)
                    for g in range(EV_HEADS):
                        ins = dve.scalar_tensor_tensor(ev_o[:, t, NB + g * HD:NB + (g + 1) * HD], bank[2 + t][:, g * HD:(g + 1) * HD],
                                                       st[:, 144 + g:145 + g], ev_p[:, t, 3 * NB + g * HD:3 * NB + (g + 1) * HD],
                                                       ALU.add, ALU.mult)
                        if g < EV_HEADS - 1:
                            ins.then_inc(*c.up(s["dve_step"]))
                    release(ins, 2 + t)
                attention(ev_jobs)
                turned([0, 1])
                residual(first["ev_out"], [(n, t) for n in range(2) for t in range(2)])

            def cross(l):
                norm([2, 3], 0, lo=LO_X)
                norm([0, 1], 1, lo=LO_X)
                filled(2, 2)
                for i in range(2):
                    ahead(first[f"xa_q{l}"] + i)
                    copy_out((2 * i + 1) % 4, xa_q[:, 1, i * NB:(i + 1) * NB])
                for i in range(4):
                    ahead(first[f"xa_kv{l}"] + i)
                    copy_out((2 * i + 1) % 4, (xa_k, xa_v)[i // 2][:, 1, (i % 2) * NB:(i % 2 + 1) * NB])
                    settle()
                    if i % 2 == 0:
                        dve.wait_ge(*c.next(s["proj_act"]))
                    src, gain = ((xa_q, 0), (xa_k, X_HD))[i // 2]
                    group_norm(src[:, i % 2, :], X_HEADS, X_HD, [(0, X_HEADS, bc[:, 2, gain:gain + X_HD])])
                    flag(s["prep_ready"])
                for dst in (xa_qT, xa_kT):
                    for t in range(2):
                        hi_chunks(dst[:, 4:8, t * P:(t + 1) * P])
                attention(xa_jobs)
                turned([0, 1])
                residual(first[f"xa_out{l}"], [(n, t) for n in range(2) for t in range(2)])

            def feed_forward(l):
                norm([0, 1], 0)
                n = 2 * FF_SLOTS
                for u in range(n + 2):
                    if u < n:
                        if u % 2 == 0:
                            ahead(first[f"ff_in{l}"] + u // 2)
                        dve.wait_ge(*c.next(s["sil_ready"]))
                        dve.tensor_tensor(ff_act[:, u % 2, :], ff_sil[:, u % 2, :], bank[u % 4][:, FF_W:2 * FF_W], ALU.mult).then_inc(*c.up(s["mul_ready"]))
                    if u >= 2:
                        i, t = (u - 2) // 2, (u - 2) % 2
                        hi, lo = (ff_T[:, q, 2 * i:2 * i + 2, t * P:(t + 1) * P] for q in range(2))
                        low_parts((T0, T1)[t], lo, hi, 2)
                settle()
                n0 = first[f"ff_out{l}"]
                for q in range(4):
                    ahead(n0 + q)
                residual(None, [(0, t) for t in range(2)])
                for q in range(4, 6):
                    ahead(n0 + q)
                residual(None, [(1, t) for t in range(2)], u0=2)

            def linear_attention():
                norm([0, 1], 0)
                filled(1)
                filled(2)
                dve.memset(gl_qT.rearrange("p a b c -> p (a b c)"), 0.0).then_inc(*c.up(s["dve_step"]))
                for t in range(2):
                    copy_out(S0 + t, z1[:, t, :], bank[S0 + t][:, 0:16])
                for i in range(2):
                    ahead(first["od_in"] + i)
                    copy_out((2 * i + 1) % 4, gl_p[:, 1, i * NB:(i + 1) * NB])
                for t in range(2):
                    copy_out(S0 + t, z1T[:, t, :], bank[S0 + t][0:16, 0:P])
                for i in range(2, 4):
                    ahead(first["od_in"] + i)
                    copy_out((2 * i + 1) % 4, gl_p[:, 1, i * NB:(i + 1) * NB])
                z = lambda t: hb[:, t, 0:NB]
                w = lambda t: hb[:, t, NB:2 * NB]
                for t in range(2):
                    take(S0 + t)
                    release(dve.tensor_tensor(z(t), bank[S0 + t][:, :], bc[:, 2, 0:NB], ALU.add), S0 + t)
                    settle()
                    dve.scalar_tensor_tensor(w(t), z(t), -1.0, z(t), ALU.mult, ALU.max).then_inc(*c.up(s["act_go"]))
                for i in range(4, 6):
                    ahead(first["od_in"] + i)
                dve.wait_ge(*c.next(s["proj_act"]))
                for t in range(2):
                    dve.wait_ge(*c.next(s["act_back"]))
                    dve.scalar_tensor_tensor(z(t), z(t), 0.0, w(t), ALU.min, ALU.subtract).then_inc(*c.up(s["gla_dve"]))
                for t in range(2):
                    copy_out(S1, w(t))
                    settle()
                    dve.wait_ge(*c.next(s["act_back"]))
                    dve.tensor_tensor(w(t), w(t), gl_b[:, t, :], ALU.subtract).then_inc(*c.up(s["act_go"]))
                    dve.wait_ge(*c.next(s["act_back"]))
                    q, k = gl_p[:, t, 0:NB], gl_p[:, t, NB:2 * NB]
                    for half in range(2):
                        dve.scalar_tensor_tensor(gl_ks[:, t, half, :], k, cst[:, C_HALF + half:C_HALF + half + 1], w(t), ALU.mult, ALU.mult)\
                           .then_inc(*c.up(s["dve_step"]))
                    step(dve.tensor_tensor(k, k, gl_b[:, t, :], ALU.mult))
                    dve.scalar_tensor_tensor(q, q, GL_DK ** -0.5, z(t), ALU.mult, ALU.mult).then_inc(*c.up(s["prep_ready"]))
                for t in range(2):
                    hi_chunks(gl_kT[:, :, t * P:(t + 1) * P])
                for n in range(9):
                    if n < 8:
                        h = n % GL_HEADS
                        if n < GL_HEADS:
                            take(T0)
                            step(dve.tensor_copy(gl_S[:, h, 0, :], bank[T0][:, 0:GL_DV]))
                            release(dve.scalar_tensor_tensor(gl_S[:, h, 1, :], gl_S[:, h, 0, :], dec[:, 0, h, 1:2], bank[T0][:, GL_DV:2 * GL_DV],
                                                             ALU.mult, ALU.add), T0)
                            settle()
                            take(T1)
                            release(dve.scalar_tensor_tensor(gl_S[:, h, 2, :], gl_S[:, h, 1, :], dec[:, 1, h, 0:1], bank[T1][:, 0:GL_DV],
                                                             ALU.mult, ALU.add), T1)
                        take(S0 + n % 2)
                        dve.tensor_tensor(gl_att[:, n % 4, :], bank[S0 + n % 2][:, 0:P], cst[:, C_CHUNK:C_CHUNK + P], ALU.mult).then_inc(*c.up(s["gla_dve"]))
                    if n >= 1:
                        t, h = (n - 1) // GL_HEADS, (n - 1) % GL_HEADS
                        copy_out((n - 1) % 4, gl_o[:, t, h * GL_DV:(h + 1) * GL_DV], bank[(n - 1) % 4][:, 0:GL_DV])
                settle()
                for t in range(2):
                    o = gl_o[:, t, :]
                    group_norm(o, GL_HEADS, GL_DV, [])
                    step(dve.tensor_tensor(o, o, bc[:, 1, :], ALU.mult))
                    dve.tensor_tensor(o, o, gl_p[:, t, 2 * D:3 * D], ALU.mult).then_inc(*c.up(s["prep_ready"]))
                    settle()
                turned([0, 1])
                residual(first["od_out"], [(n, t) for n in range(2) for t in range(2)])

            def rotate(x, cos, sin, dst, tmp, heads):
                wide = lambda v: v.unsqueeze(1).to_broadcast([P, heads, HD])
                h3 = lambda v: v.rearrange("p (h d) -> p h d", d=HD)
                h4 = lambda v: v.rearrange("p (h a b i) -> p h a b i", h=heads, a=2, b=2)
                dve.tensor_tensor(h3(dst), h3(x), wide(cos), ALU.mult).then_inc(*c.up(s["dve_step"]))
                s4 = sin.rearrange("p (a b i) -> p a b i", a=2, b=2)
                for b in range(2):
                    sw = s4[:, :, b, :].unsqueeze(1).to_broadcast([P, heads, 2, 16])
                    dve.tensor_tensor(h4(tmp)[:, :, :, b, :], h4(x)[:, :, :, 1 - b, :], sw, ALU.mult).then_inc(*c.up(s["dve_step"]))
                settle()

            def joint(l):
                norm([0, 1], 0, 1, lo=LO_J, meanwhile=None if l == 0 else lambda: split(moe_at[0]))
                if l == 0:
                    dve.wait_ge(s["ctx_loaded"], 32)
                norm([2, 3], 0, 1, lo=LO_J)
                if l == 0:
                    for i in range(3):
                        ahead(first["qkv0"] + i)
                        for t in (1, 3):
                            copy_out(t, jq[:, t, i * NB:(i + 1) * NB])
                else:
                    for i in range(2):
                        ahead(first["qkv1"] + i)
                        copy_out((2 * i + 1) % 4, jq[:, 1, i * NB:(i + 1) * NB])
                    ahead(first["qkv1"] + 2)
                    for t in (1, 3):
                        copy_out(t, jq[:, t, 2 * NB:3 * NB])
                settle()
                dve.wait_ge(*c.next(s["proj_act"]))
                hbf = hb[:].rearrange("p a b -> p (a b)")
                if l == 1:
                    filled(0, 2)
                    for t in range(2):
                        group_squares(jq[:, t, 0:20 * HD], 20, HD, t)
                for t in range(4):
                    k = jq[:, t, D:D + KV_HEADS * HD]
                    if l == 1:
                        gk = bc[:, 0, HD:2 * HD]
                        if t < 2:
                            group_norm(jq[:, t, 0:20 * HD], 20, HD, [(0, 16, bc[:, 0, 0:HD]), (16, 4, gk)], q=t, squared=True)
                        else:
                            group_norm(k, 4, HD, [(0, 4, gk)])
                    if t < 2:
                        rotate(k, cst[:, C_COS + HD * t:C_COS + HD * (t + 1)], cst[:, C_SIN + HD * t:C_SIN + HD * (t + 1)],
                               hbf[:, 0:256], hbf[:, 256:512], KV_HEADS)
                        dve.tensor_tensor(k, hbf[:, 0:256], hbf[:, 256:512], ALU.add).then_inc(*c.up(s["prep_ready"]))
                        settle()
                    else:
                        flag(s["prep_ready"])
                for t in range(4):
                    heads_out(lambda h: j_kT[0:HD, h:h + 4, t * P:(t + 1) * P], KV_HEADS, t)
                for t in range(4 if l == 0 else 2):
                    settle()
                    if t < 2:
                        rotate(jq[:, t, 0:D], cst[:, C_COS + HD * t:C_COS + HD * (t + 1)], cst[:, C_SIN + HD * t:C_SIN + HD * (t + 1)],
                               hb[:, 0, :], hb[:, 1, :], Q_HEADS)
                        dve.tensor_tensor(hb[:, 0, :], hb[:, 0, :], hb[:, 1, :], ALU.add).then_inc(*c.up(s["prep_ready"]))
                        heads_out(lambda h: j_qT[0:HD, 0, h:h + 4, :], Q_HEADS)
                    else:
                        flag(s["prep_ready"])
                    heads_out(lambda h: j_qT[0:HD, 1, h:h + 4, :], Q_HEADS)
                    if l == 0 and t == 0:
                        step(dve.tensor_scalar(sink8, sink1, float(HD ** 0.5), None, ALU.mult))
                    group_attention(joint_jobs(l, t))
                tiles = range(4 if l == 0 else 2)
                for t in tiles:
                    dve.wait_ge(*c.next(s["x_hi"]))
                    v = low(LO_J, t)
                    dve.tensor_tensor(rnd(v), j_oT[:, t], whole(hT[:, :, t * P:(t + 1) * P]), ALU.subtract).then_inc(*c.up(s["dve_step"]))
                flag(s["prep_ready"])
                filled(2)
                if l == 0:
                    filled(0)
                residual(first[f"w_o{l}"], [(n, t) for n in range(2) for t in tiles], gates=(2, 0))

            def route(l, tiles):
                norm([0, 1], 0, 1, lo=None)
                if tiles == 4:
                    norm([2, 3], 0, 1, stored=16, lo=None)
                T = tiles
                dve.wait_ge(*c.next(s["small_l"], 64))
                for t in range(T):
                    take(t)
                    release(dve.tensor_tensor(mlog[:, t, :], bank[t][:, 0:36], rb, ALU.add), t)
                settle()
                lg, lr = mlog[:, 0:T, 0:4], mlog[:, 0:T, 4:36]
                wide = lambda v, n: v.unsqueeze(2).to_broadcast([P, T, n])
                gmax, e4 = st[:, 0:T], st[:, 32:32 + 4 * T].rearrange("p (t g) -> p t g", g=4)
                step(dve.tensor_reduce(gmax, lg, AX, ALU.max))
                dve.tensor_tensor(e4, lg, wide(gmax, 4), ALU.subtract).then_inc(*c.up(s["act_go"]))
                w4 = mtmp[:, 0, 0:4 * T].rearrange("p (t g) -> p t g", g=4)
                grp = st[:, 4:4 + T]
                step(dve.tensor_tensor(w4, lg, wide(gmax, 4), ALU.is_equal))
                iota4 = cst[:, C_IOTA:C_IOTA + 4].unsqueeze(1).to_broadcast([P, T, 4])
                step(dve.scalar_tensor_tensor(w4, w4, -100.0, iota4, ALU.mult, ALU.add))
                step(dve.tensor_reduce(grp, w4, AX, ALU.min))
                m32 = mtmp[:, 1, 0:N_EXP * T].rearrange("p (t e) -> p t e", e=N_EXP)
                n32 = mtmp[:, 2, 0:N_EXP * T].rearrange("p (t e) -> p t e", e=N_EXP)
                group = cst[:, C_GROUP:C_GROUP + N_EXP].unsqueeze(1).to_broadcast([P, T, N_EXP])
                step(dve.tensor_tensor(m32, group, wide(grp, N_EXP), ALU.is_equal))
                step(dve.tensor_tensor(lr, lr, m32, ALU.mult))
                step(dve.tensor_scalar(n32, m32, 1.0, -MASKED, ALU.subtract, ALU.mult))
                step(dve.tensor_tensor(n32, n32, lr, ALU.add))
                best = mtmp[:, 3, 0:8 * T].rearrange("p (t e) -> p t e", e=8)
                where = mtmp[:, 3, 32:32 + 8 * T].bitcast(U32).rearrange("p (t e) -> p t e", e=8)
                for t in range(T):
                    step(dve.max(best[:, t, :], n32[:, t, :]))
                    step(dve.max_index(where[:, t, :], best[:, t, :], n32[:, t, :]))
                eid = mtmp[:, 3, 64:64 + 2 * T].rearrange("p (t j) -> p t j", j=2)
                step(dve.tensor_copy(eid, where[:, :, 0:2]))
                dve.tensor_tensor(st[:, 48:48 + T], best[:, :, 1], best[:, :, 0], ALU.subtract).then_inc(*c.up(s["act_go"]))
                hot = monehot[:, 0:T, :, :]
                iota = cst[:, C_IOTA:C_IOTA + N_EXP].unsqueeze(1).to_broadcast([P, T, N_EXP])
                for j in range(2):
                    step(dve.tensor_tensor(hot[:, :, j, :], iota, wide(eid[:, :, j], N_EXP), ALU.is_equal))
                dve.tensor_tensor(mtmp[:, 0:T, 0:N_EXP], hot[:, :, 0, :], hot[:, :, 1, :], ALU.add).then_inc(*c.up(s["marks_ready"]))
                dve.wait_ge(*c.next(s["act_back"], 2))
                total, e21, p, q = st[:, 0:T], st[:, 48:48 + T], st[:, 4:4 + T], st[:, 8:8 + T]
                settle()
                step(dve.tensor_reduce(total, e4, AX, ALU.add))
                step(dve.tensor_scalar(q, e21, 1.0, None, ALU.add))
                step(dve.tensor_tensor(total, total, q, ALU.mult))
                step(dve.reciprocal(p, total))
                w2 = mwt[:, 0:2 * T].rearrange("p (t j) -> p t j", j=2)
                step(dve.tensor_copy(w2[:, :, 0], p))
                step(dve.tensor_tensor(w2[:, :, 1], p, e21, ALU.mult))
                take(S0)
                rank = bank[S0][:, 0:N_EXP * T].rearrange("p (t e) -> p t e", e=N_EXP)
                r = st[:, 32:32 + 2 * T].rearrange("p (t j) -> p t j", j=2)
                prod = mtmp[:, 1, 0:N_EXP * T].rearrange("p (t e) -> p t e", e=N_EXP)
                for j in range(2):
                    step(dve.tensor_tensor(prod, hot[:, :, j, :], rank, ALU.mult))
                    step(dve.tensor_reduce(r[:, :, j], prod, AX, ALU.add))
                step(dve.scalar_tensor_tensor(r, eid, float(CAP), r, ALU.mult, ALU.add))
                dve.tensor_copy(mdest[:, 0:2 * T], st[:, 32:32 + 2 * T]).then_inc(*c.up(s["dest_ready"]))
                most, n = st[:, 0:1], st[:, 1:2]
                release(dve.tensor_reduce(most, bank[S0][:, 4 * N_EXP:5 * N_EXP], AX, ALU.max), S0)
                settle()
                step(dve.tensor_scalar(n, most, float(ROWS), 1.0, ALU.is_gt, ALU.add))
                for k in range(2, T * P // ROWS):
                    step(dve.scalar_tensor_tensor(n, most, float(k * ROWS), n, ALU.is_gt, ALU.add))
                dve.tensor_scalar(steps_i[:], n, float(N_EXP // 2), -2.0, ALU.mult, ALU.add).then_inc(*c.up(s["steps_ready"]))
                take(S1)
                release(dve.tensor_copy(idx[:, 0, :], bank[S1][0:ROWS, 0:2 * P]), S1)
                settle()
                dve.tensor_scalar(idx[:, 1, :], idx[:, 0, :], 1, None, ALU.logical_shift_right).then_inc(*c.up(s["idx_ready"]))
                settle()

            def experts(l):
                m = moe[l]
                less_2 = steps_less_2(dve)
                steps = less_2 + 2

                def low_w(j, e, part):
                    slot = ring[3 * j + part][:].rearrange("p (h k n) -> p h k n", h=2, k=KD // 2)
                    for h in range(2):
                        dve.wait_ge(m["w_hi"], e * 4 + 2 * part + h + 1)
                        dve.tensor_tensor(rnd(slot[:, h, :, :]), slot[:, h, :, :], whole(mwh[2 * part + h]), ALU.subtract).then_inc(m["w_lo"], 1)

                def low_x(j, e):
                    dve.wait_ge(m["x_hi"], e + 1)
                    dve.tensor_tensor(rnd(mxT[:, j, :, ROWS:P]), bank[T0 + j][:, :].rearrange("p (k n) -> p k n", k=KD),
                                      whole(mxT[:, j, :, 0:ROWS]), ALU.subtract).then_inc(m["x_lo"], 1)

                def turned_act(j, e):
                    dve.wait_ge(m["pe_aT"], e + 1)
                    dve.tensor_copy(mactT[:, j, :, :], bank[2 * j][:, 0:4 * ROWS].rearrange("p (k n) -> p k n", k=4)).then_inc(m["aT"], 1)

                def y_hi(j, e):
                    dve.wait_ge(m["pe_y_hi"], e + 1)
                    since(dve, m["my_free"], e - 1)
                    dve.tensor_copy(my[0:ROWS, j, NB:2 * NB], bank[S1][0:ROWS, :]).then_inc(m["y_hi"], 1)

                def pair(i, last):
                    for j in range(2):
                        e = i * 2 + j
                        before = not (isinstance(i, int) and j == 0)
                        more = not (last and j == 1)
                        if before:
                            turned_act(1 - j, e - 1)
                        g = msil[0:ROWS, j, :]
                        dve.wait_ge(m["gate_low"], e + 1)
                        dve.tensor_tensor(g, g, bank[2 * j][0:ROWS, :], ALU.add).then_inc(m["gate_sum"], 1)
                        if more:
                            low_w(1 - j, e + 1, 0)
                        dve.wait_ge(m["up_low"], e + 1)
                        dve.tensor_tensor(mup[0:ROWS, :], mup[0:ROWS, :], bank[2 * j + 1][0:ROWS, :], ALU.add).then_inc(m["up_sum"], 1)
                        dve.wait_ge(m["silu"], e + 1)
                        dve.wait_ge(m["up_sum"], e + 1)
                        dve.tensor_tensor(mact[0:ROWS, j, :], g, mup[0:ROWS, :], ALU.mult).then_inc(m["acted"], 1)
                        if more:
                            low_x(1 - j, e + 1)
                            low_w(1 - j, e + 1, 1)
                        if before:
                            y_hi(1 - j, e - 1)

                low_w(0, 0, 0)
                low_x(0, 0)
                low_w(0, 0, 1)
                expert_steps(dve, less_2, pair)
                turned_act(1, less_2 * 2 + 3)
                y_hi(1, less_2 * 2 + 3)
                tiles = 4 - 2 * l
                y = view(0, 4, 2, D)
                filled(2)
                if l == 0:
                    filled(0)
                for t in range(tiles):
                    a, b = y[:, t, 0, :], y[:, t, 1, :]
                    if t % 2 == 0:
                        dve.wait_ge(*c.next(s[f"y_loaded{t // 2}"], 32))
                    dve.wait_ge(*c.next(s["y_scaled"]))
                    step(dve.scalar_tensor_tensor(a, b, mwt[:, 2 * t + 1:2 * t + 2], a, ALU.mult, ALU.add))
                    step(dve.tensor_tensor(a, a, bc[:, 2 if t < 2 else 0, :], ALU.mult))
                    step(dve.tensor_tensor(xs[:, t, :], xs[:, t, :], a, ALU.add))

            dve.wait_ge(s["in_loaded"], 64)
            zeros = cst[:, 0:KD * 64].rearrange("p (k c) -> p k c", c=64)
            dve.tensor_scalar(rnd(silu_s), zeros, 0.0, None, ALU.mult).then_inc(*c.up(s["act_go"]))
            settle()
            dve.wait_ge(*c.next(s["act_back"]))
            dve.tensor_tensor(rnd(silu_s[:, :, 32:34]), silu_c, whole(silu_s[:, :, 0:2]), ALU.subtract).then_inc(*c.up(s["prep_ready"]))
            rope_angles()
            modulation()
            dve.wait_ge(s["x_loaded"], 32)
            even_mixer()
            cross(0)
            feed_forward(0)
            linear_attention()
            cross(1)
            feed_forward(1)
            for l in range(2):
                joint(l)
                route(l, 4 - 2 * l)
                experts(l)
            settle()
            inv_rms([0, 1])
            filled(0)
            for i in range(2):
                dve.wait_ge(*c.next(s["rstd_ready"]))
                step(dve.scalar_tensor_tensor(hb[:, i, :], xs[:, i, :], st[:, 8 + i:9 + i], bc[:, 0, :], ALU.mult, ALU.mult))
            flag(s["fin_ready"])

        def experts(pool, c, step, l):
            m = moe[l]
            tiles = 4 - 2 * l
            pool.wait_ge(*c.next(s["idx_ready"]))
            pool.wait_ge(*c.next(s["steps_ready"]))
            for q in range(2):
                pool.wait_ge(*c.next(s[f"tok_stored{q}"], 16 * tiles // 2))
            less_2 = steps_less_2(pool)
            steps = less_2 + 2

            def apart():
                pool.sem_inc(s["pool_passed"], 1)

            def column(kind, e):
                return idx[:, kind, e:e + 1] if isinstance(e, int) else idx[:, kind, bass.ds(e, 1)]

            def gather(j, e):
                since(pool, m["pe_xT"], e - 1)
                apart()
                pool.tensor_copy(pick[:, 0, j:j + 1], column(1, e)).then_inc(m["picked_in"], 1)
                pool.wait_ge(m["picked_in"], e + 1)
                apart()
                pool.indirect_dma_start(out=mx[0:ROWS, j, :], out_offset=None, in_=DR["tok"],
                                        in_offset=bass.IndirectOffsetOnAxis(ap=pick[:, 0, j:j + 1], axis=0),
                                        bounds_check=tiles * P - 1, oob_is_err=False).then_inc(m[f"rows{j}"], 16)

            def store(j, e):
                pool.tensor_copy(pick[:, 1, j:j + 1], column(0, e)).then_inc(m["picked_out"], 1)
                pool.wait_ge(m["picked_out"], e + 1)
                pool.wait_ge(m["y_lo"], e + 1)
                pool.wait_ge(m["y_hi"], e + 1)
                apart()
                pool.indirect_dma_start(out=DR["y"][l], out_offset=bass.IndirectOffsetOnAxis(ap=pick[:, 1, j:j + 1], axis=0),
                                        in_=my[0:ROWS, j, :], in_offset=None,
                                        bounds_check=2 * tiles * P - 1, oob_is_err=False).then_inc(m[f"stored{j}"], 16)

            def pair(i, last):
                for j in range(2):
                    if not last:
                        gather(j, i * 2 + j + 2)
                    if not isinstance(i, int):
                        pool.wait_ge(m[f"stored{j}"], i * 16)
                        pool.sem_inc(m["my_free"], 1)
                    if not (isinstance(i, int) and j == 0):
                        store(1 - j, i * 2 + j - 1)

            gather(0, 0)
            gather(1, 1)
            expert_steps(pool, less_2, pair)
            store(1, less_2 * 2 + 3)
            for j in range(2):
                pool.wait_ge(m[f"stored{j}"], steps * 16)
            apart()
            y = view(0, 4, 2, D)
            for t in range(tiles):
                pool.dma_start(y[:, t, :, :], DR["y"][l][2 * t * P:2 * (t + 1) * P, :].rearrange("(p j) d -> p j d", j=2)).then_inc(s[f"y_loaded{t // 2}"], 16)

        @block.gpsimd
        def _(pool):
            c = Tally()

            def step(ins):
                ins.then_inc(*c.up(s["pool_step"]))
                pool.wait_ge(*c.last())

            def fill(slot, *rows):
                at = 0
                for row in rows:
                    n = row.shape[-1]
                    pool.dma_start(bc[:, slot, at:at + n], row.partition_broadcast(P)).then_inc(s[f"bc{slot}"], 16)
                    at += n

            def norms(n=2):
                for i in range(n):
                    pool.wait_ge(*c.next(s["ms_ready"]))
                    pool.tensor_tensor(st[:, 8 + i:9 + i], st[:, 4 + i:5 + i], cst[:, C_POW:C_POW + 1], ALU.pow).then_inc(*c.up(s["rstd_ready"]))

            def normed(n=2):
                pool.wait_ge(*c.next(s["h_ready"], n))

            def stats(*groups, places=None):
                for i, g in enumerate(groups):
                    q = places[i] if places else 0
                    pool.wait_ge(*c.next(s["stat_ready"]))
                    pool.tensor_tensor(st[:, RSTD[q]:RSTD[q] + g], st[:, STAT[q]:STAT[q] + g], cst[:, C_POW:C_POW + g], ALU.pow).then_inc(*c.up(s["stat_rstd"]))

            def mod(l, which, k):
                return dr_mod[l, which, k * D:(k + 1) * D]

            for l in range(2):
                for q in range(2):
                    pool.dma_start(modrow[q:q + 1, l, :], I["b_ada_2"][l:l + 1, :]).then_inc(s["rows_loaded"], 16)
            for l in range(2):
                for q, name in enumerate(("g_attn_2", "g_ffn_2")):
                    dst = hb[0:2, q, :] if l == 0 else bc[0:2, 1 + q, :]
                    pool.dma_start(dst, I[name][l].partition_broadcast(2)).then_inc(s["rows_loaded"], 16)
            fill(0, I["norm_mix"][0])
            pool.wait_ge(s["in_loaded"], 64)
            for l in range(2):
                pool.wait_ge(*c.next(s["mod_rows"]))
                pool.dma_start(dr_mod[l], modrow[0:2, l, :]).then_inc(s["mod_stored"], 16)
                if l == 0:
                    norms()
            pool.wait_ge(s["mod_stored"], 32)

            def cross(l):
                fill(2, I["xa_q_gain"][l], I["xa_k_gain"][l])
                norms()
                normed()
                if l == 1:
                    pool.dma_start(xs[:, 2:4, :], I["ctx_2"][0].rearrange("(t p) d -> p t d", p=P)).then_inc(s["ctx_loaded"], 16)
                norms()
                normed()
                fill(0, I["norm_ffn"][l])
                stats(X_HEADS, X_HEADS, X_HEADS, X_HEADS)

            fill(1, I["ev_ln_g"][0].rearrange("g d -> (g d)"), I["ev_ln_b"][0].rearrange("g d -> (g d)"))
            fill(2, I["ev_q_gain"][0], I["ev_k_gain"][0])
            pool.dma_start(ev_ws, I["ev_w_s"][0].rearrange("g i j -> i g j")).then_inc(s["small_loaded"], 16)
            with nc.allow_non_contiguous_dma(reason="spatial biases by token"):
                pool.dma_start(st[:, 144:152], I["ev_b_s"][0].rearrange("g i -> i g")).then_inc(s["small_loaded"], 16)
            normed()
            fill(0, I["norm_mem_kv"][0])
            stats(16, 16, 8, 8)
            pool.wait_ge(s["ms_ready"], c.count(s["ms_ready"]) + 1)
            fill(1, I["norm_mem_q"][0])
            cross(0)
            norms()
            normed()
            fill(0, I["norm_mix"][1])
            fill(1, I["od_o_gain"][0].rearrange("h v -> (h v)"))
            fill(2, I["od_b_g"][0])
            norms()
            pool.dma_start(g1, I["od_w_g1"][0].rearrange("(k p) n -> p k n", p=P)).then_inc(s["small_loaded"], 16)
            pool.dma_start(g2, I["od_w_g2"][0]).then_inc(s["small_loaded"], 16)
            normed()
            fill(0, I["norm_mem_kv"][1])
            stats(GL_HEADS, GL_HEADS)
            pool.wait_ge(s["ms_ready"], c.count(s["ms_ready"]) + 1)
            fill(1, I["norm_mem_q"][1])
            cross(1)
            norms()
            normed()
            for l in range(2):
                if l == 1:
                    pool.wait_ge(s["ms_ready"], c.count(s["ms_ready"]) + 1)
                fill(0, mod(l, 0, 1))
                fill(1, mod(l, 0, 0))
                norms()
                if l == 0:
                    with nc.allow_non_contiguous_dma(reason="a short row"):
                        pool.dma_start(sink1, I["sink_a_2"][0].partition_broadcast(P)).then_inc(s["ctx_loaded"], 16)
                fill(2, mod(l, 0, 2))
                normed()
                fill(0, mod(l, 1, 1))
                fill(1, mod(l, 1, 0))
                norms()
                normed()
                if l == 0:
                    fill(0, mod(l, 1, 2))
                else:
                    fill(0, I["gq_b_2"][0], I["gk_b_2"][0])
                    stats(20, 20, 4, 4, places=(0, 1, 0, 0))
                tiles = 4 - 2 * l
                pool.wait_ge(s["ms_ready"], c.count(s["ms_ready"]) + 1)
                fill(0, mod(l, 0, 4))
                fill(1, mod(l, 0, 3))
                norms()
                fill(2, mod(l, 0, 5))
                with nc.allow_non_contiguous_dma(reason="router's narrow weights"):
                    for n0, n1, w, b in ((0, 4, "w_group_2", "b_group_2"), (4, 36, "w_router_2", "b_router_2")):
                        pool.dma_start(mw[:, :, n0:n1], I[w][l].rearrange("(k p) n -> p k n", p=P)).then_inc(s["small_l"], 16)
                        pool.dma_start(rb[:, n0:n1], I[b][l].partition_broadcast(P)).then_inc(s["small_l"], 16)
                normed()
                if tiles == 4:
                    fill(0, mod(l, 1, 4))
                    fill(1, mod(l, 1, 3))
                    norms()
                    normed()
                    fill(0, mod(l, 1, 5))
                tab = DR["tab"][l]
                step(pool.memset(mtab.rearrange("p q s -> p (q s)"), float(EMPTY)))
                pool.dma_start(tab.rearrange("(p s) o -> p (s o)", p=P), mtab.rearrange("p q s -> p (q s)")).then_inc(s["tab_done"], 16)
                step(pool.memset(view(0, 2 * D), 0.0))
                pool.wait_ge(*c.next(s["tab_done"], 16))
                pool.wait_ge(*c.next(s["dest_ready"]))
                for q in range(2 * tiles):
                    pool.indirect_dma_start(out=tab, out_offset=bass.IndirectOffsetOnAxis(ap=mdest[:, q:q + 1], axis=0),
                                            in_=cst[:, C_ASG + q:C_ASG + q + 1], in_offset=None).then_inc(s["tab_done"], 16)
                pool.wait_ge(*c.next(s["tab_done"], 32 * tiles))
                rows = tab.rearrange("(e q r s) o -> r e q (s o)", e=N_EXP, q=2, r=4)
                for r in range(4):
                    pool.dma_start(mtab[r * N_EXP:(r + 1) * N_EXP, :, :], rows[r]).then_inc(s["tab_loaded"], 16)
                experts(pool, c, step, l)
            pool.wait_ge(s["ms_ready"], c.count(s["ms_ready"]) + 1)
            fill(0, I["g_final_2"])
            norms()


INPUTS = [
    "x", "mem", "positions", "norm_mix", "norm_mem_q", "norm_mem_kv", "norm_ffn", "ev_w_in", "ev_q_gain",
    "ev_k_gain", "ev_w_s", "ev_b_s", "ev_ln_g", "ev_ln_b", "ev_w_out", "od_w_in", "od_w_g1", "od_w_g2", "od_b_g",
    "od_o_gain", "od_w_out", "xa_w_q", "xa_w_kv", "xa_q_gain", "xa_k_gain", "xa_w_out", "ffn_w_gu", "ffn_w_down",
    "c_2", "ctx_2", "c_ctx_2", "w_ada_2", "b_ada_2", "g_attn_2", "w_qkv_2", "w_o_2", "sink_a_2", "gq_b_2", "gk_b_2",
    "g_ffn_2", "w_group_2", "b_group_2", "w_router_2", "b_router_2", "w_gate_2", "w_up_2", "w_down_2",
    "g_final_2",
]


def kernel(**inputs):
    from concourse import bacc
    from concourse.bass_utils import run_bass_kernel_spmd

    nc = bacc.Bacc("TRN2", target_bir_lowering=False, num_devices=1)
    arrays, aps = {}, {}
    for name in INPUTS:
        arrays["in_" + name] = np.ascontiguousarray(inputs[name])
    arrays["in_shape_constants"] = shape_constants()
    for key, a in arrays.items():
        aps[key[3:]] = nc.dram_tensor(key, a.shape, mybir.dt.from_np(a.dtype), kind="ExternalInput").ap()
    shape = tuple(np.shape(inputs["x"]))
    out = nc.dram_tensor("out_0", shape, F32, kind="ExternalOutput").ap()
    build_program(nc, aps, out)
    r = run_bass_kernel_spmd(nc, [arrays], core_ids=[0])
    return r.results[0]["out_0"]
```
